# Optimizing a Trainium2 kernel written in Bass

```python
import jax
import jax.numpy as jnp
from jax import lax
import numpy as np
import jax, jax.numpy as jnp

D_MODEL = 1024
BATCH = 1
SEQ = 256
DEPTH = 2

N_HEADS = 16
HEAD_DIM = D_MODEL // N_HEADS
N_KV_GROUPS = 4
HEADS_PER_GROUP = N_HEADS // N_KV_GROUPS
N_BRANCH = 3
CMP_LEN = 32
CMP_STRIDE = 16
CMP_HIDDEN = 4 * HEAD_DIM
SLC_LEN = 64
SLC_TOP_N = 16
WINDOW = 512
Q_BLOCK = 64
D_FF = 2816
CONV_WIDTH = 3
RMS_EPS = 1e-6
NEG_INF = -1e30
FORCE_SCORE = 1e30


def rms_norm(x, g):
    x32 = x.astype(jnp.float32)
    y = x32 * lax.rsqrt(jnp.mean(x32 * x32, axis=-1, keepdims=True) + RMS_EPS)
    return (y * g.astype(jnp.float32)).astype(x.dtype)

def masked_softmax(s, mask):
    s = jnp.where(mask, s, NEG_INF)
    m = jnp.max(s, axis=-1, keepdims=True)
    e = jnp.where(mask, jnp.exp(s - m), 0.0)
    return e / jnp.maximum(jnp.sum(e, axis=-1, keepdims=True), 1e-30)

def alibi_slopes():
    h = jnp.arange(1, N_HEADS + 1, dtype=jnp.float32)
    return jnp.exp2(-8.0 * h / N_HEADS).reshape(N_KV_GROUPS, HEADS_PER_GROUP)

def modulate_pre(x, g_pre, shift, scale):
    return rms_norm(x, g_pre) * (1.0 + scale[:, None, :]) + shift[:, None, :]

def gated_post_add(x, y, g_post, gate, weight):
    return x + weight * gate[:, None, :] * rms_norm(y, g_post)

def swiglu_ffn(h, w_in, w_out):
    g, u = jnp.split(h @ w_in, 2, axis=-1)
    return (jax.nn.silu(g) * u) @ w_out

def causal_shift(v, n):
    if n == 0:
        return v
    return jnp.pad(v[:, :-n], ((0, 0), (n, 0), (0, 0)))

def short_conv_mixer(h, w_in, conv_w, w_out):
    b_gate, c_gate, u = jnp.split(h @ w_in, 3, axis=-1)
    v = c_gate * u
    y = sum(conv_w[k] * causal_shift(v, CONV_WIDTH - 1 - k) for k in range(CONV_WIDTH))
    return (b_gate * y) @ w_out

def build_shared_kv(x, c, kv_norm_g, kv_ada_w, kv_ada_b, kv_w, cmp_pos, cmp_w1, cmp_w2):
    B, S, _ = x.shape
    G, dh = N_KV_GROUPS, HEAD_DIM
    shift, scale = jnp.split(jax.nn.silu(c) @ kv_ada_w + kv_ada_b, 2, axis=-1)
    h = modulate_pre(x, kv_norm_g, shift, scale)
    kv = (h @ kv_w).reshape(B, S, N_BRANCH, 2, G, dh)
    kv = jnp.transpose(kv, (2, 3, 0, 4, 1, 5))
    n_cmp = (S - CMP_LEN) // CMP_STRIDE + 1
    tok = jnp.arange(n_cmp)[:, None] * CMP_STRIDE + jnp.arange(CMP_LEN)[None, :]
    blocks = kv[0][:, :, :, tok] + cmp_pos[:, None, None, None]
    blocks = blocks.reshape(2, B, G, n_cmp, CMP_LEN * dh)
    hid = jax.nn.gelu(jnp.einsum('kbgnf,kfh->kbgnh', blocks, cmp_w1))
    kv_cmp = jnp.einsum('kbgnh,khd->kbgnd', hid, cmp_w2)
    kv_slc = kv[1].reshape(2, B, G, S // SLC_LEN, SLC_LEN, dh)
    kv_win = jnp.pad(kv[2], ((0, 0), (0, 0), (0, 0), (WINDOW, 0), (0, 0)))
    return kv_cmp, kv_slc, kv_win

def nsa_mixer(h, kv_cmp, kv_slc, kv_win, w_in, w_out):
    B, S, _ = h.shape
    G, R, dh = N_KV_GROUPS, HEADS_PER_GROUP, HEAD_DIM
    f32 = jnp.float32
    proj = h @ w_in
    q = proj[..., :N_HEADS * dh].reshape(B, S, G, R, dh) * (dh ** -0.5)
    gates = jax.nn.sigmoid(proj[..., N_HEADS * dh:].astype(f32)).reshape(B, S, N_BRANCH, G, R)
    k_cmp, v_cmp = kv_cmp[0], kv_cmp[1]
    k_slc, v_slc = kv_slc[0], kv_slc[1]
    k_win, v_win = kv_win[0], kv_win[1]
    n_cmp = k_cmp.shape[2]
    n_slc = k_slc.shape[2]
    top_n = min(SLC_TOP_N, n_slc)
    cmp_start = jnp.arange(n_cmp) * CMP_STRIDE
    cmp_end = cmp_start + CMP_LEN - 1
    slc_start = jnp.arange(n_slc) * SLC_LEN
    overlap = ((cmp_start[:, None] < slc_start[None, :] + SLC_LEN)
               & (cmp_end[:, None] >= slc_start[None, :])).astype(f32)
    slopes = alibi_slopes()
    sl5 = slopes[None, :, :, None, None]
    bi = jnp.arange(B)[:, None, None, None]
    gi = jnp.arange(G)[None, :, None, None]
    blk = jnp.arange(n_slc)

    def attend_block(qi):
        q0 = qi * Q_BLOCK
        qb = lax.dynamic_slice_in_dim(q, q0, Q_BLOCK, axis=1)
        t = q0 + jnp.arange(Q_BLOCK)
        d_cmp = t[:, None] - cmp_end[None, :]
        s = jnp.einsum('bqgrd,bgnd->bgrqn', qb, k_cmp, preferred_element_type=f32)
        s = s - sl5 * d_cmp.astype(f32)
        p_cmp = masked_softmax(s, d_cmp >= 0)
        o_cmp = jnp.einsum('bgrqn,bgnd->bqgrd', p_cmp.astype(v_cmp.dtype), v_cmp)
        imp = jnp.einsum('bgrqn,nj->bgqj', p_cmp, overlap)
        cur = t // SLC_LEN
        forced = (blk[None, :] == 0) | (blk[None, :] == cur[:, None]) | (blk[None, :] == cur[:, None] - 1)
        future = slc_start[None, :] > t[:, None]
        imp = jnp.where(forced, FORCE_SCORE, jnp.where(future, NEG_INF, imp))
        _, idx = lax.top_k(imp, top_n)
        k_sel = k_slc[bi, gi, idx]
        v_sel = v_slc[bi, gi, idx]
        d_sel = t[None, None, :, None, None] - (idx[..., None] * SLC_LEN + jnp.arange(SLC_LEN))
        s = jnp.einsum('bqgrd,bgqnld->bgrqnl', qb, k_sel, preferred_element_type=f32)
        s = s - slopes[None, :, :, None, None, None] * d_sel[:, :, None].astype(f32)
        s = s.reshape(B, G, R, Q_BLOCK, top_n * SLC_LEN)
        m_sel = (d_sel >= 0)[:, :, None].reshape(B, G, 1, Q_BLOCK, top_n * SLC_LEN)
        p_sel = masked_softmax(s, m_sel).reshape(B, G, R, Q_BLOCK, top_n, SLC_LEN)
        o_sel = jnp.einsum('bgrqnl,bgqnld->bqgrd', p_sel.astype(v_sel.dtype), v_sel)
        kw = lax.dynamic_slice_in_dim(k_win, q0, WINDOW + Q_BLOCK, axis=2)
        vw = lax.dynamic_slice_in_dim(v_win, q0, WINDOW + Q_BLOCK, axis=2)
        spos = q0 - WINDOW + jnp.arange(WINDOW + Q_BLOCK)
        d_win = t[:, None] - spos[None, :]
        m_win = (d_win >= 0) & (d_win < WINDOW) & (spos[None, :] >= 0)
        s = jnp.einsum('bqgrd,bgkd->bgrqk', qb, kw, preferred_element_type=f32)
        s = s - sl5 * d_win.astype(f32)
        p_win = masked_softmax(s, m_win)
        o_win = jnp.einsum('bgrqk,bgkd->bqgrd', p_win.astype(vw.dtype), vw)
        g = lax.dynamic_slice_in_dim(gates, q0, Q_BLOCK, axis=1)
        o = (g[:, :, 0, :, :, None] * o_cmp.astype(f32)
             + g[:, :, 1, :, :, None] * o_sel.astype(f32)
             + g[:, :, 2, :, :, None] * o_win.astype(f32))
        return o.astype(h.dtype)

    o = lax.map(attend_block, jnp.arange(S // Q_BLOCK))
    o = jnp.moveaxis(o, 0, 1).reshape(B, S, N_HEADS * dh)
    return o @ w_out

def first_inputs(seed: int = 0) -> dict:
    key = jax.random.key(seed)
    ks = jax.random.split(key, 20)
    f32 = jnp.float32
    D = D_MODEL
    n_a = DEPTH // 2
    n_b = DEPTH - n_a
    kv_cols = N_BRANCH * 2 * N_KV_GROUPS * HEAD_DIM

    def dense(k, shape, fan_in):
        return jax.random.normal(k, shape, f32) * fan_in ** -0.5

    def small(k, shape, s):
        return jax.random.normal(k, shape, f32) * s

    return {
        "x": jax.random.normal(ks[0], (BATCH, SEQ, D), f32),
        "c": jax.random.normal(ks[1], (BATCH, D), f32),
        "ada_w": dense(ks[2], (DEPTH, D, 9 * D), D),
        "ada_b": small(ks[3], (DEPTH, 9 * D), 0.01),
        "norm_g": 1.0 + small(ks[4], (DEPTH, 3, 2, D), 0.05),
        "ffn_w_in": dense(ks[5], (DEPTH, 2, D, 2 * D_FF), D),
        "ffn_w_out": dense(ks[6], (DEPTH, 2, D_FF, D), D_FF),
        "a_w_in": dense(ks[7], (n_a, D, 3 * D), D),
        "a_conv": dense(ks[8], (n_a, CONV_WIDTH, D), CONV_WIDTH),
        "a_w_out": dense(ks[9], (n_a, D, D), D),
        "kv_norm_g": 1.0 + small(ks[10], (D,), 0.05),
        "kv_ada_w": dense(ks[11], (D, 2 * D), D),
        "kv_ada_b": small(ks[12], (2 * D,), 0.01),
        "kv_w": dense(ks[13], (D, kv_cols), D),
        "cmp_pos": small(ks[14], (2, CMP_LEN, HEAD_DIM), 0.1),
        "cmp_w1": dense(ks[15], (2, CMP_LEN * HEAD_DIM, CMP_HIDDEN), CMP_LEN * HEAD_DIM),
        "cmp_w2": dense(ks[16], (2, CMP_HIDDEN, HEAD_DIM), CMP_HIDDEN),
        "b_w_in": dense(ks[17], (n_b, D, N_HEADS * HEAD_DIM + N_BRANCH * N_HEADS), D),
        "b_w_out": dense(ks[18], (n_b, N_HEADS * HEAD_DIM, D), N_HEADS * HEAD_DIM),
    }

def first_block(x, c, ada_w, ada_b, norm_g, ffn_w_in, ffn_w_out, a_w_in, a_conv, a_w_out,
              kv_norm_g, kv_ada_w, kv_ada_b, kv_w, cmp_pos, cmp_w1, cmp_w2, b_w_in, b_w_out):
    B = x.shape[0]
    D = x.shape[-1]
    n_a = DEPTH // 2
    kv_cmp = kv_slc = kv_win = None
    for layer in range(DEPTH):
        if layer == n_a:
            kv_cmp, kv_slc, kv_win = build_shared_kv(
                x, c, kv_norm_g, kv_ada_w, kv_ada_b, kv_w, cmp_pos, cmp_w1, cmp_w2)
        mod = (jax.nn.silu(c) @ ada_w[layer] + ada_b[layer]).reshape(B, 3, 3, D)
        g = norm_g[layer]
        h = modulate_pre(x, g[0, 0], mod[:, 0, 0], mod[:, 0, 1])
        y = swiglu_ffn(h, ffn_w_in[layer, 0], ffn_w_out[layer, 0])
        x = gated_post_add(x, y, g[0, 1], mod[:, 0, 2], 0.5)
        h = modulate_pre(x, g[1, 0], mod[:, 1, 0], mod[:, 1, 1])
        if layer < n_a:
            y = short_conv_mixer(h, a_w_in[layer], a_conv[layer], a_w_out[layer])
        else:
            y = nsa_mixer(h, kv_cmp, kv_slc, kv_win, b_w_in[layer - n_a], b_w_out[layer - n_a])
        x = gated_post_add(x, y, g[1, 1], mod[:, 1, 2], 1.0)
        h = modulate_pre(x, g[2, 0], mod[:, 2, 0], mod[:, 2, 1])
        y = swiglu_ffn(h, ffn_w_in[layer, 1], ffn_w_out[layer, 1])
        x = gated_post_add(x, y, g[2, 1], mod[:, 2, 2], 0.5)
    return x


CHUNK = 128
RET_HEADS = 4
RET_QK_DIM = 128
RET_V_DIM = 256
RET_QK_WIDTH = RET_HEADS * RET_QK_DIM
RET_V_WIDTH = RET_HEADS * RET_V_DIM
GMLP_GROUPS = 4
GMLP_WIDTH = D_MODEL
GMLP_GROUP_DIM = GMLP_WIDTH // GMLP_GROUPS
POOL_WINDOWS = (2, 4, 8, 16)
POOL_GROUPS = 4
POOL_WIDTH = D_MODEL
POOL_GROUP_DIM = POOL_WIDTH // POOL_GROUPS
BRANCH_WIDTH = D_MODEL
D_FF_2 = 4 * D_MODEL
N_MOD = 6
ROPE_BASE = 10000.0
EPS = 1e-6
SPLITS = (RET_QK_WIDTH, RET_QK_WIDTH, RET_V_WIDTH, RET_V_WIDTH,
          GMLP_WIDTH, GMLP_WIDTH, POOL_WIDTH, N_BRANCH * D_MODEL)
D_IN = 2 * RET_QK_WIDTH + 2 * RET_V_WIDTH + 2 * GMLP_WIDTH + POOL_WIDTH + N_BRANCH * D_MODEL


def rms_norm_2(x, gain=None):
    xf = x.astype(jnp.float32)
    y = xf * lax.rsqrt(jnp.mean(xf * xf, axis=-1, keepdims=True) + EPS)
    if gain is not None:
        y = y * gain.astype(jnp.float32)
    return y.astype(x.dtype)

def split_columns(proj):
    pieces, start = [], 0
    for w in SPLITS:
        pieces.append(proj[..., start:start + w])
        start += w
    return pieces

def rotary(x, positions):
    half = x.shape[-1] // 2
    inv_freq = ROPE_BASE ** (-jnp.arange(half, dtype=jnp.float32) / half)
    ang = positions.astype(jnp.float32)[:, :, None] * inv_freq
    cos = jnp.cos(ang)[:, :, None, :]
    sin = jnp.sin(ang)[:, :, None, :]
    xf = x.astype(jnp.float32)
    x1, x2 = xf[..., :half], xf[..., half:]
    return jnp.concatenate([x1 * cos - x2 * sin, x2 * cos + x1 * sin], axis=-1).astype(x.dtype)

def retention(q, k, v, g, positions):
    B, S, _ = q.shape
    nc = S // CHUNK
    dt = q.dtype
    q = rotary(q.reshape(B, S, RET_HEADS, RET_QK_DIM), positions)
    k = rotary(k.reshape(B, S, RET_HEADS, RET_QK_DIM), positions) * (RET_QK_DIM ** -0.5)
    v = v.reshape(B, S, RET_HEADS, RET_V_DIM)
    log_gamma = jnp.log1p(-jnp.power(2.0, -5.0 - jnp.arange(RET_HEADS, dtype=jnp.float32)))
    pos = jnp.arange(CHUNK, dtype=jnp.float32)
    rel = pos[:, None] - pos[None, :]
    causal = rel >= 0
    decay_intra = jnp.where(causal[None],
                            jnp.exp(log_gamma[:, None, None] * jnp.where(causal, rel, 0.0)[None]),
                            0.0)
    decay_q = jnp.exp(log_gamma[:, None] * (pos + 1.0)[None])
    decay_k = jnp.exp(log_gamma[:, None] * (CHUNK - 1.0 - pos)[None])
    decay_chunk = jnp.exp(log_gamma * CHUNK)

    qc = q.reshape(B, nc, CHUNK, RET_HEADS, RET_QK_DIM)
    kc = k.reshape(B, nc, CHUNK, RET_HEADS, RET_QK_DIM)
    vc = v.reshape(B, nc, CHUNK, RET_HEADS, RET_V_DIM)
    scores = jnp.einsum('bnihd,bnjhd->bnhij', qc, kc) * decay_intra.astype(dt)
    intra = jnp.einsum('bnhij,bnjhe->bnihe', scores, vc)
    kv = jnp.einsum('bnjhd,hj,bnjhe->nbhde', kc, decay_k.astype(dt), vc).astype(jnp.float32)

    def step(state, kv_n):
        return decay_chunk[None, :, None, None] * state + kv_n, state

    _, prev = lax.scan(step, jnp.zeros((B, RET_HEADS, RET_QK_DIM, RET_V_DIM), jnp.float32), kv)
    cross = jnp.einsum('bnihd,hi,nbhde->bnihe', qc, decay_q.astype(dt), prev.astype(dt))
    o = (intra + cross).reshape(B, S, RET_HEADS, RET_V_DIM)
    o = rms_norm_2(o).reshape(B, S, RET_V_WIDTH)
    return jax.nn.silu(g) * o

def spatial_gating(u, v, w_s, b_s, v_gain):
    B, S, _ = u.shape
    nc = S // CHUNK
    u = jax.nn.gelu(u)
    v = rms_norm_2(jax.nn.gelu(v), v_gain)
    vc = v.reshape(B, nc, CHUNK, GMLP_GROUPS, GMLP_GROUP_DIM)
    mask = jnp.tril(jnp.ones((CHUNK, CHUNK), dtype=bool))
    w = jnp.where(mask[None], w_s, jnp.zeros_like(w_s))
    mixed = jnp.einsum('gts,bnsgc->bntgc', w, vc) + b_s.T[None, None, :, :, None]
    return u * mixed.reshape(B, S, GMLP_WIDTH)

def multiscale_pool(p, w_pool, b_pool, scale):
    B, S, _ = p.shape
    pg = p.reshape(B, S, POOL_GROUPS, POOL_GROUP_DIM).astype(jnp.float32)
    cs = jnp.concatenate([jnp.zeros((B, 1, POOL_GROUPS, POOL_GROUP_DIM), jnp.float32),
                          jnp.cumsum(pg, axis=1)], axis=1)
    t = jnp.arange(1, S + 1)
    outs = []
    for gi, w in enumerate(POOL_WINDOWS):
        start = jnp.maximum(t - w, 0)
        window_sum = cs[:, 1:, gi] - cs[:, start, gi]
        count = jnp.minimum(t, w).astype(jnp.float32)[None, :, None]
        outs.append(window_sum / count - pg[:, :, gi])
    pooled = jnp.stack(outs, axis=2).astype(p.dtype)
    mixed = jnp.einsum('bsgc,gce->bsge', pooled, w_pool) + b_pool[None, None]
    return mixed.reshape(B, S, POOL_WIDTH) * scale

def second_inputs(seed: int = 0) -> dict:
    key = jax.random.key(seed)
    ks = jax.random.split(key, 20)
    f32 = jnp.float32
    nrm = lambda k, shape, s: jax.random.normal(k, shape, f32) * s
    return {
        "x": nrm(ks[0], (BATCH, SEQ, D_MODEL), 1.0),
        "c": nrm(ks[1], (BATCH, D_MODEL), 1.0),
        "positions": jnp.broadcast_to(jnp.arange(SEQ, dtype=jnp.int32), (BATCH, SEQ)),
        "w_ada": nrm(ks[2], (DEPTH, D_MODEL, N_MOD * D_MODEL), 0.5 * D_MODEL ** -0.5),
        "b_ada": nrm(ks[3], (DEPTH, N_MOD * D_MODEL), 0.01),
        "norm1": 1.0 + nrm(ks[4], (DEPTH, D_MODEL), 0.02),
        "norm2": 1.0 + nrm(ks[5], (DEPTH, D_MODEL), 0.02),
        "w_in": nrm(ks[6], (DEPTH, D_MODEL, D_IN), D_MODEL ** -0.5),
        "ws_gmlp": nrm(ks[7], (DEPTH, GMLP_GROUPS, CHUNK, CHUNK), CHUNK ** -0.5),
        "bs_gmlp": 1.0 + nrm(ks[8], (DEPTH, GMLP_GROUPS, CHUNK), 0.1),
        "vnorm_gmlp": 1.0 + nrm(ks[9], (DEPTH, GMLP_WIDTH), 0.02),
        "w_pool": nrm(ks[10], (DEPTH, POOL_GROUPS, POOL_GROUP_DIM, POOL_GROUP_DIM), POOL_GROUP_DIM ** -0.5),
        "b_pool": nrm(ks[11], (DEPTH, POOL_GROUPS, POOL_GROUP_DIM), 0.01),
        "pool_scale": 1.0 + nrm(ks[12], (DEPTH, POOL_WIDTH), 0.1),
        "w_branch": nrm(ks[13], (DEPTH, N_BRANCH, BRANCH_WIDTH, D_MODEL), BRANCH_WIDTH ** -0.5),
        "w_out": nrm(ks[14], (DEPTH, D_MODEL, D_MODEL), D_MODEL ** -0.5),
        "w_ff1": nrm(ks[15], (DEPTH, D_MODEL, D_FF_2), D_MODEL ** -0.5),
        "w_ff2": nrm(ks[16], (DEPTH, D_FF_2, D_MODEL), D_FF_2 ** -0.5),
        "final_norm": 1.0 + nrm(ks[17], (D_MODEL,), 0.02),
    }

def second_block(x, c, positions, w_ada, b_ada, norm1, norm2, w_in, ws_gmlp, bs_gmlp, vnorm_gmlp,
              w_pool, b_pool, pool_scale, w_branch, w_out, w_ff1, w_ff2, final_norm):
    B, S, _ = x.shape
    c_act = jax.nn.silu(c)
    for l in range(DEPTH):
        mod = c_act @ w_ada[l] + b_ada[l]
        sh1, sc1, gt1, sh2, sc2, gt2 = [m[:, None, :] for m in jnp.split(mod, N_MOD, axis=-1)]

        h = rms_norm_2(x, norm1[l]) * (1.0 + sc1) + sh1
        proj = h @ w_in[l]
        q, k, v, g, u, vs, p, gate_cols = split_columns(proj)
        y_ret = retention(q, k, v, g, positions)
        y_sgu = spatial_gating(u, vs, ws_gmlp[l], bs_gmlp[l], vnorm_gmlp[l])
        y_pool = multiscale_pool(p, w_pool[l], b_pool[l], pool_scale[l])
        branches = jnp.stack([y_ret, y_sgu, y_pool], axis=2)
        branch_proj = jnp.einsum('bsnc,ncd->bsnd', branches, w_branch[l])
        gates = jax.nn.sigmoid(gate_cols.reshape(B, S, N_BRANCH, D_MODEL))
        merged = jnp.sum(gates * branch_proj, axis=2)
        x = x + gt1 * (merged @ w_out[l])

        h2 = rms_norm_2(x, norm2[l]) * (1.0 + sc2) + sh2
        hidden = jnp.square(jax.nn.relu(h2 @ w_ff1[l]))
        x = x + gt2 * (hidden @ w_ff2[l])
    return rms_norm_2(x, final_norm)


def setup_inputs(seed=0):
    out = dict(first_inputs(seed))
    for name, value in second_inputs(seed + 1).items():
        if name != "x":
            out[name + "_2"] = value
    return out


def reference(
    x, c, ada_w, ada_b, norm_g, ffn_w_in, ffn_w_out, a_w_in, a_conv, a_w_out, kv_norm_g,
    kv_ada_w, kv_ada_b, kv_w, cmp_pos, cmp_w1, cmp_w2, b_w_in, b_w_out, c_2, positions_2,
    w_ada_2, b_ada_2, norm1_2, norm2_2, w_in_2, ws_gmlp_2, bs_gmlp_2, vnorm_gmlp_2, w_pool_2,
    b_pool_2, pool_scale_2, w_branch_2, w_out_2, w_ff1_2, w_ff2_2, final_norm_2,
):
    x = first_block(
        x, c, ada_w, ada_b, norm_g, ffn_w_in, ffn_w_out, a_w_in, a_conv, a_w_out, kv_norm_g,
        kv_ada_w, kv_ada_b, kv_w, cmp_pos, cmp_w1, cmp_w2, b_w_in, b_w_out,
    )
    return second_block(
        x, c_2, positions_2, w_ada_2, b_ada_2, norm1_2, norm2_2, w_in_2, ws_gmlp_2, bs_gmlp_2,
        vnorm_gmlp_2, w_pool_2, b_pool_2, pool_scale_2, w_branch_2, w_out_2, w_ff1_2, w_ff2_2,
        final_norm_2,
    )


_drawn_inputs = setup_inputs


def setup_inputs(seed=0):
    import zlib

    import numpy as np

    out = dict(_drawn_inputs(seed))
    spreads = {}
    factors = {'ada_b': 2.719,
     'kv_norm_g': 2.944,
     'kv_ada_b': 8.0,
     'cmp_pos': 3.071,
     'b_ada_2': 3.435,
     'norm1_2': 8.0,
     'norm2_2': 6.572,
     'bs_gmlp_2': 4.803,
     'vnorm_gmlp_2': 26.484,
     'b_pool_2': 43.888,
     'pool_scale_2': 4.109,
     'final_norm_2': 7.955}
    for name, (base, spread) in spreads.items():
        noise = np.random.default_rng([zlib.crc32(name.encode()), seed]).standard_normal(out[name].shape)
        drawn = base * np.exp(spread * noise) if base else spread * noise
        out[name] = jnp.asarray(drawn.astype(out[name].dtype))
    for name, factor in factors.items():
        out[name] = (out[name] * factor).astype(out[name].dtype)
    return out
```

```python
from contextlib import ExitStack

import numpy as np

import concourse.bass as bass
from concourse import mybir

F32 = mybir.dt.float32
F32R = mybir.dt.float32r
I32 = mybir.dt.int32
ALU = mybir.AluOpType
ACT = mybir.ActivationFunctionType
AX = mybir.AxisListType

P = 128
D = 1024
T = 256
KT = D // P
DEPTH = 2
D_FF = 2816
FFN_STEPS = D_FF // 256
D_FF_2 = 4 * D
FF2_STEPS = D_FF_2 // 256
HEADS, DH, GROUPS = 16, 64, 4
R = HEADS // GROUPS
N_CMP = (T - 32) // 16 + 1
NEG = -1e30
EPS = 1e-6
RING = 3
CHUNK = 2048
ADA_W = 1536
POOL_WINDOWS = (2, 4, 8, 16)
POOL_ADDS = (1, 3, 5)

_at = 0
CH = {}
for _name, _n in (("ffn00", 3 * FFN_STEPS), ("conv_in", 12), ("conv_out", 4), ("ffn01", 3 * FFN_STEPS),
                  ("kv", 6), ("cmp", 4), ("ffn10", 3 * FFN_STEPS), ("nsa_in", 5), ("nsa_out", 4),
                  ("ffn11", 3 * FFN_STEPS),
                  ("mix0", 48), ("mix0_out", 4), ("ff0", 2 * FF2_STEPS),
                  ("mix1", 48), ("mix1_out", 4), ("ff1", 2 * FF2_STEPS)):
    CH[_name] = _at
    _at += _n
N_CHUNKS = _at

HID0 = {}
_at = 0
for _name, _n in (("ffn00", FFN_STEPS), ("ffn01", FFN_STEPS), ("ffn10", FFN_STEPS), ("ffn11", FFN_STEPS),
                  ("ff0", FF2_STEPS), ("ff1", FF2_STEPS)):
    HID0[_name] = _at
    _at += _n

VEC = {}
_v = 0
for _name, _n in (("norm_g", 96), ("ada_b", 144), ("kv_norm_g", 8), ("kv_ada_b", 16), ("b_ada_2", 96),
                  ("norm1_2", 16), ("norm2_2", 16), ("a_conv", 24), ("vnorm", 16), ("b_pool", 16),
                  ("pool_scale", 16), ("final", 8), ("c", 8), ("c_2", 8)):
    VEC[_name] = _v
    _v += _n
N_VEC = _v


def slopes():
    return [2.0 ** (-8.0 * (h + 1) / HEADS) for h in range(HEADS)]


def tables():
    f = np.float32
    ident = np.eye(P, dtype=f)
    ones = np.full((P, P), 1.0 / D, f)
    base = np.concatenate([ident, ones, np.ones((P, 1), f)], 1)
    i = np.arange(P)[:, None]
    j = np.arange(T)[None, :]
    dist = (j - (P + i)).astype(f)
    dist[(j - (P + i)) > 0] = NEG
    sel = np.zeros((P, 2, P), f)
    for u in range(2):
        for m in range(P):
            sel[u * 64 + m % 64, u, m] = 1.0
    sl = slopes()
    cb = np.zeros((P, 2, R, GROUPS, N_CMP), f)
    for ic in range(2):
        d = (ic * P + np.arange(P)[:, None]) - (np.arange(N_CMP)[None, :] * 16 + 31)
        for r in range(R):
            for g in range(GROUPS):
                cb[:, ic, r, g] = np.where(d >= 0, -f(sl[g * R + r]) * d.astype(f), f(NEG))
    nsa = np.concatenate([dist, cb.reshape(P, -1), sel.reshape(P, -1)], 1)
    decay = np.zeros((P, 4, T), f)
    for h in range(4):
        lg = np.log1p(-(2.0 ** (-5.0 - h)))
        rel = j - i
        decay[:, h] = np.where(rel >= 0, np.exp(lg * np.maximum(rel, 0)), 0.0) * 128.0 ** -0.5
    rot = np.zeros((P, P), f)
    for d in range(64):
        rot[d + 64, d] = -1.0
        rot[d, d + 64] = 1.0
    half = 64
    inv = (np.float32(10000.0) ** (-np.arange(half, dtype=f) / f(half))).astype(f)
    invf = np.concatenate([inv, inv])[:, None]
    cnt = np.stack([1.0 / np.minimum(np.arange(1, 17), w) for w in POOL_WINDOWS]).astype(f)
    cnt = np.broadcast_to(cnt.reshape(1, 64), (P, 64))
    b2 = np.concatenate([decay.reshape(P, -1), rot, invf, cnt], 1)
    return {n: np.ascontiguousarray(a, dtype=f) for n, a in (("t_base", base), ("t_nsa", nsa), ("t_b2", b2))}


class Steps:

    def __init__(self, sem, key, seen):
        self.sem, self.key, self.seen, self.n = sem, key, seen, 0

    def __call__(self, ins, mark=None):
        ins.then_inc(self.sem, 1)
        self.n += 1
        if mark:
            self.seen[self.key, mark] = self.n
        return self.n


def build(nc, I, out, at):
    seen = {}
    ctx = ExitStack()
    with ctx:
        def sb(name, shape, dt=F32):
            return ctx.enter_context(nc.sbuf_tensor(name, shape, dt))

        def sem(name):
            return ctx.enter_context(nc.semaphore(name))

        raw = [sb(f"raw{i}", [P, CHUNK]) for i in range(RING)]
        whi = [sb(f"whi{i}", [P, CHUNK], F32R) for i in range(RING)]
        wlo = [sb(f"wlo{i}", [P, CHUNK], F32R) for i in range(RING)]
        adaw = sb("adaw", [P, 2, ADA_W])
        acc = sb("acc", [P, 4 * ADA_W])
        x = sb("x", [P, KT, T])
        oph = {"A": sb("opA_hi", [P, KT, T], F32R), "B": sb("opB_hi", [P, KT, T], F32R)}
        opl = {"A": sb("opA_lo", [P, KT, T], F32R), "B": sb("opB_lo", [P, KT, T], F32R)}
        tmp8 = sb("tmp8", [P, KT, T])
        gact = sb("gact", [P, 2, T])
        hidf = sb("hidf", [P, 2, T])
        base = sb("base", [P, 257])
        ident, onesD, one = base[:, 0:128], base[:, 128:256], base[:, 256:257]
        vec = sb("vecs", [P, N_VEC])
        csil = sb("csil", [P, 16])
        mod = sb("mod", [P, 256])
        scl = sb("scl", [P, 11 * 8])
        gat = sb("gat", [P, 10 * 8])
        epsc = sb("epsc", [P, 1])
        sd = sb("sd", [P, 2])
        rsd = sb("rsd", [P, 2])
        diag = sb("diag", [P, T])
        rstd = sb("rstd", [P, T])
        warm = sb("warm", [P, 1])
        MIX = 10240
        mix = sb("mix", [P, MIX])
        PA = ctx.enter_context(nc.psum_tensor("PA", [P, 4, T], F32))
        PB = ctx.enter_context(nc.psum_tensor("PB", [P, 4, T], F32))
        PY = ctx.enter_context(nc.psum_tensor("PY", [P, 8, T], F32))
        PS = {"A": PA, "B": PB, "Y": PY}
        flat = {k: v[:].rearrange("p a b -> p (a b)") for k, v in PS.items()}

        def V(name, i=0, n=KT):
            return vec[:, VEC[name] + i:VEC[name] + i + n]

        raw_ready = [sem(f"raw_ready{i}") for i in range(RING)]
        hi_ready = sem("hi_ready")
        lo_ready = sem("lo_ready")
        multiplied = sem("multiplied")
        ada_ready = [sem(f"ada_ready{i}") for i in range(4)]
        ada_used = [sem(f"ada_used{i}") for i in range(4)]
        act_made = sem("act_made")
        hid_made = sem("hid_made")
        hid_hi = sem("hid_hi")
        hid_lo = sem("hid_lo")
        ada_free = sem("ada_free")
        x_in = sem("x_in")
        vec_in = sem("vec_in")
        base_in = sem("base_in")
        nsa_in = sem("nsa_in")
        cmp_in = sem("cmp_in")
        b2_in = sem("b2_in")
        lay_in = sem("lay_in")
        out_done = sem("out_done")
        steps = {"T": sem("tensor_step"), "S": sem("scalar_step"), "V": sem("vector_step"), "G": sem("gpsimd_step")}

        def need(eng, key, mark):
            eng.wait_ge(steps[key], at[key, mark])

        def area(o, n):
            if o < MIX:
                assert o + n <= MIX, (o, n)
                return mix[:, o:o + n]
            assert o - MIX + n <= 4 * ADA_W
            return acc[:, o - MIX:o - MIX + n]

        def macc(h):
            return t3(X[2], 8)[:, 4 * h:4 * h + 4, :]

        def t3(ap, a):
            return ap.rearrange("p (a b) -> p a b", a=a)

        cb_, cc_ = t3(area(0, 2048), 8), t3(area(2048, 2048), 8)
        cv_ = t3(area(4096, 8 * 258), 8)
        cy_ = t3(area(6160, 2048), 8)
        o = 0
        kslc, kwin = t3(area(0, 512), 2), t3(area(512, 512), 2)
        vtok = {"slc": t3(area(1024, 512), 2), "win": t3(area(1536, 512), 2)}
        kcmp, vcmp = area(2048, 60), area(2112, 64)
        hidc = area(2176, 240).rearrange("p (k m c) -> p k m c", k=2, m=2)
        pos2 = area(2416, 32).rearrange("p (k l) -> p k l", k=2)
        cw2 = area(2448, 384)
        w2k, w2v = t3(cw2[:, 0:256], 2), t3(cw2[:, 256:384], 2)
        tnsa = area(2832, 256 + 480 + 256)
        dist, cbias = tnsa[:, 0:256], tnsa[:, 256:736].rearrange("p (i h n) -> p i h n", i=2, n=N_CMP)
        selu = t3(tnsa[:, 736:992], 2)
        kvc = t3(area(3840, 1024), 4)
        vtmp = {"slc": t3(area(4864, 512), 2), "win": t3(area(5376, 512), 2)}
        qf = t3(area(5888, 2048), 8)
        gates = area(7936, 96).rearrange("p (i c) -> p i c", i=2)
        gexp = area(8032, 96)
        ptc = area(8128, 1024).rearrange("p (i r c) -> p i r c", i=2, r=R)
        small = area(9152, 128)
        pc32 = area(MIX, 1024).rearrange("p (i h n) -> p i h n", i=2, n=32)
        sc_ = area(MIX + 1024, 480).rearrange("p (i h n) -> p i h n", i=2, n=N_CMP)
        ssb = [t3(area(MIX + 1536 + 1024 * i, 1024), 4) for i in range(2)]
        ptsb = t3(area(MIX + 3584, 1024), 8)
        tb2 = area(0, 1024 + 128 + 1 + 64)
        decay, rotm, invf = t3(tb2[:, 0:1024], 4), tb2[:, 1024:1152], tb2[:, 1152:1153]
        cnt = t3(tb2[:, 1153:1217], 4)
        cos_, sin_ = area(1220, 256), area(1476, 256)
        wT, bs = t3(area(1732, 512), 4), t3(area(2244, 512), 4)
        X = [area(2756 + 2048 * i, 2048) for i in range(3)] + [area(MIX + 2048 * i, 2048) for i in range(3)]
        slabs = adaw[:].rearrange("p a b -> p (a b)")
        wpool, wsr = slabs[:, 0:2048], slabs[:, 2048:2560]
        posi = area(8900, 256)
        rr = area(9156, 1024)
        assert 2756 + 3 * 2048 <= 8900

        slab = [adaw[:, 0, :], adaw[:, 1, :], area(MIX - 2 * ADA_W, ADA_W), area(MIX - ADA_W, ADA_W)]

        def job(which, parts):
            total = sum(n for _, _, n in parts)
            width = total // 4
            slots, at_, left = [], 0, list(parts)
            for q in range(4):
                loads, o = [], 0
                while o < width:
                    w, c0, n = left.pop(0)
                    m = min(n, width - o)
                    loads.append((w, c0, m, o))
                    if m < n:
                        left.insert(0, (w, c0 + m, n - m))
                    o += m
                slots.append((q, width, q * width, loads))
            return which, slots, total

        a0, a1 = I["ada_w"][0], I["ada_w"][1]
        JOBS = {
            "first": job(0, [(a0, 0, 2048)]),
            "ffn00": job(0, [(a0, 2048, 6144)]),
            "ffn01": job(0, [(a0, 8192, 1024), (a1, 0, 3072), (I["kv_ada_w"], 0, 2048)]),
            "ffn10": job(0, [(a1, 3072, 6144)]),
            "ffn11": job(1, [(I["w_ada_2"][0], 0, 6144)]),
            "ff0": job(1, [(I["w_ada_2"][1], 0, 6144)]),
        }
        MODS = {
            "first": [(0, 16, 0, V("ada_b", 0, 16))],
            "ffn00": [(0, 48, 16, V("ada_b", 16, 48))],
            "ffn01": [(0, 8, 64, V("ada_b", 64, 8)), (8, 24, 72, V("ada_b", 72, 24)), (32, 16, 144, V("kv_ada_b", 0, 16))],
            "ffn10": [(0, 48, 96, V("ada_b", 96, 48))],
            "ffn11": [(0, 48, 160, V("b_ada_2", 0, 48))],
            "ff0": [(0, 48, 208, V("b_ada_2", 48, 48))],
        }
        SUB = {}
        for l in range(2):
            for s in range(3):
                g = (l * 3 + s) * 16
                SUB[f"{l}{s}"] = dict(i=l * 3 + s, shift=72 * l + 24 * s, g_pre=V("norm_g", g), g_post=V("norm_g", g + 8),
                                      w=1.0 if s == 1 else 0.5)
        SUB["kv"] = dict(i=10, shift=144, g_pre=V("kv_norm_g"))
        for l in range(2):
            for s in range(2):
                SUB[f"b{l}{s}"] = dict(i=6 + 2 * l + s, shift=160 + 48 * l + 24 * s, w=1.0,
                                       g_pre=V(("norm1_2", "norm2_2")[s], 8 * l), g_post=None)
        SCALES = {"first": ["00"], "ffn00": ["01", "02"], "ffn01": ["10", "kv"], "ffn10": ["11", "12"],
                  "ffn11": ["b00", "b01"], "ff0": ["b10", "b11"]}
        GATES = {"first": [], "ffn00": ["00", "01"], "ffn01": ["02", "10"], "ffn10": ["11", "12"],
                 "ffn11": ["b00", "b01"], "ff0": ["b10", "b11"]}

        def A_(s):
            return scl[:, SUB[s]["i"] * 8:SUB[s]["i"] * 8 + 8]

        def B_(s):
            return mod[:, SUB[s]["shift"]:SUB[s]["shift"] + 8]

        def G_(s):
            return gat[:, SUB[s]["i"] * 8:SUB[s]["i"] * 8 + 8]

        ADA0, LOADS0, _n = {}, {}, 0
        _loads = [0] * 4
        for name, (_, slots, _) in JOBS.items():
            ADA0[name] = _n
            LOADS0[name] = list(_loads)
            _n += KT
            for q in range(4):
                _loads[q] += KT * len(slots[q][3])

        def wv(w):
            return w.rearrange("(k p) n -> p k n", p=P)

        def src_ffn_in(w, j, half):
            return [(wv(w)[:, 4 * half:4 * half + 4, bass.ds(two * D_FF + j, 256)], t * 1024, 4) for t, two in ((0, 0), (1, 1))]

        def src_in512(w, c0, half):
            return [(wv(w)[:, 4 * half + 2 * q:4 * half + 2 * q + 2, c0:c0 + 512], q * 1024, 2) for q in range(2)]

        def src_in256(w, c0, k0=0):
            return [(wv(w)[:, k0 + 4 * q:k0 + 4 * q + 4, bass.ds(c0, 256)], q * 1024, 4) for q in range(2)]

        def src_out(w, row):
            return [(w[bass.ds(row + P * q, P), :], q * 1024, 1) for q in range(2)]

        def src_gates(w):
            return [(wv(w)[:, 4 * q:4 * q + 4, D:D + 48], q * 192, 4) for q in range(2)]

        def tile_ffn_in(k, m):
            return (m // 2) * 1024 + k * 256 + (m % 2) * 128

        def tile_in512(k, m):
            return k * 512 + m * 128

        def tile_in256(k, m):
            return k * 256 + m * 128

        def tile_out(k, m):
            return k * 1024 + m * 128

        block = ctx.enter_context(nc.Block())

        @block.sync
        def _(sp):
            def chunk(c, src, slot=None):
                slot = c % RING if slot is None else slot
                if not isinstance(c, int) or c >= RING:
                    sp.wait_ge(lo_ready, c - (RING - 1))
                for ap, o_, k in src:
                    dst = raw[slot][:, o_:o_ + k * ap.shape[-1]]
                    sp.dma_start(dst if len(ap.shape) == 2 else t3(dst, k), ap).then_inc(raw_ready[slot], 16)

            def ffn(name, w_in, w_out):
                c0 = CH[name]
                chunk(c0, src_ffn_in(w_in, 0, 0))
                chunk(c0 + 1, src_ffn_in(w_in, 0, 1))

                def body(j):
                    chunk(c0 + 3 * j - 1, src_ffn_in(w_in, j * 256, 0), (c0 + 2) % RING)
                    chunk(c0 + 3 * j, src_ffn_in(w_in, j * 256, 1), c0 % RING)
                    chunk(c0 + 3 * j + 1, src_out(w_out, (j - 1) * 256), (c0 + 1) % RING)

                with sp.Fori(0, 10) as i:
                    body(i + 1)
                chunk(c0 + 32, src_out(w_out, 10 * 256))

            def ff2(l, w_in, w_out):
                c0 = CH[f"ff{l}"]
                chunk(c0, src_in256(w_in, 0))

                def body(j, jj):
                    chunk(c0 + 2 * j - 1, src_in256(w_in, j * 256), (c0 + 2 * jj - 1) % RING)
                    chunk(c0 + 2 * j, src_out(w_out, (j - 1) * 256), (c0 + 2 * jj) % RING)

                with sp.Fori(0, 5) as i:
                    for jj in range(1, 4):
                        body(i * 3 + jj, jj)
                chunk(c0 + 31, src_out(w_out, 15 * 256))

            sp.dma_start(vec[:], I["vec"]).then_inc(vec_in, 16)
            sp.dma_start(base[:], I["t_base"]).then_inc(base_in, 16)
            sp.dma_start(x[:], I["x_fm"]).then_inc(x_in, 16)
            ffn("ffn00", I["ffn_w_in"][0, 0], I["ffn_w_out"][0, 0])
            for g in range(6):
                for h in range(2):
                    chunk(CH["conv_in"] + 2 * g + h, src_in512(I["a_w_in"], 512 * g, h))
            for k in range(4):
                chunk(CH["conv_out"] + k, src_out(I["a_w_out"], 256 * k))
            ffn("ffn01", I["ffn_w_in"][0, 1], I["ffn_w_out"][0, 1])
            sp.wait_ge(multiplied, CH["conv_out"] + 4)
            sp.dma_start(tnsa, I["t_nsa"]).then_inc(nsa_in, 16)
            sp.dma_start(pos2, I["cmp_pos2"]).then_inc(cmp_in, 16)
            w2 = I["cmp_w2"].rearrange("k (m p) d -> k p m d", p=P)
            for u in range(2):
                sp.dma_start(w2k[:, :, 64 * u:64 * u + 64], w2[0]).then_inc(cmp_in, 16)
            sp.dma_start(w2v, w2[1]).then_inc(cmp_in, 16)
            for g in range(3):
                for h in range(2):
                    chunk(CH["kv"] + 2 * g + h, src_in512(I["kv_w"], 512 * g, h))
            for kv in range(2):
                for h in range(2):
                    chunk(CH["cmp"] + 2 * kv + h, src_in256(I["cmp_w1"][kv], 0, 8 * h))
            ffn("ffn10", I["ffn_w_in"][1, 0], I["ffn_w_out"][1, 0])
            for g in range(2):
                for h in range(2):
                    chunk(CH["nsa_in"] + 2 * g + h, src_in512(I["b_w_in_p"], 512 * g, h))
            chunk(CH["nsa_in"] + 4, src_gates(I["b_w_in_p"]))
            for k in range(4):
                chunk(CH["nsa_out"] + k, src_out(I["b_w_out_p"], 256 * k))
            ffn("ffn11", I["ffn_w_in"][1, 1], I["ffn_w_out"][1, 1])
            sp.wait_ge(multiplied, CH["nsa_out"] + 4)
            sp.dma_start(tb2, I["t_b2"]).then_inc(b2_in, 16)
            for l in range(2):
                c = CH[f"mix{l}"]
                for slot in range(2):
                    sp.wait_ge(ada_used[slot], ADA0["ff0"] + KT * l)
                if l == 0:
                    sp.wait_ge(ada_used[2], ADA0["ff0"])
                    sp.wait_ge(ada_used[3], ADA0["ff0"])
                    sp.dma_start(posi.bitcast(I32), I["positions"].partition_broadcast(P)).then_inc(b2_in, 16)
                if l == 1:
                    need(sp, "V", "b0.branch_done")
                sp.dma_start(wsr, I["ws"][l]).then_inc(lay_in, 16)
                sp.dma_start(bs, I["bs"][l:l + 1].partition_broadcast(P)).then_inc(lay_in, 16)
                sp.dma_start(wpool.rearrange("p (g k n) -> p g k n", g=4, k=2).rearrange("p g k n -> p (g k) n"),
                             I["w_pool"][l].rearrange("(g p) n -> p g n", p=P)).then_inc(lay_in, 16)
                for g in range(12):
                    for h in range(2):
                        chunk(c + 2 * g + h, src_in512(I["w_in_2"][l], 512 * g, h))
                c += 24
                for b in range(3):
                    for g in range(2):
                        for h in range(2):
                            chunk(c, src_in512(I["w_in_2"][l], 512 * (12 + 2 * b + g), h))
                            c += 1
                    for g in range(2):
                        for h in range(2):
                            chunk(c, src_in512(I["w_branch"][l, b], 512 * g, h))
                            c += 1
                for k in range(4):
                    chunk(c + k, src_out(I["w_out_2"][l], 256 * k))
                ff2(l, I["w_ff1"][l], I["w_ff2"][l])
            need(sp, "V", "fin.t7")
            sp.dma_start(out, tmp8[:]).then_inc(out_done, 16)
            sp.wait_ge(out_done, 16)

        @block.tensor
        def _(pe):
            S = Steps(steps["T"], "T", seen)
            freed = {}

            def take(buf):
                if buf in freed:
                    s, v = freed.pop(buf)
                    pe.wait_ge(s, v)

            def by(buf, key, mark):
                freed[buf] = (steps[key], at[key, mark])

            def mm3(o_, c_slot, woff, X2, rhs, start, stop):
                xh, xl = X2
                w1, w2_ = whi[c_slot][:, woff:woff + P], wlo[c_slot][:, woff:woff + P]
                nc.tensor.matmul(o_, w1, rhs(xh), start=start, stop=False, skip_group_check=True)
                nc.tensor.matmul(o_, w1, rhs(xl), start=False, stop=False, skip_group_check=True)
                return nc.tensor.matmul(o_, w2_, rhs(xh), start=False, stop=stop, skip_group_check=True)

            def chunk(c, slot, ps, tile, kts, ms, op, k_first, k_last, before=None, n=T, m0=0, tag=None):
                pe.wait_ge(lo_ready, c + 1)
                for kk, k in enumerate(kts):
                    if before:
                        before(k)
                    for m in range(ms):
                        last = mm3(ps[:, m0 + m, 0:n], slot, tile(kk, m), (oph[op], opl[op]),
                                   lambda t_, k=k: t_[:, k, :] if n == T else t_(k), k == k_first and m % 2 == 0, k == k_last)
                        if tag and k == k_last and m in (1, 3, 5):
                            S(last, f"{tag}.bank{m // 2}")
                last.then_inc(multiplied, 1)

            def group512(c, buf, op, before=None):
                for h in range(2):
                    chunk(c + h, (c + h) % RING, PS[buf], tile_in512, range(4 * h, 4 * h + 4), 4, op, 0, 7, before)

            def out1024(c, op, tag, before=None):
                take("Y")
                for q in range(4):
                    chunk(c + q, (c + q) % RING, PY, tile_out, (2 * q, 2 * q + 1), 8, op, 0, 7, before, tag=tag if q == 3 else None)

            def ssq(tag):
                take("B")
                for k in range(KT):
                    if k % 2 == 0:
                        need(pe, "S", f"{tag}.sq{k // 2}")
                    for j in range(2):
                        last = nc.tensor.matmul(flat["B"][:, j:j + 1], tmp8[:, k, j * P:j * P + P], onesD[:, 0:1],
                                                start=k == 0 and j == 0, stop=k == KT - 1, skip_group_check=True)
                S(last, f"{tag}.ssq")

            def spread(tag, key, mark):
                need(pe, "V", f"{tag}.diag")
                S(nc.tensor.matmul(PB[:, 2, :], onesD, diag[:], start=True, stop=True), f"{tag}.spread")
                by("B", key, mark)

            def finish_mods(name):
                n = JOBS[name][2] // P
                for slot in range(4):
                    pe.wait_ge(ada_used[slot], ADA0[name] + KT)
                take("B")
                for t in range(n):
                    last = nc.tensor.matmul(flat["B"][:, t:t + 1], acc[:, t * P:t * P + P], one, start=True, stop=True)
                S(last, f"{name}.mods")
                by("B", "V", f"{name}.mod")

            def lo_of(tag):
                return lambda k: need(pe, "V", f"{tag}.lo{k}")

            def ffn(name, i_ffn, tag):
                c0 = CH[name]
                h0 = HID0[name]

                def inp(j, jj, first=None):
                    ca = c0 + 3 * j - 1 if first is None else c0
                    s = (c0 + 3 * jj - 1) % RING if first is None else c0 % RING
                    for h in range(2):
                        chunk(ca + h, (s + h) % RING, PA, tile_ffn_in, range(4 * h, 4 * h + 4), 4, "A", 0, 7, first)

                def outp(j, jj, k_first, k_last, c=None, out_tag=None):
                    pe.wait_ge(hid_lo, h0 + j + 1)
                    cc = c0 + 3 * j + 4 if c is None else c
                    s = (c0 + 3 * jj + 4) % RING if c is None else c % RING
                    pe.wait_ge(lo_ready, cc + 1)
                    for k in range(2):
                        for m in range(KT):
                            last = mm3(PY[:, m, :], s, tile_out(k, m), (oph["B"], opl["B"]), lambda t_, k=k: t_[:, k, :],
                                       k_first and k == 0 and m % 2 == 0, k_last and k == 1)
                            if out_tag and k == 1 and m in (1, 3, 5):
                                S(last, f"{out_tag}.bank{m // 2}")
                    last.then_inc(multiplied, 1)

                take("A")
                inp(0, 0, lo_of(tag))
                take("Y")
                pe.wait_ge(hid_made, h0 + 1)
                inp(1, 1)
                outp(0, 0, True, False)
                with pe.Fori(0, 8) as i:
                    pe.wait_ge(hid_made, h0 + 2 + i)
                    inp(i + 2, 2)
                    outp(i + 1, 1, False, False)
                pe.wait_ge(hid_made, h0 + 10)
                inp(10, 10)
                outp(9, 9, False, False)
                finish_mods(name)
                outp(10, 10, False, True, c0 + 32, tag)
                freed["A"] = (hid_made, h0 + 11)

            def ff2(l, tag):
                c0 = CH[f"ff{l}"]
                h0 = HID0[f"ff{l}"]

                def inp(j, jj, first=None):
                    c = c0 + 2 * j - 1 if first is None else c0
                    s = (c0 + 2 * jj - 1) % RING if first is None else c0 % RING
                    chunk(c, s, PA, tile_in256, range(8), 2, "A", 0, 7, first)

                def outp(j, jj, k_first, k_last, c=None, out_tag=None):
                    pe.wait_ge(hid_lo, h0 + j + 1)
                    cc = c0 + 2 * j + 2 if c is None else c
                    s = (c0 + 2 * jj + 2) % RING if c is None else c % RING
                    pe.wait_ge(lo_ready, cc + 1)
                    for k in range(2):
                        for m in range(KT):
                            last = mm3(PY[:, m, :], s, tile_out(k, m), (oph["B"], opl["B"]), lambda t_, k=k: t_[:, k, :],
                                       k_first and k == 0 and m % 2 == 0, k_last and k == 1)
                            if out_tag and k == 1 and m in (1, 3, 5):
                                S(last, f"{out_tag}.bank{m // 2}")
                    last.then_inc(multiplied, 1)

                take("A")
                inp(0, 0, lo_of(tag))
                take("Y")
                for j in range(1, 4):
                    pe.wait_ge(act_made, HID0[f"ff{l}"] + j)
                    inp(j, j)
                    outp(j - 1, j - 1, j == 1, False)
                with pe.Fori(0, 4) as i:
                    for jj in range(4, 7):
                        pe.wait_ge(act_made, HID0[f"ff{l}"] + i * 3 + jj)
                        inp(i * 3 + jj, jj)
                        outp(i * 3 + jj - 1, jj - 1, False, False)
                if l == 0:
                    finish_mods("ff0")
                outp(15, 15, False, True, c0 + 31, tag)
                freed["A"] = (act_made, HID0[f"ff{l}"] + 16)

            def boundary(sub, nsub):
                if not sub.startswith("b"):
                    ssq(f"{sub}.y")
                    spread(f"{sub}.y", "S", f"{sub}.y.rstd")
                ssq(f"{nsub}.x")
                spread(f"{nsub}.x", "V", f"{nsub}.t7")

            pe.wait_ge(base_in, 16)
            ssq("00.x")
            spread("00.x", "S", "00.x.rstd")
            finish_mods("first")
            ffn("ffn00", 0, "00")
            by("Y", "V", "00.u7")
            boundary("00", "01")
            for g in range(6):
                buf = "AB"[g % 2]
                take(buf)
                group512(CH["conv_in"] + 2 * g, buf, "A", lo_of("01") if g == 0 else None)
                by(buf, *(("S", f"conv{g}") if g < 4 else ("V", f"conv{g}")))
            out1024(CH["conv_out"], "B", "01", lambda k: need(pe, "V", f"conv.lo{k // 4}"))
            by("Y", "V", "01.u7")
            boundary("01", "02")
            ffn("ffn01", 1, "02")
            by("Y", "V", "02.u7")
            boundary("02", "10")
            for g in range(3):
                buf = "ABA"[g]
                take(buf)
                group512(CH["kv"] + 2 * g, buf, "B", lo_of("kv") if g == 0 else None)
                by(buf, "S", f"kv{g}")
            pe.wait_ge(nsa_in, 16)
            for kv in range(2):
                buf = "BA"[kv]
                take(buf)
                need(pe, "S", "kv0")
                for g in range(GROUPS):
                    last = nc.tensor.matmul(PS[buf][:, g, :], selu[:, g % 2, :], kvc[:, 2 * kv + g // 2, :],
                                            start=True, stop=True)
                S(last, f"dup{kv}")
                by(buf, "V", f"blk{kv}")
            take("Y")
            for n_, br in enumerate(("slc", "win")):
                need(pe, "S", f"kv{n_ + 1}")
                for a in range(2):
                    for jc in range(2):
                        last = nc.tensor.transpose(flat["Y"][:, (n_ * 4 + jc * 2 + a) * P:(n_ * 4 + jc * 2 + a + 1) * P],
                                                   vtmp[br][:, a, jc * P:jc * P + P], ident)
            S(last, "vtrans")
            by("Y", "S", "vtok")
            take("A")
            bh, bl = (oph["B"][:].rearrange("p a b -> p (a b)"), opl["B"][:].rearrange("p a b -> p (a b)"))
            for kv in range(2):
                need(pe, "V", f"blo{kv}")
                for h in range(2):
                    c = CH["cmp"] + 2 * kv + h
                    pe.wait_ge(lo_ready, c + 1)
                    for k in range(8):
                        for m in range(2):
                            last = mm3(PA[:, 2 * kv + m, 0:60], c % RING, tile_in256(k, m), (bh, bl),
                                       lambda t_, kk=8 * h + k, kv=kv: t_[:, (kv * 16 + kk) * 60:(kv * 16 + kk) * 60 + 60],
                                       h == 0 and k == 0 and m == 0, h == 1 and k == 7)
                    last.then_inc(multiplied, 1)
            by("A", "S", "gelu")
            need(pe, "S", "gelu")
            pe.wait_ge(cmp_in, 64)
            take("B")
            for m in range(2):
                last = nc.tensor.matmul(PB[:, 0, 0:60], w2k[:, m, :], hidc[:, 0, m, :], start=m == 0, stop=m == 1)
            for g in range(GROUPS):
                for m in range(2):
                    last = nc.tensor.matmul(PB[32 * g:32 * g + N_CMP, 2, 0:64], hidc[:, 1, m, g * N_CMP:(g + 1) * N_CMP],
                                            w2v[:, m, :], start=m == 0, stop=m == 1, tile_position=(0, 32 * g))
            S(last, "cmpkv")
            by("B", "V", "vcmp")
            ffn("ffn10", 2, "10")
            by("Y", "V", "10.u7")
            boundary("10", "11")
            for g in range(2):
                buf = "AB"[g]
                take(buf)
                group512(CH["nsa_in"] + 2 * g, buf, "A", lo_of("11") if g == 0 else None)
                by(buf, "S", f"q{g}")
            take("A")
            c = CH["nsa_in"] + 4
            pe.wait_ge(lo_ready, c + 1)
            for ic in range(2):
                for k in range(KT):
                    o_ = flat["A"][:, ic * 48:ic * 48 + 48]
                    ts = slice(ic * P, ic * P + P)
                    wh_, wl_ = whi[c % RING][:, k * 48:k * 48 + 48], wlo[c % RING][:, k * 48:k * 48 + 48]
                    nc.tensor.matmul(o_, oph["A"][:, k, ts], wh_, start=k == 0, stop=False)
                    nc.tensor.matmul(o_, oph["A"][:, k, ts], wl_, start=False, stop=False)
                    last = nc.tensor.matmul(o_, opl["A"][:, k, ts], wh_, start=False, stop=k == KT - 1)
            last.then_inc(multiplied, 1)
            by("A", "S", "gexp")
            take("B")
            for u in range(2):
                for ic in range(2):
                    for r in range(R):
                        for a in range(2):
                            g = 2 * a + u
                            o_ = ic * 120 + (r * 2 + a) * N_CMP
                            last = nc.tensor.matmul(flat["B"][:, u * 512 + o_:u * 512 + o_ + N_CMP],
                                                    qf[u * 64:u * 64 + 64, a * 4 + r, ic * P:ic * P + P],
                                                    kcmp[u * 64:u * 64 + 64, g * N_CMP:(g + 1) * N_CMP], start=True, stop=True)
            S(last, "scmp")
            by("B", "V", "scmp")

            UNITS = [(ic, a, r) for ic in range(2) for a in range(2) for r in range(R)]

            def scores(n_):
                ic, a, r = UNITS[n_]
                buf = "AB"[n_ % 2]
                take(buf)
                for u in range(2):
                    for b_, kk in enumerate((kslc, kwin)):
                        last = nc.tensor.matmul(PS[buf][:, 2 * u + b_, 0:(ic + 1) * P],
                                                qf[u * 64:u * 64 + 64, a * 4 + r, ic * P:ic * P + P],
                                                kk[u * 64:u * 64 + 64, a, 0:(ic + 1) * P], start=True, stop=True)
                S(last, f"sc{n_}")
                by(buf, "V", f"s{n_}")

            scores(0)
            scores(1)
            take("Y")
            for ic in range(2):
                need(pe, "G", "ppad")
                need(pe, "V", f"pc{ic}")
                for r in range(R):
                    last = nc.tensor.transpose(flat["Y"][:, (ic * 4 + r) * P:(ic * 4 + r + 1) * P],
                                               pc32[:, ic, 4 * r:4 * r + 4, :].rearrange("p h n -> p (h n)"), ident)
            S(last, "pct")
            by("Y", "S", "ptc")
            for n_, (ic, a, r) in enumerate(UNITS):
                need(pe, "V", f"p{n_}")
                take("Y")
                for jc in range(ic + 1):
                    for x_ in range(4):
                        last = nc.tensor.transpose(flat["Y"][:, (jc * 4 + x_) * P:(jc * 4 + x_ + 1) * P],
                                                   ssb[n_ % 2][:, x_, jc * P:jc * P + P], ident)
                S(last, f"pt{n_}")
                by("Y", "S", f"pt{n_}")
                if n_ + 2 < len(UNITS):
                    scores(n_ + 2)
                need(pe, "S", f"pt{n_}")
                if n_ >= 2:
                    need(pe, "V", f"olo{n_ - 2}")
                oo = PY[:, 4 + 2 * (n_ % 2), 0:P]
                for u in range(2):
                    g = 2 * a + u
                    nc.tensor.matmul(oo[u * 64:u * 64 + 64], vcmp[32 * g:32 * g + 32, :],
                                     ptc[32 * g:32 * g + 32, ic, r, :], start=True, stop=False, tile_position=(32 * g, 64 * u))
                for u in range(2):
                    g = 2 * a + u
                    for b_, br in enumerate(("slc", "win")):
                        for jc in range(ic + 1):
                            last = nc.tensor.matmul(oo[u * 64:u * 64 + 64], vtok[br][:, jc, g * 64:g * 64 + 64],
                                                    ptsb[:, jc * 4 + 2 * u + b_, :], start=False,
                                                    stop=b_ == 1 and jc == ic, tile_position=(0, 64 * u))
                S(last, f"o{n_}")
            need(pe, "V", "olo15")
            out1024(CH["nsa_out"], "B", "11")
            by("Y", "V", "11.u7")
            boundary("11", "12")
            ffn("ffn11", 3, "12")
            by("Y", "V", "12.u7")
            boundary("12", "b00")
            for l in range(2):
                c = CH[f"mix{l}"]

                def group(name, buf, key="S", before=None, op="A"):
                    nonlocal c
                    take(buf)
                    group512(c, buf, op, before)
                    c += 2
                    by(buf, key, f"b{l}.{name}")

                group("q", "A", before=lo_of(f"b{l}0"))
                group("k", "B")
                group("v0", "A")
                pe.wait_ge(b2_in, 32)
                take("Y")
                need(pe, "S", f"b{l}.k")
                for t in range(8):
                    last = nc.tensor.matmul(PY[:, t, :], rotm, t3(X[0], 8)[:, t, :], start=True, stop=True)
                S(last, f"b{l}.rot")
                by("Y", "V", f"b{l}.rot")
                group("v1", "B")
                group("g0", "A")
                take("Y")
                need(pe, "S", f"b{l}.v1")
                for jc in range(2):
                    for t in range(8):
                        last = nc.tensor.transpose(flat["Y"][:, (jc * 8 + t) * P:(jc * 8 + t + 1) * P],
                                                   t3(X[1], 8)[:, t, jc * P:jc * P + P], ident)
                S(last, f"b{l}.vt")
                by("Y", "S", f"b{l}.vtok")
                group("g1", "B")
                group("u0", "A")
                take("Y")
                need(pe, "V", f"b{l}.rotk")
                X0 = t3(X[0], 8)
                for h in range(4):
                    nc.tensor.matmul(PY[:, 2 * h, :], X0[:, 4 + h, 0:P], X0[:, h, :], start=True, stop=True)
                    last = nc.tensor.matmul(PY[:, 2 * h + 1, 0:P], X0[:, 4 + h, P:2 * P], X0[:, h, P:2 * P],
                                            start=True, stop=True)
                S(last, f"b{l}.sc")
                by("Y", "V", f"b{l}.dec")
                group("u1", "B")
                take("Y")
                sd_ = t3(tmp8[:].rearrange("p a b -> p (a b)")[:, 0:1536], 4)
                vt = X[3].rearrange("p (j e) -> p j e", j=2)
                for h in range(4):
                    for e in range(2):
                        t = 2 * h + e
                        nc.tensor.matmul(PY[:, t, :], vt[:, 0, t * P:t * P + P], sd_[:, h, 0:T], start=e == 0, stop=False,
                                         skip_group_check=True)
                        last = nc.tensor.matmul(PY[:, t, P:T], vt[:, 1, t * P:t * P + P], sd_[:, h, T:T + P], start=False,
                                                stop=True, skip_group_check=True)
                S(last, f"b{l}.o")
                by("Y", "V", f"b{l}.rety")
                group("s0", "A")
                take("B")
                for h in range(4):
                    need(pe, "S", f"b{l}.osq{h}")
                    for e in range(2):
                        last = nc.tensor.matmul(PB[:, h, :], onesD, tmp8[:, 2 * h + e, :], start=e == 0 and h % 2 == 0,
                                                stop=e == 1, skip_group_check=True)
                S(last, f"b{l}.ossq")
                by("B", "S", f"b{l}.osd")
                group("s1", "A")
                group("p0", "B")
                group("p1", "A")
                ssq(f"b{l}.v")
                group("h00", "A")
                spread(f"b{l}.v", "S", f"b{l}.v.rstd")
                group("h01", "B")
                take("A")
                need(pe, "G", f"b{l}.tril")
                for g in range(4):
                    last = nc.tensor.transpose(flat["A"][:, g * P:g * P + P], wsr[:, g * P:g * P + P], ident)
                S(last, f"b{l}.wt")
                by("A", "S", f"b{l}.wT")
                group("r00", "A", "V", lambda k, l=l: need(pe, "V", f"b{l}.rlo") if k == 0 else None, "B")
                group("r01", "B", "V", None, "B")
                take("Y")
                need(pe, "V", f"b{l}.vn7")
                for jc in range(2):
                    for t in range(8):
                        last = nc.tensor.transpose(flat["Y"][:, (jc * 8 + t) * P:(jc * 8 + t + 1) * P],
                                                   t3(X[5], 8)[:, t, jc * P:jc * P + P], ident)
                S(last, f"b{l}.vnt")
                by("Y", "S", f"b{l}.vntok")
                group("h10", "A")
                take("Y")
                for t in range(8):
                    for n_ in range(2):
                        last = nc.tensor.matmul(PY[:, t, n_ * P:n_ * P + P], vt[:, n_, t * P:t * P + P], wT[:, t // 2, :],
                                                start=t % 2 == 0 and n_ == 0, stop=True, skip_group_check=True)
                S(last, f"b{l}.mix")
                by("Y", "V", f"b{l}.mix")
                group("h11", "B")
                group("r10", "A", "V", lambda k, l=l: need(pe, "V", f"b{l}.slo") if k == 0 else None, "B")
                group("r11", "B", "V", None, "B")
                group("h20", "A")
                take("Y")
                need(pe, "V", f"b{l}.pooled")
                pe.wait_ge(lay_in, 48 * (l + 1))
                wp = wpool.rearrange("p (g k n) -> p g k n", g=4, k=2)
                for g in range(4):
                    for m in range(2):
                        for k in range(2):
                            last = nc.tensor.matmul(PY[:, 2 * g + m, :], wp[:, g, k, m * P:m * P + P],
                                                    t3(X[3], 8)[:, 2 * g + k, :], start=m == 0 and k == 0, stop=k == 1,
                                                    skip_group_check=True)
                S(last, f"b{l}.pm")
                by("Y", "V", f"b{l}.pm7")
                group("h21", "B")
                group("r20", "A", "V", lambda k, l=l: need(pe, "V", f"b{l}.plo") if k == 0 else None, "B")
                group("r21", "B", "V", None, "B")
                out1024(c, "A", f"b{l}0", lambda k, l=l: need(pe, "V", f"b{l}.mlo{k // 4}"))
                by("Y", "V", f"b{l}0.u7")
                boundary(f"b{l}0", f"b{l}1")
                ff2(l, f"b{l}1")
                by("Y", "V", f"b{l}1.u7")
                boundary("b01" if l == 0 else "b11", "b10" if l == 0 else "fin")

        @block.scalar
        def _(act):
            S = Steps(steps["S"], "S", seen)
            nxt = [0]
            AC = nc.scalar.activation

            def prep(c, slot, w=CHUNK):
                act.wait_ge(raw_ready[slot], 32 * (c // RING + 1))
                if c >= RING:
                    act.wait_ge(multiplied, c - (RING - 1))
                AC(whi[slot][:, 0:w], raw[slot][:, 0:w], ACT.Copy).then_inc(hi_ready, 1)

            def prep_to(c, w=CHUNK):
                while nxt[0] < min(c, N_CHUNKS):
                    prep(nxt[0], nxt[0] % RING, 384 if nxt[0] == CH["nsa_in"] + 4 else w)
                    nxt[0] += 1

            def dyn(c0, per, i, k):
                c = c0 + k
                slot = c % RING
                act.wait_ge(raw_ready[slot], 32 * (c // RING + 1) + i * (32 * (per // RING)))
                act.wait_ge(multiplied, i * per + c - (RING - 1))
                AC(whi[slot][:], raw[slot][:], ACT.Copy).then_inc(hi_ready, 1)

            def squares(tag, src, wait, own=None):
                if own:
                    need(act, "S", own)
                for q in range(4):
                    wait(q)
                    S(AC(tmp8[:, 2 * q:2 * q + 2, :], src[:, 2 * q:2 * q + 2, :], ACT.Square), f"{tag}.sq{q}")

            def root(tag):
                need(act, "T", f"{tag}.ssq")
                S(AC(sd[:], flat["B"][:, 0:2], ACT.Sqrt, bias=epsc[:]), f"{tag}.sd")

            def fetch(tag):
                need(act, "T", f"{tag}.spread")
                S(AC(rstd[:], PB[:, 2, :], ACT.Copy), f"{tag}.rstd")

            def load_table(func):
                own_n = S.n
                act.wait_ge(steps["S"], own_n)
                S(AC(warm[:], epsc[:], func))

            def pre(sub, op, tag=None):
                tag = tag or sub
                for k in range(KT):
                    need(act, "V", f"{tag}.t{k}")
                    S(AC(oph[op][:, k, :], tmp8[:, k, :], ACT.Identity, bias=B_(sub)[:, k:k + 1]), f"{tag}.hi{k}")

            def boundary(sub, nsub, c_done, c_next, ops=None):
                prep_to(c_next + 2)
                load_table(ACT.Sqrt)

                def y_there(q):
                    if q < 3:
                        need(act, "T", f"{sub}.bank{q}")
                    else:
                        act.wait_ge(multiplied, c_done)

                def x_there(q):
                    if sub.startswith("b"):
                        need(act, "V", f"{sub}.u{2 * q + 1}")
                        return
                    for k in (2 * q, 2 * q + 1):
                        need(act, "G" if k in POOL_ADDS else "V", f"{sub}.x{k}")

                if not sub.startswith("b"):
                    squares(f"{sub}.y", PY, y_there)
                    root(f"{sub}.y")
                    fetch(f"{sub}.y")
                squares(f"{nsub}.x", x, x_there)
                root(f"{nsub}.x")
                for s_, op in ops or [(nsub, "A")]:
                    pre(s_, op)
                prep_to(c_next + 3)

            def ffn(name):
                c0 = CH[name]
                h0 = HID0[name]
                prep_to(c0 + 3)

                def made(j, c_in):
                    act.wait_ge(multiplied, c_in + 1)
                    AC(gact[:], PA[:, 0:2, :], ACT.Silu).then_inc(act_made, 1)

                def high(j, c_prev):
                    act.wait_ge(hid_made, h0 + j + 1)
                    act.wait_ge(multiplied, c_prev + 1)
                    AC(oph["B"][:, 0:2, :], hidf[:], ACT.Copy).then_inc(hid_hi, 1)

                made(0, c0 + 1)
                prep_to(c0 + 4)
                act.wait_ge(hid_made, h0 + 1)
                AC(oph["B"][:, 0:2, :], hidf[:], ACT.Copy).then_inc(hid_hi, 1)
                prep_to(c0 + 6)
                with act.Fori(0, 8) as i:
                    made(i + 1, i * 3 + (c0 + 3))
                    dyn(c0, 3, i, 6)
                    high(i + 1, i * 3 + (c0 + 4))
                    dyn(c0, 3, i, 7)
                    dyn(c0, 3, i, 8)
                nxt[0] = c0 + 30
                made(9, c0 + 27)
                prep_to(c0 + 31)
                high(9, c0 + 28)
                prep_to(c0 + 33)
                made(10, c0 + 30)
                prep_to(c0 + 34)
                high(10, c0 + 31)

            def ff2(l):
                c0 = CH[f"ff{l}"]
                h0 = HID0[f"ff{l}"]
                prep_to(c0 + 2)

                def made(j, c_in):
                    act.wait_ge(multiplied, c_in + 1)
                    act.wait_ge(hid_made, h0 + j)
                    act.wait_ge(hid_hi, h0 + j)
                    AC(gact[:], PA[:, 0:2, :], ACT.Relu).then_inc(act_made, 1)

                def high(j, c_prev):
                    act.wait_ge(multiplied, c_prev + 1)
                    act.wait_ge(act_made, HID0[f"ff{l}"] + j + 1)
                    AC(oph["B"][:, 0:2, :], gact[:], ACT.Square).then_inc(hid_hi, 1)

                made(0, c0)
                prep_to(c0 + 3)
                high(0, c0 - 1)
                prep_to(c0 + 4)
                for j in range(1, 4):
                    made(j, c0 + 2 * j - 1)
                    prep_to(c0 + 2 * j + 3)
                    high(j, c0 + 2 * j)
                    prep_to(c0 + 2 * j + 4)
                with act.Fori(0, 3) as i:
                    for jj in range(4, 7):
                        made(i * 3 + jj, i * 6 + (c0 + 2 * jj - 1))
                        dyn(c0, 6, i, 2 * jj + 2)
                        high(i * 3 + jj, i * 6 + (c0 + 2 * jj))
                        dyn(c0, 6, i, 2 * jj + 3)
                nxt[0] = c0 + 28
                for j in range(13, 16):
                    made(j, c0 + 2 * j - 1)
                    prep_to(min(c0 + 2 * j + 3, c0 + 32))
                    high(j, c0 + 2 * j)
                    prep_to(min(c0 + 2 * j + 4, c0 + 32))

            act.wait_ge(vec_in, 16)
            S(AC(csil[:], V("c", 0, 16), ACT.Silu), "csil")
            act.wait_ge(x_in, 16)
            need(act, "G", "consts")
            squares("00.x", x, lambda q: None)
            root("00.x")
            fetch("00.x")
            prep_to(2)
            pre("00", "A")
            ffn("ffn00")
            boundary("00", "01", CH["conv_in"], CH["conv_in"])
            for g in range(4):
                c = CH["conv_in"] + 2 * g
                prep_to(c + 4)
                act.wait_ge(multiplied, c + 2)
                dst = (cb_, cc_)[g // 2]
                S(AC(dst[:, 4 * (g % 2):4 * (g % 2) + 4, :], PS["AB"[g % 2]][:], ACT.Copy), f"conv{g}")
            prep_to(CH["conv_out"] + 1)
            for g in range(2):
                need(act, "V", f"conv.y{g}")
                S(AC(oph["B"][:, 4 * g:4 * g + 4, :], cy_[:, 4 * g:4 * g + 4, :], ACT.Copy), f"conv.hi{g}")
                prep_to(CH["conv_out"] + 2 + g)
            boundary("01", "02", CH["ffn01"], CH["ffn01"])
            ffn("ffn01")
            boundary("02", "10", CH["kv"], CH["kv"], [("kv", "B"), ("10", "A")])
            for g in range(3):
                c = CH["kv"] + 2 * g
                prep_to(c + 4)
                act.wait_ge(multiplied, c + 2)
                ps = PS["ABA"[g]]
                if g == 0:
                    S(AC(kvc, ps[:], ACT.Copy), "kv0")
                else:
                    S(AC((kslc, kwin)[g - 1], ps[:, 0:2, :], ACT.Copy))
                    S(AC(vtmp[("slc", "win")[g - 1]], ps[:, 2:4, :], ACT.Copy), f"kv{g}")
            need(act, "T", "vtrans")
            for n_, br in enumerate(("slc", "win")):
                S(AC(vtok[br], t3(flat["Y"][:, n_ * 512:n_ * 512 + 512], 2), ACT.Copy), "vtok")
            bh = oph["B"][:].rearrange("p a b -> p (a b)")
            tf = tmp8[:].rearrange("p a b -> p (a b)")
            act.wait_ge(multiplied, CH["kv"] + 6)
            for kv in range(2):
                need(act, "V", f"blk{kv}")
                S(AC(bh[:, kv * 960:kv * 960 + 960], tf[:, kv * 960:kv * 960 + 960], ACT.Copy), f"bhi{kv}")
            prep_to(CH["cmp"] + 4)
            act.wait_ge(multiplied, CH["cmp"] + 4)
            S(AC(hidc.rearrange("p k m c -> p (k m) c"), PA[:, :, 0:60], ACT.Gelu_apprx_tanh), "gelu")
            ffn("ffn10")
            boundary("10", "11", CH["nsa_in"], CH["nsa_in"])
            for g in range(2):
                c = CH["nsa_in"] + 2 * g
                prep_to(c + 4)
                act.wait_ge(multiplied, c + 2)
                S(AC(qf[:, 4 * g:4 * g + 4, :], PS["AB"[g]][:], ACT.Copy, scale=DH ** -0.5), f"q{g}")
            prep_to(CH["nsa_in"] + 6)
            act.wait_ge(multiplied, CH["nsa_in"] + 5)
            S(AC(gexp, flat["A"][:, 0:96], ACT.Exp, scale=-1.0), "gexp")
            prep_to(CH["nsa_in"] + 8)
            UNITS = [(ic, a, r) for ic in range(2) for a in range(2) for r in range(R)]
            for ic in range(2):
                need(act, "V", f"csub{ic}")
                S(AC(pc32[:, ic, :, 0:N_CMP], sc_[:, ic], ACT.Exp), f"cexp{ic}")

            def exps(n_):
                ic = UNITS[n_][0]
                need(act, "V", f"m{n_}")
                for x_ in range(4):
                    S(AC(ssb[n_ % 2][:, x_, 0:(ic + 1) * P], ssb[n_ % 2][:, x_, 0:(ic + 1) * P], ACT.Exp,
                         bias=small[:, 4 * (n_ % 2) + x_:4 * (n_ % 2) + x_ + 1],
                         accum_out=small[:, 8 + 4 * (n_ % 2) + x_:9 + 4 * (n_ % 2) + x_]), f"e{n_}")

            exps(0)
            need(act, "T", "pct")
            S(AC(ptc.rearrange("p i r c -> p (i r c)"), flat["Y"][:, 0:1024], ACT.Copy), "ptc")
            for n_, (ic, a, r) in enumerate(UNITS):
                if n_ + 1 < 16:
                    exps(n_ + 1)
                need(act, "T", f"pt{n_}")
                if n_:
                    need(act, "T", f"o{n_ - 1}")
                nb = 4 * (ic + 1)
                S(AC(ptsb[:, 0:nb, :].rearrange("p a b -> p (a b)"), flat["Y"][:, 0:nb * P], ACT.Copy), f"pt{n_}")
                need(act, "T", f"o{n_}")
                S(AC(oph["B"][:, a * 4 + r, ic * P:ic * P + P], PY[:, 4 + 2 * (n_ % 2), 0:P], ACT.Copy), f"ohi{n_}")
            boundary("11", "12", CH["ffn11"], CH["ffn11"])
            ffn("ffn11")
            boundary("12", "b00", CH["mix0"], CH["mix0"])
            for l in range(2):
                c = CH[f"mix{l}"]
                q_ = f"b{l}."
                if l == 0:
                    need(act, "V", "ang")
                    S(AC(sin_, sin_, ACT.Sin))
                    S(AC(cos_, cos_, ACT.Sin), "sincos")

                def group(name, i, buf, dst, func, wait=None):
                    prep_to(c + 2 * i + 4)
                    act.wait_ge(multiplied, c + 2 * i + 2)
                    if wait:
                        need(act, *wait)
                    S(AC(dst, PS[buf][:], func), q_ + name)

                def half(i, h):
                    return t3(X[i], 8)[:, 4 * h:4 * h + 4, :]

                group("q", 0, "A", half(0, 0), ACT.Copy)
                group("k", 1, "B", half(0, 1), ACT.Copy)
                group("v0", 2, "A", half(1, 0), ACT.Copy)
                group("v1", 3, "B", half(1, 1), ACT.Copy)
                group("g0", 4, "A", half(2, 0), ACT.Silu)
                need(act, "T", q_ + "vt")
                S(AC(X[3], flat["Y"], ACT.Copy), q_ + "vtok")
                group("g1", 5, "B", half(2, 1), ACT.Silu)
                group("u0", 6, "A", half(4, 0), ACT.Gelu_apprx_tanh)
                group("u1", 7, "B", half(4, 1), ACT.Gelu_apprx_tanh)
                need(act, "T", q_ + "o")
                for h in range(4):
                    S(AC(tmp8[:, 2 * h:2 * h + 2, :], PY[:, 2 * h:2 * h + 2, :], ACT.Square), q_ + f"osq{h}")
                group("s0", 8, "A", half(5, 0), ACT.Gelu_apprx_tanh)
                need(act, "T", q_ + "ossq")
                S(AC(t3(rr, 4), PB[:], ACT.Sqrt, bias=epsc[:], scale=D / 256.0), q_ + "osd")
                group("s1", 9, "A", half(5, 1), ACT.Gelu_apprx_tanh)
                need(act, "V", q_ + "rety2")
                S(AC(oph["B"][:], tmp8[:], ACT.Copy), q_ + "rhi")
                group("p0", 10, "B", half(1, 0), ACT.Copy)
                need(act, "V", q_ + "rlo")
                squares(f"b{l}.v", t3(X[5], 8), lambda q: None, own=q_ + "s1")
                group("p1", 11, "A", half(1, 1), ACT.Copy)
                root(f"b{l}.v")
                group("h00", 12, "A", half(0, 0), ACT.Sigmoid)
                fetch(f"b{l}.v")
                group("h01", 13, "B", half(0, 1), ACT.Sigmoid)
                need(act, "T", q_ + "wt")
                S(AC(wT.rearrange("p g t -> p (g t)"), flat["A"][:, 0:512], ACT.Copy), q_ + "wT")
                prep_to(c + 34)
                need(act, "T", q_ + "vnt")
                S(AC(X[3], flat["Y"], ACT.Copy), q_ + "vntok")
                group("h10", 16, "A", half(0, 0), ACT.Sigmoid, ("V", q_ + "m0.0"))
                need(act, "V", q_ + "sgu")
                act.wait_ge(multiplied, c + 32)
                S(AC(oph["B"][:], tmp8[:], ACT.Copy), q_ + "shi")
                group("h11", 17, "B", half(0, 1), ACT.Sigmoid, ("V", q_ + "m0.1"))
                group("h20", 20, "A", half(0, 0), ACT.Sigmoid, ("V", q_ + "m1.0"))
                need(act, "V", q_ + "pm7")
                act.wait_ge(multiplied, c + 40)
                S(AC(oph["B"][:], tmp8[:], ACT.Copy), q_ + "phi")
                group("h21", 21, "B", half(0, 1), ACT.Sigmoid, ("V", q_ + "m1.1"))
                prep_to(c + 50)
                for h in range(2):
                    need(act, "V", q_ + f"m2.{h}")
                    act.wait_ge(multiplied, c + 44)
                    S(AC(oph["A"][:, 4 * h:4 * h + 4, :], macc(h), ACT.Copy), q_ + f"mhi{h}")
                boundary(f"b{l}0", f"b{l}1", CH[f"ff{l}"], CH[f"ff{l}"])
                ff2(l)
                if l == 0:
                    boundary("b01", "b10", CH["mix1"], CH["mix1"])
                else:
                    squares("fin.x", x, lambda q: need(act, "V", f"b11.u{2 * q + 1}"))
                    root("fin.x")

        @block.vector
        def _(dve):
            S = Steps(steps["V"], "V", seen)
            nxt = [0]
            TT, STT, TS = nc.vector.tensor_tensor, nc.vector.scalar_tensor_tensor, nc.vector.tensor_scalar

            def own(v):
                dve.wait_ge(steps["V"], v)

            def settle():
                dve.wait_ge(steps["V"], S.n)

            def split(slot, w=CHUNK):
                TT(wlo[slot][:, 0:w], raw[slot][:, 0:w], whi[slot][:, 0:w].bitcast(F32), ALU.subtract).then_inc(lo_ready, 1)

            def prep_to(c):
                while nxt[0] < min(c, N_CHUNKS):
                    dve.wait_ge(hi_ready, nxt[0] + 1)
                    split(nxt[0] % RING, 384 if nxt[0] == CH["nsa_in"] + 4 else CHUNK)
                    nxt[0] += 1

            def dyn(c0, per, i, k):
                dve.wait_ge(hi_ready, i * per + (c0 + k + 1))
                split((c0 + k) % RING)

            def ada(name, f, i=0, per=0):
                which, slots, _ = JOBS[name]
                slot, width, o_, loads = slots[f % 4]
                k, n = f // 4, 16 * len(loads)
                cs = csil[:, bass.ds(i * per + (KT * which + k), 1)] if per else csil[:, KT * which + k:KT * which + k + 1]
                dve.wait_ge(ada_ready[slot], i * (per * n) + (16 * LOADS0[name][slot] + n * (k + 1)))
                if ADA0[name] + k > 0:
                    dve.wait_ge(ada_used[slot], i * per + (ADA0[name] + k))
                STT(acc[:, o_:o_ + width], slab[slot][:, 0:width], cs, acc[:, o_:o_ + width],
                    ALU.mult, ALU.add).then_inc(ada_used[slot], 1)

            def mods(name):
                need(dve, "T", f"{name}.mods")
                for t0, n, m0, bias in MODS[name]:
                    v = S(TT(mod[:, m0:m0 + n], flat["B"][:, t0:t0 + n], bias, ALU.add), f"{name}.mod")
                own(v)
                for s_ in SCALES[name]:
                    sh = SUB[s_]["shift"]
                    v = S(STT(A_(s_), mod[:, sh + 8:sh + 16], 1.0, SUB[s_]["g_pre"], ALU.add, ALU.mult))
                for s_ in GATES[name]:
                    sh = SUB[s_]["shift"]
                    if SUB[s_]["g_post"] is not None:
                        v = S(STT(G_(s_), mod[:, sh + 16:sh + 24], SUB[s_]["w"], SUB[s_]["g_post"], ALU.mult, ALU.mult))
                    else:
                        v = S(TS(G_(s_), mod[:, sh + 16:sh + 24], 1.0, None, ALU.mult))
                own(v)

            def inverse(tag):
                need(dve, "S", f"{tag}.sd")
                settle()
                own(S(nc.vector.reciprocal(rsd[:], sd[:])))
                for j in range(2):
                    S(TS(diag[:, j * P:j * P + P], ident, rsd[:, j:j + 1], float(D), ALU.mult, ALU.mult), f"{tag}.diag")

            def spread_of(tag):
                need(dve, "T", f"{tag}.spread")
                return PB[:, 2, :]

            def pre(sub, op, rs, hold=None):
                if hold:
                    settle()
                if hold:
                    settle()

                def low(k):
                    need(dve, "S", f"{sub}.hi{k}")
                    S(STT(opl[op][:, k, :], tmp8[:, k, :], B_(sub)[:, k:k + 1], oph[op][:, k, :].bitcast(F32),
                          ALU.add, ALU.subtract), f"{sub}.lo{k}")

                for k in range(KT):
                    if hold:
                        need(dve, "S", f"{hold}.hi{k}")
                    S(STT(tmp8[:, k, :], x[:, k, :], A_(sub)[:, k:k + 1], rs, ALU.mult, ALU.mult), f"{sub}.t{k}")
                    if k > 0:
                        low(k - 1)
                low(KT - 1)

            def boundary(sub, nsub, c_done, c_next, ops=None, last=False):
                prep_to(c_next + 2)
                if not sub.startswith("b"):
                    inverse(f"{sub}.y")
                    need(dve, "S", f"{sub}.y.rstd")

                    def add(k):
                        if k not in POOL_ADDS:
                            need(dve, "V", f"{sub}.u{k}")
                            S(TT(x[:, k, :], x[:, k, :], tmp8[:, k, :], ALU.add), f"{sub}.x{k}")

                    for k in range(KT):
                        S(STT(tmp8[:, k, :], PY[:, k, :], G_(sub)[:, k:k + 1], rstd[:], ALU.mult, ALU.mult), f"{sub}.u{k}")
                        if k > 0:
                            add(k - 1)
                    add(KT - 1)
                else:
                    for k in range(KT):
                        if k == 6:
                            dve.wait_ge(multiplied, c_done)
                        elif k % 2 == 0:
                            need(dve, "T", f"{sub}.bank{k // 2}")
                        S(STT(x[:, k, :], PY[:, k, :], G_(sub)[:, k:k + 1], x[:, k, :], ALU.mult, ALU.add), f"{sub}.u{k}")
                if last:
                    return
                inverse(f"{nsub}.x")
                rs = spread_of(f"{nsub}.x")
                hold = None
                for s_, op in ops or [(nsub, "A")]:
                    pre(s_, op, rs, hold)
                    hold = s_
                prep_to(c_next + 3)

            def ffn(name):
                c0 = CH[name]
                h0 = HID0[name]
                prep_to(c0 + 3)

                def made(j):
                    dve.wait_ge(act_made, h0 + j + 1)
                    if not (isinstance(j, int) and h0 + j == 0):
                        dve.wait_ge(hid_lo, h0 + j)
                    TT(hidf[:], gact[:], PA[:, 2:4, :], ALU.mult).then_inc(hid_made, 1)

                def low(j):
                    dve.wait_ge(hid_hi, h0 + j + 1)
                    TT(opl["B"][:, 0:2, :], hidf[:], oph["B"][:, 0:2, :].bitcast(F32), ALU.subtract).then_inc(hid_lo, 1)

                made(0)
                prep_to(c0 + 4)
                low(0)
                prep_to(c0 + 6)
                need(dve, "G", f"{name}.zero")
                for f in range(4):
                    ada(name, f)
                with dve.Fori(0, 2) as i:
                    for u in range(4):
                        made(i * 4 + (u + 1))
                        dyn(c0, 12, i, 3 * u + 6)
                        ada(name, 4 + 3 * u, i, 3)
                        low(i * 4 + (u + 1))
                        dyn(c0, 12, i, 3 * u + 7)
                        ada(name, 5 + 3 * u, i, 3)
                        dyn(c0, 12, i, 3 * u + 8)
                        ada(name, 6 + 3 * u, i, 3)
                nxt[0] = c0 + 30
                made(9)
                prep_to(c0 + 31)
                ada(name, 28)
                low(9)
                ada(name, 29)
                prep_to(c0 + 33)
                ada(name, 30)
                ada(name, 31)
                made(10)
                prep_to(c0 + 34)
                low(10)
                mods(name)

            def ff2(l):
                c0 = CH[f"ff{l}"]
                h0 = HID0[f"ff{l}"]
                prep_to(c0 + 2)

                def made(j):
                    dve.wait_ge(act_made, h0 + j + 1)
                    dve.wait_ge(hid_lo, h0 + j)
                    TT(hidf[:], gact[:], gact[:], ALU.mult).then_inc(hid_made, 1)

                def low(j):
                    dve.wait_ge(hid_made, h0 + j + 1)
                    dve.wait_ge(hid_hi, h0 + j + 1)
                    TT(opl["B"][:, 0:2, :], hidf[:], oph["B"][:, 0:2, :].bitcast(F32), ALU.subtract).then_inc(hid_lo, 1)

                made(0)
                prep_to(c0 + 3)
                low(0)
                prep_to(c0 + 4)
                for j in range(1, 3):
                    made(j)
                    prep_to(c0 + 2 * j + 3)
                    low(j)
                    prep_to(c0 + 2 * j + 4)
                    if l == 0:
                        if j == 1:
                            need(dve, "G", "ff0.zero")
                        for f in range(4 * j - 4, 4 * j):
                            ada("ff0", f)
                with dve.Fori(0, 2) as i:
                    for u in range(6):
                        made(i * 6 + (u + 3))
                        dyn(c0, 12, i, 2 * u + 8)
                        if l == 0:
                            ada("ff0", 8 + 2 * u, i, 3)
                        low(i * 6 + (u + 3))
                        dyn(c0, 12, i, 2 * u + 9)
                        if l == 0:
                            ada("ff0", 9 + 2 * u, i, 3)
                nxt[0] = c0 + 32
                made(15)
                low(15)
                if l == 0:
                    mods("ff0")

            need(dve, "S", "csil")
            inverse("00.x")
            need(dve, "G", "first.zero")
            for f in range(4 * KT):
                ada("first", f)
            mods("first")
            prep_to(2)
            need(dve, "S", "00.x.rstd")
            pre("00", "A", rstd[:])
            ffn("ffn00")
            boundary("00", "01", CH["conv_in"], CH["conv_in"])
            for g in range(4):
                prep_to(CH["conv_in"] + 2 * g + 4)
            need(dve, "G", "cpad")
            for g in range(2):
                c = CH["conv_in"] + 8 + 2 * g
                prep_to(c + 4)
                dve.wait_ge(multiplied, c + 2)
                need(dve, "S", f"conv{2 + g}")
                ts = range(4 * g, 4 * g + 4)
                own(S(TT(cv_[:, 4 * g:4 * g + 4, 2:258], PS["AB"[g]][:], cc_[:, 4 * g:4 * g + 4, :], ALU.mult), f"conv{4 + g}"))
                for t in ts:
                    v = S(TS(cy_[:, t, :], cv_[:, t, 0:256], V("a_conv", t, 1), None, ALU.mult))
                for tap in (1, 2):
                    for n_, t in enumerate(ts):
                        own(v - 3 + n_)
                        S(STT(cy_[:, t, :], cv_[:, t, tap:tap + 256], V("a_conv", 8 * tap + t, 1), cy_[:, t, :],
                              ALU.mult, ALU.add))
                    v += 4
                own(v)
                own(S(TT(cy_[:, 4 * g:4 * g + 4, :], cy_[:, 4 * g:4 * g + 4, :], cb_[:, 4 * g:4 * g + 4, :], ALU.mult),
                      f"conv.y{g}"))
                need(dve, "S", f"conv.hi{g}")
                S(TT(opl["B"][:, 4 * g:4 * g + 4, :], cy_[:, 4 * g:4 * g + 4, :], oph["B"][:, 4 * g:4 * g + 4, :].bitcast(F32),
                     ALU.subtract), f"conv.lo{g}")
            boundary("01", "02", CH["ffn01"], CH["ffn01"])
            ffn("ffn01")
            boundary("02", "10", CH["kv"], CH["kv"], [("kv", "B"), ("10", "A")])
            prep_to(CH["kv"] + 6)
            tf = tmp8[:].rearrange("p a b -> p (a b)")
            bh, bl = (z["B"][:].rearrange("p a b -> p (a b)") for z in (oph, opl))
            dve.wait_ge(cmp_in, 64)
            for k in range(KT):
                need(dve, "S", f"10.hi{k}")
            for kv in range(2):
                need(dve, "T", f"dup{kv}")
                ps = PS["BA"[kv]]
                for g in range(GROUPS):
                    for hf in range(2):
                        ps_h = slice(64 * hf, 64 * hf + 64)
                        for l8 in range(2):
                            src = ps[ps_h, g, 16 * l8:16 * l8 + 16 * N_CMP].rearrange("p (n l b) -> p l n b", l=8, b=2)[:, :, :, hf]
                            dst = tf[ps_h, kv * 960:kv * 960 + 960].rearrange("p (l g n) -> p l g n", l=16, g=4)[:, 8 * l8:8 * l8 + 8, g, :]
                            ps_pos = pos2[ps_h, kv, 8 * l8:8 * l8 + 8].unsqueeze(2).broadcast_to([64, 8, N_CMP])
                            v = S(TT(dst, src, ps_pos, ALU.add), f"blk{kv}")
            for kv in range(2):
                need(dve, "S", f"bhi{kv}")
                sl = slice(kv * 960, kv * 960 + 960)
                S(TT(bl[:, sl], tf[:, sl], bh[:, sl].bitcast(F32), ALU.subtract), f"blo{kv}")
            prep_to(CH["cmp"] + 4)
            need(dve, "T", "cmpkv")
            need(dve, "G", "vpad")
            S(nc.vector.tensor_copy(kcmp, PB[:, 0, 0:60]))
            for g in range(GROUPS):
                S(nc.vector.tensor_copy(vcmp[32 * g:32 * g + N_CMP, :], PB[32 * g:32 * g + N_CMP, 2, 0:64]), "vcmp")
            ffn("ffn10")
            boundary("10", "11", CH["nsa_in"], CH["nsa_in"])
            prep_to(CH["nsa_in"] + 8)
            need(dve, "S", "gexp")
            v = S(TS(gexp, gexp, 1.0, None, ALU.add))
            own(v)
            S(nc.vector.reciprocal(gates.rearrange("p i c -> p (i c)"), gexp), "gates")
            need(dve, "T", "scmp")
            for ic in range(2):
                for u in range(2):
                    dst = sc_[:, ic].rearrange("p (x u) n -> p x u n", u=2)[:, :, u, :]
                    bia = cbias[:, ic].rearrange("p (x u) n -> p x u n", u=2)[:, :, u, :]
                    src = flat["B"][:, u * 512 + ic * 120:u * 512 + ic * 120 + 120].rearrange("p (x n) -> p x n", n=N_CMP)
                    v = S(TT(dst, src, bia, ALU.add), "scmp")
            own(v)
            mx = [small[:, 16 + 16 * ic:32 + 16 * ic] for ic in range(2)]
            sm = [small[:, 48 + 16 * ic:64 + 16 * ic] for ic in range(2)]
            for ic in range(2):
                v = S(nc.vector.tensor_reduce(mx[ic], sc_[:, ic], AX.X, ALU.max))
            own(v)
            for ic in range(2):
                v = S(TS(mx[ic], mx[ic], NEG / 1e10, None, ALU.max))
            own(v)
            for ic in range(2):
                S(TT(sc_[:, ic], sc_[:, ic], mx[ic].unsqueeze(2).broadcast_to([P, 16, N_CMP]), ALU.subtract), f"csub{ic}")
            UNITS = [(ic, a, r) for ic in range(2) for a in range(2) for r in range(R)]
            sl_ = slopes()

            def soft(n_):
                ic, a, r = UNITS[n_]
                W = (ic + 1) * P
                need(dve, "T", f"sc{n_}")
                if n_ >= 2:
                    need(dve, "T", f"pt{n_ - 2}")
                for u in range(2):
                    h = (2 * a + u) * R + r
                    v = S(STT(ssb[n_ % 2][:, 2 * u:2 * u + 2, 0:W], dist[:, T - W:T].unsqueeze(1).broadcast_to([P, 2, W]),
                              sl_[h], PS["AB"[n_ % 2]][:, 2 * u:2 * u + 2, 0:W], ALU.mult, ALU.add), f"s{n_}")
                own(v)
                S(nc.vector.tensor_reduce(small[:, 4 * (n_ % 2):4 * (n_ % 2) + 4], ssb[n_ % 2][:, :, 0:W], AX.X, ALU.max,
                                          negate=True), f"m{n_}")

            soft(0)
            for ic in range(2):
                need(dve, "S", f"cexp{ic}")
                own(S(nc.vector.tensor_reduce(sm[ic], pc32[:, ic, :, 0:N_CMP], AX.X, ALU.add)))
                own(S(TS(sm[ic], sm[ic], 1e-30, None, ALU.max)))
                own(S(nc.vector.reciprocal(sm[ic], sm[ic])))
                own(S(TT(sm[ic], sm[ic], gates[:, ic, 0:16], ALU.mult)))
                S(TT(pc32[:, ic, :, 0:N_CMP], pc32[:, ic, :, 0:N_CMP], sm[ic].unsqueeze(2).broadcast_to([P, 16, N_CMP]),
                     ALU.mult), f"pc{ic}")

            def olow(n_):
                ic, a, r = UNITS[n_]
                need(dve, "S", f"ohi{n_}")
                S(TT(opl["B"][:, a * 4 + r, ic * P:ic * P + P], PY[:, 4 + 2 * (n_ % 2), 0:P],
                     oph["B"][:, a * 4 + r, ic * P:ic * P + P].bitcast(F32), ALU.subtract), f"olo{n_}")

            for n_, (ic, a, r) in enumerate(UNITS):
                rs = small[:, 80 + 4 * (n_ % 2):84 + 4 * (n_ % 2)]
                W = (ic + 1) * P
                if n_ + 1 < 16:
                    soft(n_ + 1)
                need(dve, "S", f"e{n_}")
                own(S(nc.vector.reciprocal(rs, small[:, 8 + 4 * (n_ % 2):12 + 4 * (n_ % 2)])))
                gt = gates[:, ic, 16:48].rearrange("p (b h) -> p h b", b=2)[:, r * 4 + 2 * a:r * 4 + 2 * a + 2, :]
                own(S(TT(t3(rs, 2), t3(rs, 2), gt, ALU.mult)))
                S(TT(ssb[n_ % 2][:, :, 0:W], ssb[n_ % 2][:, :, 0:W], rs.unsqueeze(2).broadcast_to([P, 4, W]), ALU.mult), f"p{n_}")
                if n_:
                    olow(n_ - 1)
            olow(15)
            boundary("11", "12", CH["ffn11"], CH["ffn11"])
            ffn("ffn11")
            boundary("12", "b00", CH["mix0"], CH["mix0"])
            for l in range(2):
                c = CH[f"mix{l}"]
                q_ = f"b{l}."
                if l == 0:
                    dve.wait_ge(b2_in, 32)
                    t0, t1, t2 = (rr[:, 256 * i:256 * i + 256] for i in range(3))
                    TWO_PI = 2 * np.pi
                    C1 = 6.28125
                    C2 = 0.0019350051879882812
                    C3 = TWO_PI - C1 - C2
                    MAGIC = 12582912.0
                    own(S(nc.vector.tensor_copy(t0, posi.bitcast(I32))))
                    own(S(TS(t0, t0, invf, None, ALU.mult)))
                    own(S(TS(t1, t0, 1.0 / TWO_PI, None, ALU.mult)))
                    own(S(TS(t1, t1, MAGIC, None, ALU.add)))
                    own(S(TS(t1, t1, -MAGIC, None, ALU.add)))
                    for cc in (C1, C2, C3):
                        own(S(STT(t0, t1, -cc, t0, ALU.mult, ALU.add)))
                    own(S(TS(sin_, t0, 3.1415925, -3.1415925, ALU.min, ALU.max)))
                    own(S(TS(t0, sin_, float(np.pi / 2), None, ALU.add)))
                    own(S(TS(t1, t0, float(np.pi), -TWO_PI, ALU.is_gt, ALU.mult)))
                    own(S(TT(t0, t0, t1, ALU.add)))
                    own(S(TS(cos_, t0, 3.1415925, -3.1415925, ALU.min, ALU.max), "ang"))
                prep_to(c + 7)
                X0 = t3(X[0], 8)
                need(dve, "S", "sincos")
                need(dve, "S", q_ + "k")
                for k in range(KT):
                    need(dve, "S", f"b{l}0.hi{k}")
                settle()
                own(S(TT(tmp8[:], X0, cos_.unsqueeze(1).broadcast_to([P, 8, T]), ALU.mult)))
                need(dve, "T", q_ + "rot")
                own(S(TT(X0, PY[:], sin_.unsqueeze(1).broadcast_to([P, 8, T]), ALU.mult), q_ + "rot"))
                own(S(TT(X0, X0, tmp8[:], ALU.add), q_ + "rotk"))
                prep_to(c + 14)
                need(dve, "T", q_ + "sc")
                settle()
                sdm = t3(tmp8[:].rearrange("p a b -> p (a b)")[:, 0:1536], 4)
                own(S(TT(sdm[:, :, 0:T], PY[:].rearrange("p (h e) t -> p h e t", h=4)[:, :, 0, :], decay, ALU.mult)))
                S(TT(sdm[:, :, T:T + P], PY[:].rearrange("p (h e) t -> p h e t", h=4)[:, :, 1, 0:P], decay[:, :, 0:P], ALU.mult),
                  q_ + "dec")
                prep_to(c + 18)
                need(dve, "S", q_ + "osd")
                settle()
                own(S(nc.vector.reciprocal(rr, rr)))
                t84 = tmp8[:].rearrange("p (h e) t -> p h e t", e=2)
                for e in range(2):
                    v = S(TT(t84[:, :, e, :], PY[:].rearrange("p (h e) t -> p h e t", e=2)[:, :, e, :], t3(rr, 4), ALU.mult), q_ + "rety")
                own(v)
                own(S(TT(tmp8[:], tmp8[:], t3(X[2], 8), ALU.mult), q_ + "rety2"))
                prep_to(c + 20)
                need(dve, "S", q_ + "rhi")
                S(TT(opl["B"][:], tmp8[:], oph["B"][:].bitcast(F32), ALU.subtract), q_ + "rlo")
                prep_to(c + 25)
                inverse(f"b{l}.v")
                prep_to(c + 28)
                need(dve, "S", q_ + "v.rstd")
                for k in range(KT):
                    S(STT(t3(X[5], 8)[:, k, :], t3(X[5], 8)[:, k, :], V("vnorm", 8 * l + k, 1), rstd[:], ALU.mult, ALU.mult),
                      q_ + f"vn{k}")
                G8 = t3(X[0], 8)

                def merge(b, h, buf, c_in):
                    prep_to(c_in + 4)
                    dve.wait_ge(multiplied, c_in + 2)
                    settle()
                    need(dve, "S", q_ + f"h{b}{h}")
                    g_ = G8[:, 4 * h:4 * h + 4, :]
                    if b == 0:
                        seen["V", q_ + f"m{b}.{h}"] = S(TT(macc(h), PS[buf][:], g_, ALU.mult), q_ + f"r{b}{h}")
                    else:
                        own(S(TT(g_, PS[buf][:], g_, ALU.mult), q_ + f"r{b}{h}"))
                        own(S(TT(macc(h), macc(h), g_, ALU.add), q_ + f"m{b}.{h}"))

                prep_to(c + 28)
                merge(0, 0, "A", c + 28)
                merge(0, 1, "B", c + 30)
                prep_to(c + 36)
                need(dve, "T", q_ + "mix")
                dve.wait_ge(lay_in, 48 * (l + 1))
                for g in range(4):
                    v = S(TT(tmp8[:, 2 * g:2 * g + 2, :].rearrange("p e (n t) -> p (e n) t", n=2),
                             PY[:, 2 * g:2 * g + 2, :].rearrange("p e (n t) -> p (e n) t", n=2),
                             bs[:, g, :].unsqueeze(1).broadcast_to([P, 4, P]), ALU.add), q_ + "mix")
                own(v)
                own(S(TT(tmp8[:], tmp8[:], t3(X[4], 8), ALU.mult), q_ + "sgu"))
                need(dve, "S", q_ + "shi")
                own(S(TT(opl["B"][:], tmp8[:], oph["B"][:].bitcast(F32), ALU.subtract), q_ + "slo"))
                prep_to(c + 38)
                p_, ping, pong = t3(X[1], 8), t3(X[4], 8), t3(X[5], 8)
                need(dve, "S", q_ + "p1")
                src = p_
                for lev in range(4):
                    dst = (ping, pong)[lev % 2]
                    sh = 1 << lev
                    t0 = 2 * lev
                    settle()
                    S(nc.vector.tensor_copy(dst[:, t0:8, 0:sh], src[:, t0:8, 0:sh]))
                    own(S(TT(dst[:, t0:8, sh:T], src[:, t0:8, sh:T], src[:, t0:8, 0:T - sh], ALU.add)))
                    res = t3(X[3], 8)[:, t0:t0 + 2, :]
                    S(STT(res[:, :, 16:T], dst[:, t0:t0 + 2, 16:T], 1.0 / POOL_WINDOWS[lev], p_[:, t0:t0 + 2, 16:T],
                          ALU.mult, ALU.subtract))
                    own(S(TT(res[:, :, 0:16], dst[:, t0:t0 + 2, 0:16], cnt[:, lev, :].unsqueeze(1).broadcast_to([P, 2, 16]), ALU.mult)))
                    S(TT(res[:, :, 0:16], res[:, :, 0:16], p_[:, t0:t0 + 2, 0:16], ALU.subtract), q_ + "pooled")
                    src = dst
                merge(1, 0, "A", c + 36)
                merge(1, 1, "B", c + 38)
                prep_to(c + 44)
                need(dve, "T", q_ + "pm")
                for k in range(KT):
                    S(TS(tmp8[:, k, :], PY[:, k, :], V("b_pool", 8 * l + k, 1), V("pool_scale", 8 * l + k, 1), ALU.add, ALU.mult),
                      q_ + f"pm{k}")
                own(S.n)
                need(dve, "S", q_ + "phi")
                own(S(TT(opl["B"][:], tmp8[:], oph["B"][:].bitcast(F32), ALU.subtract), q_ + "plo"))
                merge(2, 0, "A", c + 44)
                merge(2, 1, "B", c + 46)
                seen["V", q_ + "branch_done"] = S.n
                for h in range(2):
                    need(dve, "S", q_ + f"mhi{h}")
                    S(TT(opl["A"][:, 4 * h:4 * h + 4, :], macc(h), oph["A"][:, 4 * h:4 * h + 4, :].bitcast(F32), ALU.subtract),
                      q_ + f"mlo{h}")
                boundary(f"b{l}0", f"b{l}1", CH[f"ff{l}"], CH[f"ff{l}"])
                ff2(l)
                if l == 0:
                    boundary("b01", "b10", CH["mix1"], CH["mix1"])
                else:
                    boundary("b11", None, N_CHUNKS, N_CHUNKS, last=True)
                    inverse("fin.x")
                    rs = spread_of("fin.x")
                    for k in range(KT):
                        S(STT(tmp8[:, k, :], x[:, k, :], V("final", k, 1), rs, ALU.mult, ALU.mult), f"fin.t{k}")

        @block.gpsimd
        def _(pool):
            S = Steps(steps["G"], "G", seen)

            def zero(name):
                S(pool.memset(acc[:, 0:JOBS[name][2]], 0.0), f"{name}.zero")

            def add_x(sub):
                for k in POOL_ADDS:
                    need(pool, "V", f"{sub}.u{k}")
                    S(pool.tensor_tensor(x[:, k, :], x[:, k, :], tmp8[:, k, :], ALU.add), f"{sub}.x{k}")

            def ada(name, k):
                for slot, _, _, loads in JOBS[name][1]:
                    use = k + ADA0[name]
                    if not isinstance(use, int) or use > 0:
                        pool.wait_ge(ada_used[slot], use)
                    if not isinstance(use, int):
                        pool.sem_inc(ada_free, 1)
                    for w, c0, width, o in loads:
                        pool.dma_start(slab[slot][:, o:o + width], w[bass.ds(k * P, P), c0:c0 + width]).then_inc(ada_ready[slot], 16)

            def ada_all(name):
                with pool.Fori(0, KT) as i:
                    ada(name, i)

            zero("first")
            S(pool.memset(epsc[:], EPS), "consts")
            for k in range(KT):
                ada("first", k)
            need(pool, "T", "first.mods")
            zero("ffn00")
            S(pool.memset(cv_[:, :, 0:2], 0.0), "cpad")
            ada_all("ffn00")
            need(pool, "T", "ffn00.mods")
            zero("ffn01")
            add_x("00")
            add_x("01")
            ada_all("ffn01")
            need(pool, "T", "ffn01.mods")
            zero("ffn10")
            add_x("02")
            S(pool.memset(vcmp, 0.0), "vpad")
            ada_all("ffn10")
            need(pool, "T", "ffn10.mods")
            S(pool.memset(pc32[:, :, :, N_CMP:32], 0.0), "ppad")
            add_x("10")
            add_x("11")
            zero("ffn11")
            ada_all("ffn11")
            add_x("12")
            for l in range(2):
                pool.wait_ge(lay_in, 48 * (l + 1))
                v = wsr.rearrange("p (g s) -> p g s", g=4)
                S(pool.affine_select(out=v, in_=v, compare_op=ALU.is_ge, fill=0.0, base=0, pattern=[[0, 4], [-1, P]],
                                     channel_multiplier=1), f"b{l}.tril")
                if l == 0:
                    need(pool, "V", "b00.u7")
                    zero("ff0")
                    ada_all("ff0")

    return seen


def kernel(**inputs):
    import concourse.bacc as bacc
    from concourse.bass_utils import run_bass_kernel_spmd

    a = {k: np.asarray(v) for k, v in inputs.items()}

    def fm(v):
        return np.ascontiguousarray(v.reshape(-1, P).T)

    vec = np.concatenate([fm(a[n]) for n in ("norm_g", "ada_b", "kv_norm_g", "kv_ada_b", "b_ada_2", "norm1_2", "norm2_2",
                                             "a_conv", "vnorm_gmlp_2", "b_pool_2", "pool_scale_2", "final_norm_2", "c", "c_2")], 1)
    wb = a["b_w_in"][0]
    wq = wb[:, :D].reshape(D, 2, 2, R, DH).transpose(0, 1, 3, 2, 4).reshape(D, D)
    wg = wb[:, D:].reshape(D, 3, GROUPS, R).transpose(0, 1, 3, 2).reshape(D, 48)
    wo = a["b_w_out"][0].reshape(2, 2, R, DH, D).transpose(0, 2, 1, 3, 4).reshape(D, D)
    pos2 = a["cmp_pos"].reshape(2, 16, 2, DH).transpose(2, 3, 0, 1).reshape(P, 2, 16)
    dram = {
        "x_fm": a["x"][0].T.reshape(KT, P, T).transpose(1, 0, 2),
        "vec": vec,
        "ada_w": a["ada_w"], "kv_ada_w": a["kv_ada_w"], "w_ada_2": a["w_ada_2"],
        "ffn_w_in": a["ffn_w_in"], "ffn_w_out": a["ffn_w_out"],
        "a_w_in": a["a_w_in"][0], "a_w_out": a["a_w_out"][0],
        "kv_w": a["kv_w"], "cmp_pos2": pos2, "cmp_w1": a["cmp_w1"], "cmp_w2": a["cmp_w2"],
        "b_w_in_p": np.concatenate([wq, wg], 1), "b_w_out_p": wo,
        "positions": a["positions_2"],
        "w_in_2": a["w_in_2"], "ws": a["ws_gmlp_2"].transpose(0, 2, 1, 3).reshape(DEPTH, P, 4 * P),
        "bs": a["bs_gmlp_2"].reshape(DEPTH, 4 * P), "w_pool": a["w_pool_2"].reshape(DEPTH, D, 256),
        "w_branch": a["w_branch_2"], "w_out_2": a["w_out_2"], "w_ff1": a["w_ff1_2"], "w_ff2": a["w_ff2_2"],
        **tables(),
    }
    dram = {n: np.ascontiguousarray(v) for n, v in dram.items()}

    def program(at):
        nc = bacc.Bacc("TRN2", target_bir_lowering=False, num_devices=1)
        ins = {n: nc.dram_tensor(n, v.shape, mybir.dt.from_np(v.dtype), kind="ExternalInput").ap() for n, v in dram.items()}
        out = nc.dram_tensor("out_fm", (P, KT, T), F32, kind="ExternalOutput").ap()
        return nc, build(nc, ins, out, at)

    class Any(dict):
        def __missing__(self, key):
            return 1

    _, at = program(Any())
    nc, again = program(at)
    assert at == again
    r = run_bass_kernel_spmd(nc, [dram], core_ids=[0])
    y = r.results[0]["out_fm"]
    return np.ascontiguousarray(y.transpose(2, 1, 0).reshape(1, T, D))
```

```python
from contextlib import ExitStack

import numpy as np

import concourse.bass as bass
from concourse import mybir

F32 = mybir.dt.float32
F32R = mybir.dt.float32r
I32 = mybir.dt.int32
ALU = mybir.AluOpType
ACT = mybir.ActivationFunctionType
AX = mybir.AxisListType

P = 128
D = 1024
T = 256
KT = D // P
DEPTH = 2
D_FF = 2816
FFN_STEPS = D_FF // 256
D_FF_2 = 4 * D
FF2_STEPS = D_FF_2 // 256
HEADS, DH, GROUPS = 16, 64, 4
R = HEADS // GROUPS
N_CMP = (T - 32) // 16 + 1
NEG = -1e30
EPS = 1e-6
RING = 3
CHUNK = 2048
ADA_W = 1536
POOL_WINDOWS = (2, 4, 8, 16)
CONV_ORDER = (0, 1, 2, 4, 3, 5)
GAP_Y, GAP_X, GAP_B = 22, 16, 5
POOL_ADDS = (1, 3, 5)

_at = 0
CH = {}
for _name, _n in (("ffn00", 3 * FFN_STEPS), ("conv_in", 12), ("conv_out", 4), ("ffn01", 3 * FFN_STEPS),
                  ("kv", 6), ("cmp", 4), ("ffn10", 3 * FFN_STEPS), ("nsa_in", 5), ("nsa_out", 4),
                  ("ffn11", 3 * FFN_STEPS),
                  ("mix0", 48), ("mix0_out", 4), ("ff0", 2 * FF2_STEPS),
                  ("mix1", 48), ("mix1_out", 4), ("ff1", 2 * FF2_STEPS)):
    CH[_name] = _at
    _at += _n
N_CHUNKS = _at

HID0 = {}
_at = 0
for _name, _n in (("ffn00", FFN_STEPS), ("ffn01", FFN_STEPS), ("ffn10", FFN_STEPS), ("ffn11", FFN_STEPS),
                  ("ff0", FF2_STEPS), ("ff1", FF2_STEPS)):
    HID0[_name] = _at
    _at += _n

VEC = {}
_v = 0
for _name, _n in (("norm_g", 96), ("ada_b", 144), ("kv_norm_g", 8), ("kv_ada_b", 16), ("b_ada_2", 96),
                  ("norm1_2", 16), ("norm2_2", 16), ("a_conv", 24), ("vnorm", 16), ("b_pool", 16),
                  ("pool_scale", 16), ("final", 8), ("c", 8), ("c_2", 8)):
    VEC[_name] = _v
    _v += _n
N_VEC = _v


def slopes():
    return [2.0 ** (-8.0 * (h + 1) / HEADS) for h in range(HEADS)]


def tables():
    f = np.float32
    ident = np.eye(P, dtype=f)
    ones = np.full((P, P), 1.0 / D, f)
    base = np.concatenate([ident, ones, np.ones((P, 1), f)], 1)
    i = np.arange(P)[:, None]
    j = np.arange(T)[None, :]
    dist = (j - (P + i)).astype(f)
    dist[(j - (P + i)) > 0] = NEG
    sel = np.zeros((P, 2, P), f)
    for u in range(2):
        for m in range(P):
            sel[u * 64 + m % 64, u, m] = 1.0
    sl = slopes()
    cb = np.zeros((P, 2, R, GROUPS, N_CMP), f)
    for ic in range(2):
        d = (ic * P + np.arange(P)[:, None]) - (np.arange(N_CMP)[None, :] * 16 + 31)
        for r in range(R):
            for g in range(GROUPS):
                cb[:, ic, r, g] = np.where(d >= 0, -f(sl[g * R + r]) * d.astype(f), f(NEG))
    nsa = np.concatenate([dist, cb.reshape(P, -1), sel.reshape(P, -1)], 1)
    decay = np.zeros((P, 4, T), f)
    for h in range(4):
        lg = np.log1p(-(2.0 ** (-5.0 - h)))
        rel = j - i
        decay[:, h] = np.where(rel >= 0, np.exp(lg * np.maximum(rel, 0)), 0.0) * 128.0 ** -0.5
    rot = np.zeros((P, P), f)
    for d in range(64):
        rot[d + 64, d] = -1.0
        rot[d, d + 64] = 1.0
    half = 64
    inv = (np.float32(10000.0) ** (-np.arange(half, dtype=f) / f(half))).astype(f)
    invf = np.concatenate([inv, inv])[:, None]
    cnt = np.stack([1.0 / np.minimum(np.arange(1, 17), w) for w in POOL_WINDOWS]).astype(f)
    cnt = np.broadcast_to(cnt.reshape(1, 64), (P, 64))
    b2 = np.concatenate([decay.reshape(P, -1), rot, invf, cnt], 1)
    return {n: np.ascontiguousarray(a, dtype=f) for n, a in (("t_base", base), ("t_nsa", nsa), ("t_b2", b2))}


class Steps:

    def __init__(self, sem, key, seen):
        self.sem, self.key, self.seen, self.n = sem, key, seen, 0

    def __call__(self, ins, mark=None):
        ins.then_inc(self.sem, 1)
        self.n += 1
        if mark:
            self.seen[self.key, mark] = self.n
        return self.n


def build(nc, I, out, at):
    seen = {}
    ctx = ExitStack()
    with ctx:
        def sb(name, shape, dt=F32):
            return ctx.enter_context(nc.sbuf_tensor(name, shape, dt))

        def sem(name):
            return ctx.enter_context(nc.semaphore(name))

        raw = [sb(f"raw{i}", [P, CHUNK]) for i in range(RING)]
        whi = [sb(f"whi{i}", [P, CHUNK], F32R) for i in range(RING)]
        wlo = [sb(f"wlo{i}", [P, CHUNK], F32R) for i in range(RING)]
        adaw = sb("adaw", [P, 2, ADA_W])
        acc = sb("acc", [P, 4 * ADA_W])
        x = sb("x", [P, KT, T])
        oph = {"A": sb("opA_hi", [P, KT, T], F32R), "B": sb("opB_hi", [P, KT, T], F32R)}
        opl = {"A": sb("opA_lo", [P, KT, T], F32R), "B": sb("opB_lo", [P, KT, T], F32R)}
        tmp8 = sb("tmp8", [P, KT, T])
        gact = sb("gact", [P, 2, T])
        hidf = sb("hidf", [P, 2, T])
        base = sb("base", [P, 257])
        ident, onesD, one = base[:, 0:128], base[:, 128:256], base[:, 256:257]
        vec = sb("vecs", [P, N_VEC])
        csil = sb("csil", [P, 16])
        mod = sb("mod", [P, 256])
        scl = sb("scl", [P, 11 * 8])
        gat = sb("gat", [P, 10 * 8])
        epsc = sb("epsc", [P, 1])
        sd = sb("sd", [P, T])
        rstd = sb("rstd", [P, T])
        warm = sb("warm", [P, 1])
        osd = sb("osd", [P, 8])
        MIX = 10240
        mix = sb("mix", [P, MIX])
        PA = ctx.enter_context(nc.psum_tensor("PA", [P, 4, T], F32))
        PB = ctx.enter_context(nc.psum_tensor("PB", [P, 4, T], F32))
        PY = ctx.enter_context(nc.psum_tensor("PY", [P, 8, T], F32))
        PS = {"A": PA, "B": PB, "Y": PY}
        flat = {k: v[:].rearrange("p a b -> p (a b)") for k, v in PS.items()}

        def V(name, i=0, n=KT):
            return vec[:, VEC[name] + i:VEC[name] + i + n]

        raw_ready = [sem(f"raw_ready{i}") for i in range(RING)]
        hi_ready = sem("hi_ready")
        lo_ready = sem("lo_ready")
        multiplied = sem("multiplied")
        ada_ready = [sem(f"ada_ready{i}") for i in range(4)]
        first_ready = [sem(f"first_ready{i}") for i in range(4)]
        ada_used = [sem(f"ada_used{i}") for i in range(4)]
        act_made = sem("act_made")
        hid_made = sem("hid_made")
        hid_hi = sem("hid_hi")
        hid_lo = sem("hid_lo")
        ada_free = sem("ada_free")
        x_in = sem("x_in")
        vec_in = sem("vec_in")
        base_in = sem("base_in")
        nsa_in = sem("nsa_in")
        cmp_in = sem("cmp_in")
        b2_in = sem("b2_in")
        lay_in = sem("lay_in")
        out_done = sem("out_done")
        steps = {"T": sem("tensor_step"), "S": sem("scalar_step"), "V": sem("vector_step"), "G": sem("gpsimd_step")}

        def need(eng, key, mark):
            eng.wait_ge(steps[key], at[key, mark])

        def area(o, n):
            if o < MIX:
                assert o + n <= MIX, (o, n)
                return mix[:, o:o + n]
            assert o - MIX + n <= 4 * ADA_W
            return acc[:, o - MIX:o - MIX + n]

        def macc(h):
            return t3(X[2], 8)[:, 4 * h:4 * h + 4, :]

        def t3(ap, a):
            return ap.rearrange("p (a b) -> p a b", a=a)

        cb_, cc_ = t3(area(0, 2048), 8), t3(area(2048, 2048), 8)
        cv_ = t3(area(4096, 8 * 258), 8)
        cy_ = t3(area(6160, 2048), 8)
        o = 0
        kslc, kwin = t3(area(0, 512), 2), t3(area(512, 512), 2)
        vtok = {"slc": t3(area(1024, 512), 2), "win": t3(area(1536, 512), 2)}
        kcmp, vcmp = area(2048, 60), area(2112, 64)
        hidc = area(2176, 240).rearrange("p (k m c) -> p k m c", k=2, m=2)
        pos2 = area(2416, 32).rearrange("p (k l) -> p k l", k=2)
        cw2 = area(2448, 384)
        w2k, w2v = t3(cw2[:, 0:256], 2), t3(cw2[:, 256:384], 2)
        tnsa = area(2832, 256 + 480 + 256)
        dist, cbias = tnsa[:, 0:256], tnsa[:, 256:736].rearrange("p (i h n) -> p i h n", i=2, n=N_CMP)
        selu = t3(tnsa[:, 736:992], 2)
        kvc = t3(area(3840, 1024), 4)
        vtmp = {"slc": t3(area(4864, 512), 2), "win": t3(area(5376, 512), 2)}
        qf = t3(area(5888, 2048), 8)
        gates = area(7936, 96).rearrange("p (i c) -> p i c", i=2)
        gexp = area(8032, 96)
        ptc = area(8128, 1024).rearrange("p (i r c) -> p i r c", i=2, r=R)
        small = area(9152, 128)
        pc32 = area(MIX, 1024).rearrange("p (i h n) -> p i h n", i=2, n=32)
        sc_ = area(MIX + 1024, 480).rearrange("p (i h n) -> p i h n", i=2, n=N_CMP)
        ssb = [t3(area(MIX + 1536 + 1024 * i, 1024), 4) for i in range(3)]
        ptsb = t3(area(MIX + 4608, 1024), 8)
        tb2 = area(0, 1024 + 128 + 1 + 64)
        decay, rotm, invf = t3(tb2[:, 0:1024], 4), tb2[:, 1024:1152], tb2[:, 1152:1153]
        cnt = t3(tb2[:, 1153:1217], 4)
        cos_, sin_ = area(1220, 256), area(1476, 256)
        wT, bs = t3(area(1732, 512), 4), t3(area(2244, 512), 4)
        X = [area(2756 + 2048 * i, 2048) for i in range(3)] + [area(MIX + 2048 * i, 2048) for i in range(3)]
        slabs = adaw[:].rearrange("p a b -> p (a b)")
        wpool, wsr = slabs[:, 0:2048], slabs[:, 2048:2560]
        posi = area(8900, 256)
        rr = area(9156, 1024)
        hdiag = tmp8[:, 0:4, :]
        assert 2756 + 3 * 2048 <= 8900

        slab = [adaw[:, 0, :], adaw[:, 1, :], area(MIX - 2 * ADA_W, ADA_W), area(MIX - ADA_W, ADA_W)]

        def job(which, parts):
            total = sum(n for _, _, n in parts)
            width = total // 4
            slots, at_, left = [], 0, list(parts)
            for q in range(4):
                loads, o = [], 0
                while o < width:
                    w, c0, n = left.pop(0)
                    m = min(n, width - o)
                    loads.append((w, c0, m, o))
                    if m < n:
                        left.insert(0, (w, c0 + m, n - m))
                    o += m
                slots.append((q, width, q * width, loads))
            return which, slots, total

        a0, a1 = I["ada_w"][0], I["ada_w"][1]
        JOBS = {
            "first": job(0, [(a0, 0, 2048)]),
            "ffn00": job(0, [(a0, 2048, 6144)]),
            "ffn01": job(0, [(a0, 8192, 1024), (a1, 0, 2048), (I["kv_ada_w"], 0, 2048), (a1, 2048, 1024)]),
            "ffn10": job(0, [(a1, 3072, 6144)]),
            "ffn11": job(1, [(I["w_ada_2"][0], 0, 6144)]),
            "ff0": job(1, [(I["w_ada_2"][1], 0, 6144)]),
        }
        MODS = {
            "first": [(0, 16, 0, V("ada_b", 0, 16))],
            "ffn00": [(0, 24, 16, V("ada_b", 16, 24)), (24, 24, 40, V("ada_b", 40, 24))],
            "ffn01": [(0, 8, 64, V("ada_b", 64, 8)), (8, 16, 72, V("ada_b", 72, 16)), (24, 16, 144, V("kv_ada_b", 0, 16)),
                      (40, 8, 88, V("ada_b", 88, 8))],
            "ffn10": [(0, 24, 96, V("ada_b", 96, 24)), (24, 24, 120, V("ada_b", 120, 24))],
            "ffn11": [(0, 24, 160, V("b_ada_2", 0, 24)), (24, 24, 184, V("b_ada_2", 24, 24))],
            "ff0": [(0, 48, 208, V("b_ada_2", 48, 48))],
        }
        SUB = {}
        for l in range(2):
            for s in range(3):
                g = (l * 3 + s) * 16
                SUB[f"{l}{s}"] = dict(i=l * 3 + s, shift=72 * l + 24 * s, g_pre=V("norm_g", g), g_post=V("norm_g", g + 8),
                                      w=1.0 if s == 1 else 0.5)
        SUB["kv"] = dict(i=10, shift=144, g_pre=V("kv_norm_g"))
        for l in range(2):
            for s in range(2):
                SUB[f"b{l}{s}"] = dict(i=6 + 2 * l + s, shift=160 + 48 * l + 24 * s, w=1.0,
                                       g_pre=V(("norm1_2", "norm2_2")[s], 8 * l), g_post=None)
        SCALES = {"first": ["00"], "ffn00": ["01"], "ffn01": ["10", "kv"], "ffn10": ["11"], "ffn11": ["b00"], "ff0": ["b10", "b11"]}
        GATES = {"first": [], "ffn00": ["00"], "ffn01": ["02"], "ffn10": ["11"], "ffn11": ["b00"], "ff0": ["b10", "b11"]}
        LATER = {"ffn00": (24, ["02"], ["01"]), "ffn01": (40, [], ["10"]), "ffn10": (24, ["12"], ["12"]),
                 "ffn11": (24, ["b01"], ["b01"])}

        def A_(s):
            return scl[:, SUB[s]["i"] * 8:SUB[s]["i"] * 8 + 8]

        def B_(s):
            return mod[:, SUB[s]["shift"]:SUB[s]["shift"] + 8]

        def G_(s):
            return gat[:, SUB[s]["i"] * 8:SUB[s]["i"] * 8 + 8]

        ADA0, LOADS0, _n = {}, {}, 0
        _loads = [0] * 4
        for name, (_, slots, _) in JOBS.items():
            ADA0[name] = _n
            LOADS0[name] = list(_loads)
            _n += KT
            for q in range(4):
                _loads[q] += KT * len(slots[q][3]) if name != "first" else 0

        def wv(w):
            return w.rearrange("(k p) n -> p k n", p=P)

        def src_ffn_in(w, j, half):
            return [(wv(w)[:, 4 * half:4 * half + 4, bass.ds(two * D_FF + j, 256)], t * 1024, 4) for t, two in ((0, 0), (1, 1))]

        def src_in512(w, c0, half):
            return [(wv(w)[:, 4 * half + 2 * q:4 * half + 2 * q + 2, c0:c0 + 512], q * 1024, 2) for q in range(2)]

        def src_in256(w, c0, k0=0):
            return [(wv(w)[:, k0 + 4 * q:k0 + 4 * q + 4, bass.ds(c0, 256)], q * 1024, 4) for q in range(2)]

        def src_out(w, row):
            return [(w[bass.ds(row + P * q, P), :], q * 1024, 1) for q in range(2)]

        def src_gates(w):
            return [(wv(w)[:, 4 * q:4 * q + 4, D:D + 48], q * 192, 4) for q in range(2)]

        def tile_ffn_in(k, m):
            return (m // 2) * 1024 + k * 256 + (m % 2) * 128

        def tile_in512(k, m):
            return k * 512 + m * 128

        def tile_in256(k, m):
            return k * 256 + m * 128

        def tile_out(k, m):
            return k * 1024 + m * 128

        block = ctx.enter_context(nc.Block())

        @block.sync
        def _(sp):
            def chunk(c, src, slot=None):
                slot = c % RING if slot is None else slot
                if not isinstance(c, int) or c >= RING:
                    sp.wait_ge(lo_ready, c - (RING - 1))
                for ap, o_, k in src:
                    dst = raw[slot][:, o_:o_ + k * ap.shape[-1]]
                    sp.dma_start(dst if len(ap.shape) == 2 else t3(dst, k), ap).then_inc(raw_ready[slot], 16)

            def first_ada(rows):
                for k in rows:
                    for slot, _, _, loads in JOBS["first"][1]:
                        if k:
                            sp.wait_ge(ada_used[slot], k)
                        for w, c0, width, o in loads:
                            sp.dma_start(slab[slot][:, o:o + width], w[k * P:k * P + P, c0:c0 + width]).then_inc(first_ready[slot], 16)

            def ffn(name, w_in, w_out):
                c0 = CH[name]
                if c0 == 0:
                    first_ada(range(0, 6))
                chunk(c0, src_ffn_in(w_in, 0, 0))
                if c0 == 0:
                    first_ada(range(6, KT))
                chunk(c0 + 1, src_ffn_in(w_in, 0, 1))

                def body(j):
                    chunk(c0 + 3 * j - 1, src_ffn_in(w_in, j * 256, 0), (c0 + 2) % RING)
                    chunk(c0 + 3 * j, src_ffn_in(w_in, j * 256, 1), c0 % RING)
                    chunk(c0 + 3 * j + 1, src_out(w_out, (j - 1) * 256), (c0 + 1) % RING)

                with sp.Fori(0, 10) as i:
                    body(i + 1)
                chunk(c0 + 32, src_out(w_out, 10 * 256))

            def ff2(l, w_in, w_out):
                c0 = CH[f"ff{l}"]
                chunk(c0, src_in256(w_in, 0))

                def body(j, jj):
                    chunk(c0 + 2 * j - 1, src_in256(w_in, j * 256), (c0 + 2 * jj - 1) % RING)
                    chunk(c0 + 2 * j, src_out(w_out, (j - 1) * 256), (c0 + 2 * jj) % RING)

                with sp.Fori(0, 5) as i:
                    for jj in range(1, 4):
                        body(i * 3 + jj, jj)
                chunk(c0 + 31, src_out(w_out, 15 * 256))

            sp.dma_start(vec[:], I["vec"]).then_inc(vec_in, 16)
            sp.dma_start(base[:], I["t_base"]).then_inc(base_in, 16)
            sp.dma_start(x[:], I["x_fm"]).then_inc(x_in, 16)
            ffn("ffn00", I["ffn_w_in"][0, 0], I["ffn_w_out"][0, 0])
            for n_, g in enumerate(CONV_ORDER):
                for h in range(2):
                    chunk(CH["conv_in"] + 2 * n_ + h, src_in512(I["a_w_in"], 512 * g, h))
            for k in range(4):
                chunk(CH["conv_out"] + k, src_out(I["a_w_out"], 256 * k))
            ffn("ffn01", I["ffn_w_in"][0, 1], I["ffn_w_out"][0, 1])
            sp.wait_ge(multiplied, CH["conv_out"] + 4)
            sp.dma_start(tnsa, I["t_nsa"]).then_inc(nsa_in, 16)
            sp.dma_start(pos2, I["cmp_pos2"]).then_inc(cmp_in, 16)
            w2 = I["cmp_w2"].rearrange("k (m p) d -> k p m d", p=P)
            for u in range(2):
                sp.dma_start(w2k[:, :, 64 * u:64 * u + 64], w2[0]).then_inc(cmp_in, 16)
            sp.dma_start(w2v, w2[1]).then_inc(cmp_in, 16)
            for g in range(3):
                for h in range(2):
                    chunk(CH["kv"] + 2 * g + h, src_in512(I["kv_w"], 512 * g, h))
            for kv in range(2):
                for h in range(2):
                    chunk(CH["cmp"] + 2 * kv + h, src_in256(I["cmp_w1"][kv], 0, 8 * h))
            ffn("ffn10", I["ffn_w_in"][1, 0], I["ffn_w_out"][1, 0])
            for g in range(2):
                for h in range(2):
                    chunk(CH["nsa_in"] + 2 * g + h, src_in512(I["b_w_in_p"], 512 * g, h))
            chunk(CH["nsa_in"] + 4, src_gates(I["b_w_in_p"]))
            for k in range(4):
                chunk(CH["nsa_out"] + k, src_out(I["b_w_out_p"], 256 * k))
            ffn("ffn11", I["ffn_w_in"][1, 1], I["ffn_w_out"][1, 1])
            sp.wait_ge(multiplied, CH["nsa_out"] + 4)
            sp.dma_start(tb2, I["t_b2"]).then_inc(b2_in, 16)
            for l in range(2):
                c = CH[f"mix{l}"]
                for slot in range(2):
                    sp.wait_ge(ada_used[slot], ADA0["ff0"] + KT * l)
                if l == 0:
                    sp.wait_ge(ada_used[2], ADA0["ff0"])
                    sp.wait_ge(ada_used[3], ADA0["ff0"])
                    sp.dma_start(posi.bitcast(I32), I["positions"].partition_broadcast(P)).then_inc(b2_in, 16)
                if l == 1:
                    need(sp, "V", "b0.branch_done")
                sp.dma_start(wsr, I["ws"][l]).then_inc(lay_in, 16)
                sp.dma_start(bs, I["bs"][l:l + 1].partition_broadcast(P)).then_inc(lay_in, 16)
                sp.dma_start(wpool.rearrange("p (g k n) -> p g k n", g=4, k=2).rearrange("p g k n -> p (g k) n"),
                             I["w_pool"][l].rearrange("(g p) n -> p g n", p=P)).then_inc(lay_in, 16)
                for g in range(12):
                    for h in range(2):
                        chunk(c + 2 * g + h, src_in512(I["w_in_2"][l], 512 * g, h))
                c += 24
                for b in range(3):
                    for g in range(2):
                        for h in range(2):
                            chunk(c, src_in512(I["w_in_2"][l], 512 * (12 + 2 * b + g), h))
                            c += 1
                    for g in range(2):
                        for h in range(2):
                            chunk(c, src_in512(I["w_branch"][l, b], 512 * g, h))
                            c += 1
                for k in range(4):
                    chunk(c + k, src_out(I["w_out_2"][l], 256 * k))
                ff2(l, I["w_ff1"][l], I["w_ff2"][l])
            need(sp, "V", "fin.t7")
            sp.dma_start(out, tmp8[:]).then_inc(out_done, 16)
            sp.wait_ge(out_done, 16)

        @block.tensor
        def _(pe):
            S = Steps(steps["T"], "T", seen)
            freed = {}

            def take(buf):
                if buf in freed:
                    s, v = freed.pop(buf)
                    pe.wait_ge(s, v)

            def by(buf, key, mark):
                freed[buf] = (steps[key], at[key, mark])

            def mm3(o_, c_slot, woff, X2, rhs, start, stop):
                xh, xl = X2
                w1, w2_ = whi[c_slot][:, woff:woff + P], wlo[c_slot][:, woff:woff + P]
                nc.tensor.matmul(o_, w1, rhs(xh), start=start, stop=False, skip_group_check=True)
                nc.tensor.matmul(o_, w1, rhs(xl), start=False, stop=False, skip_group_check=True)
                return nc.tensor.matmul(o_, w2_, rhs(xh), start=False, stop=stop, skip_group_check=True)

            def chunk(c, slot, ps, tile, kts, ms, op, k_first, k_last, before=None, tag=None):
                pe.wait_ge(lo_ready, c + 1)
                for kk, k in enumerate(kts):
                    if before:
                        before(k)
                    for m in range(ms):
                        last = mm3(ps[:, m, :], slot, tile(kk, m), (oph[op], opl[op]),
                                   lambda t_, k=k: t_[:, k, :], k == k_first and m % 2 == 0, k == k_last)
                        if tag and k == k_last and m in (1, 3, 5):
                            S(last, f"{tag}.bank{m // 2}")
                last.then_inc(multiplied, 1)

            def group512(c, buf, op, before=None):
                for h in range(2):
                    chunk(c + h, (c + h) % RING, PS[buf], tile_in512, range(4 * h, 4 * h + 4), 4, op, 0, 7, before)

            def out1024(c, op, tag, before=None):
                take("Y")
                for q in range(4):
                    chunk(c + q, (c + q) % RING, PY, tile_out, (2 * q, 2 * q + 1), 8, op, 0, 7, before, tag=tag if q == 3 else None)

            def ssq_pairs(tag):
                take("B")
                for q in range(4):
                    need(pe, "V", f"{tag}.pair{q}")
                    last = nc.tensor.matmul(PB[:, 0, :], onesD, tmp8[:, 2 * q, :], start=q == 0, stop=q == 3)
                S(last, f"{tag}.ssq")
                by("B", "S", f"{tag}.sd")

            def ssq(tag, gap=0):
                take("B")
                for k in range(KT):
                    if k % 2 == 0:
                        if k:
                            idle(gap)
                        need(pe, "S", f"{tag}.sq{k // 2}")
                    last = nc.tensor.matmul(PB[:, 0, :], onesD, tmp8[:, k, :], start=k == 0, stop=k == KT - 1)
                S(last, f"{tag}.ssq")
                by("B", "S", f"{tag}.sd")

            def finish_mods(name):
                n = LATER[name][0] if name in LATER else JOBS[name][2] // P
                for slot in range(4):
                    pe.wait_ge(ada_used[slot], ADA0[name] + KT)
                take("B")
                for t in range(n):
                    last = nc.tensor.matmul(flat["B"][:, t:t + 1], acc[:, t * P:t * P + P], one, start=True, stop=True)
                S(last, f"{name}.mods")
                by("B", "V", f"{name}.mod")

            def idle(n):
                for _ in range(n):
                    nc.tensor.matmul(flat["A"][:, 0:P], ident, onesD, start=True, stop=True)

            def later(name, half):
                n0, n1 = LATER[name][0], JOBS[name][2] // P
                mid = (n0 + n1) // 2
                for t in range(n0, mid) if half == 0 else range(mid, n1):
                    last = nc.tensor.matmul(flat["B"][:, 512 + t:513 + t], acc[:, t * P:t * P + P], one, start=True, stop=True)
                if half:
                    S(last, f"{name}.mods2")
                    by("B", "V", f"{name}.mod2")
                return (mid - n0 if half == 0 else n1 - mid)

            def lo_of(tag):
                return lambda k: need(pe, "V", f"{tag}.lo{k}")

            def ffn(name, i_ffn, tag):
                c0 = CH[name]
                h0 = HID0[name]

                def inp(j, jj, first=None, ps=PA):
                    ca = c0 + 3 * j - 1 if first is None else c0
                    s = (c0 + 3 * jj - 1) % RING if first is None else c0 % RING
                    for h in range(2):
                        chunk(ca + h, (s + h) % RING, ps, tile_ffn_in, range(4 * h, 4 * h + 4), 4, "A", 0, 7, first)

                def outp(j, jj, k_first, k_last, c=None, out_tag=None):
                    pe.wait_ge(hid_lo, h0 + j + 1)
                    cc = c0 + 3 * j + 4 if c is None else c
                    s = (c0 + 3 * jj + 4) % RING if c is None else c % RING
                    pe.wait_ge(lo_ready, cc + 1)
                    for k in range(2):
                        for m in range(KT):
                            last = mm3(PY[:, m, :], s, tile_out(k, m), (oph["B"], opl["B"]), lambda t_, k=k: t_[:, k, :],
                                       k_first and k == 0 and m % 2 == 0, k_last and k == 1)
                            if out_tag and k == 1 and m in (1, 3, 5):
                                S(last, f"{out_tag}.bank{m // 2}")
                    last.then_inc(multiplied, 1)

                take("B")
                inp(0, 0, lo_of(tag), PB)
                freed["B"] = (hid_made, h0 + 1)
                take("A")
                take("Y")
                inp(1, 1)
                outp(0, 0, True, False)
                with pe.Fori(0, 8) as i:
                    pe.wait_ge(hid_made, h0 + 2 + i)
                    inp(i + 2, 2)
                    outp(i + 1, 1, False, False)
                pe.wait_ge(hid_made, h0 + 10)
                inp(10, 10)
                outp(9, 9, False, False)
                finish_mods(name)
                outp(10, 10, False, True, c0 + 32, tag)
                freed["A"] = (hid_made, h0 + 11)

            def ff2(l, tag):
                c0 = CH[f"ff{l}"]
                h0 = HID0[f"ff{l}"]

                def inp(j, jj, first=None, ps=PA):
                    c = c0 + 2 * j - 1 if first is None else c0
                    s = (c0 + 2 * jj - 1) % RING if first is None else c0 % RING
                    chunk(c, s, ps, tile_in256, range(8), 2, "A", 0, 7, first)

                def outp(j, jj, k_first, k_last, c=None, out_tag=None):
                    pe.wait_ge(hid_lo, h0 + j + 1)
                    cc = c0 + 2 * j + 2 if c is None else c
                    s = (c0 + 2 * jj + 2) % RING if c is None else c % RING
                    pe.wait_ge(lo_ready, cc + 1)
                    for k in range(2):
                        for m in range(KT):
                            last = mm3(PY[:, m, :], s, tile_out(k, m), (oph["B"], opl["B"]), lambda t_, k=k: t_[:, k, :],
                                       k_first and k == 0 and m % 2 == 0, k_last and k == 1)
                            if out_tag and k == 1 and m in (1, 3, 5):
                                S(last, f"{out_tag}.bank{m // 2}")
                    last.then_inc(multiplied, 1)

                take("B")
                inp(0, 0, lo_of(tag), PB)
                freed["B"] = (act_made, HID0[f"ff{l}"] + 1)
                take("A")
                take("Y")
                for j in range(1, 4):
                    if j > 1:
                        pe.wait_ge(act_made, HID0[f"ff{l}"] + j)
                    inp(j, j)
                    outp(j - 1, j - 1, j == 1, False)
                with pe.Fori(0, 4) as i:
                    for jj in range(4, 7):
                        pe.wait_ge(act_made, HID0[f"ff{l}"] + i * 3 + jj)
                        inp(i * 3 + jj, jj)
                        outp(i * 3 + jj - 1, jj - 1, False, False)
                if l == 0:
                    finish_mods("ff0")
                outp(15, 15, False, True, c0 + 31, tag)
                freed["A"] = (act_made, HID0[f"ff{l}"] + 16)

            def boundary(sub, nsub, job_=None):
                take("A")
                if not sub.startswith("b"):
                    ssq_pairs(f"{sub}.y")
                    idle(GAP_Y - (later(job_, 0) if job_ else 0))
                    ssq(f"{nsub}.x", 1)
                else:
                    idle(GAP_B)
                    ssq(f"{nsub}.x")
                if nsub != "fin":
                    idle(GAP_X - (later(job_, 1) if job_ else 0))

            pe.wait_ge(base_in, 16)
            ssq("00.x")
            for k in range(6, KT):
                pe.wait_ge(ada_used[3], k)
                idle(10)
            finish_mods("first")
            idle(14)
            ffn("ffn00", 0, "00")
            by("Y", "V", "00.u7")
            boundary("00", "01", "ffn00")
            for g in range(6):
                buf = "AB"[g % 2]
                take(buf)
                group512(CH["conv_in"] + 2 * g, buf, "A", lo_of("01") if g == 0 else None)
                by(buf, *(("V", f"conv{g}") if g in (3, 5) else ("S", f"conv{g}")))
            out1024(CH["conv_out"], "B", "01", lambda k: need(pe, "V", f"conv.lo{k // 4}"))
            by("Y", "V", "01.u7")
            boundary("01", "02")
            ffn("ffn01", 1, "02")
            by("Y", "V", "02.u7")
            boundary("02", "10", "ffn01")
            for g in range(3):
                buf = "ABA"[g]
                take(buf)
                group512(CH["kv"] + 2 * g, buf, "B", lo_of("kv") if g == 0 else None)
                by(buf, "S", f"kv{g}")
            pe.wait_ge(nsa_in, 16)
            for kv in range(2):
                buf = "BA"[kv]
                take(buf)
                need(pe, "S", "kv0")
                for g in range(GROUPS):
                    last = nc.tensor.matmul(PS[buf][:, g, :], selu[:, g % 2, :], kvc[:, 2 * kv + g // 2, :],
                                            start=True, stop=True)
                S(last, f"dup{kv}")
                by(buf, "V", f"blk{kv}")
            take("Y")
            for n_, br in enumerate(("slc", "win")):
                need(pe, "S", f"kv{n_ + 1}")
                for a in range(2):
                    for jc in range(2):
                        last = nc.tensor.transpose(flat["Y"][:, (n_ * 4 + jc * 2 + a) * P:(n_ * 4 + jc * 2 + a + 1) * P],
                                                   vtmp[br][:, a, jc * P:jc * P + P], ident)
            S(last, "vtrans")
            by("Y", "S", "vtok")
            take("A")
            bh, bl = (oph["B"][:].rearrange("p a b -> p (a b)"), opl["B"][:].rearrange("p a b -> p (a b)"))
            for kv in range(2):
                need(pe, "V", f"blo{kv}")
                for h in range(2):
                    c = CH["cmp"] + 2 * kv + h
                    pe.wait_ge(lo_ready, c + 1)
                    for k in range(8):
                        for m in range(2):
                            last = mm3(PA[:, 2 * kv + m, 0:60], c % RING, tile_in256(k, m), (bh, bl),
                                       lambda t_, kk=8 * h + k, kv=kv: t_[:, (kv * 16 + kk) * 60:(kv * 16 + kk) * 60 + 60],
                                       h == 0 and k == 0 and m == 0, h == 1 and k == 7)
                    last.then_inc(multiplied, 1)
            by("A", "S", "gelu")
            need(pe, "S", "gelu")
            pe.wait_ge(cmp_in, 64)
            take("B")
            for m in range(2):
                last = nc.tensor.matmul(PB[:, 0, 0:60], w2k[:, m, :], hidc[:, 0, m, :], start=m == 0, stop=m == 1)
            for g in range(GROUPS):
                for m in range(2):
                    last = nc.tensor.matmul(PB[32 * g:32 * g + N_CMP, 2, 0:64], hidc[:, 1, m, g * N_CMP:(g + 1) * N_CMP],
                                            w2v[:, m, :], start=m == 0, stop=m == 1, tile_position=(0, 32 * g))
            S(last, "cmpkv")
            by("B", "V", "vcmp")
            ffn("ffn10", 2, "10")
            by("Y", "V", "10.u7")
            boundary("10", "11", "ffn10")
            for g in range(2):
                buf = "AB"[g]
                take(buf)
                group512(CH["nsa_in"] + 2 * g, buf, "A", lo_of("11") if g == 0 else None)
                by(buf, "S", f"q{g}")
            take("A")
            c = CH["nsa_in"] + 4
            pe.wait_ge(lo_ready, c + 1)
            for ic in range(2):
                for k in range(KT):
                    o_ = flat["A"][:, ic * 48:ic * 48 + 48]
                    ts = slice(ic * P, ic * P + P)
                    wh_, wl_ = whi[c % RING][:, k * 48:k * 48 + 48], wlo[c % RING][:, k * 48:k * 48 + 48]
                    nc.tensor.matmul(o_, oph["A"][:, k, ts], wh_, start=k == 0, stop=False)
                    nc.tensor.matmul(o_, oph["A"][:, k, ts], wl_, start=False, stop=False)
                    last = nc.tensor.matmul(o_, opl["A"][:, k, ts], wh_, start=False, stop=k == KT - 1)
            last.then_inc(multiplied, 1)
            by("A", "S", "gexp")
            take("B")
            for u in range(2):
                for ic in range(2):
                    for r in range(R):
                        for a in range(2):
                            g = 2 * a + u
                            o_ = ic * 120 + (r * 2 + a) * N_CMP
                            last = nc.tensor.matmul(flat["B"][:, u * 512 + o_:u * 512 + o_ + N_CMP],
                                                    qf[u * 64:u * 64 + 64, a * 4 + r, ic * P:ic * P + P],
                                                    kcmp[u * 64:u * 64 + 64, g * N_CMP:(g + 1) * N_CMP], start=True, stop=True)
            S(last, "scmp")
            by("B", "V", "scmp")

            UNITS = [(ic, a, r) for ic in range(2) for a in range(2) for r in range(R)]

            def scores(n_):
                ic, a, r = UNITS[n_]
                buf = "AB"[n_ % 2]
                take(buf)
                for u in range(2):
                    for b_, kk in enumerate((kslc, kwin)):
                        last = nc.tensor.matmul(PS[buf][:, 2 * u + b_, 0:(ic + 1) * P],
                                                qf[u * 64:u * 64 + 64, a * 4 + r, ic * P:ic * P + P],
                                                kk[u * 64:u * 64 + 64, a, 0:(ic + 1) * P], start=True, stop=True)
                S(last, f"sc{n_}")
                by(buf, "V", f"s{n_}")

            scores(0)
            scores(1)
            take("Y")
            for ic in range(2):
                need(pe, "G", "ppad")
                need(pe, "V", f"pc{ic}")
                for r in range(R):
                    last = nc.tensor.transpose(flat["Y"][:, (ic * 4 + r) * P:(ic * 4 + r + 1) * P],
                                               pc32[:, ic, 4 * r:4 * r + 4, :].rearrange("p h n -> p (h n)"), ident)
            S(last, "pct")
            by("Y", "S", "ptc")
            for n_, (ic, a, r) in enumerate(UNITS):
                if n_ + 2 < len(UNITS):
                    scores(n_ + 2)
                need(pe, "V", f"p{n_}")
                take("Y")
                for jc in range(ic + 1):
                    for x_ in range(4):
                        last = nc.tensor.transpose(flat["Y"][:, (jc * 4 + x_) * P:(jc * 4 + x_ + 1) * P],
                                                   ssb[n_ % 3][:, x_, jc * P:jc * P + P], ident)
                S(last, f"pt{n_}")
                by("Y", "S", f"pt{n_}")
                need(pe, "S", f"pt{n_}")
                if n_ >= 2:
                    need(pe, "V", f"olo{n_ - 2}")
                oo = PY[:, 4 + 2 * (n_ % 2), 0:P]
                for u in range(2):
                    g = 2 * a + u
                    nc.tensor.matmul(oo[u * 64:u * 64 + 64], vcmp[32 * g:32 * g + 32, :],
                                     ptc[32 * g:32 * g + 32, ic, r, :], start=True, stop=False, tile_position=(32 * g, 64 * u))
                for u in range(2):
                    g = 2 * a + u
                    for b_, br in enumerate(("slc", "win")):
                        for jc in range(ic + 1):
                            last = nc.tensor.matmul(oo[u * 64:u * 64 + 64], vtok[br][:, jc, g * 64:g * 64 + 64],
                                                    ptsb[:, jc * 4 + 2 * u + b_, :], start=False,
                                                    stop=b_ == 1 and jc == ic, tile_position=(0, 64 * u))
                S(last, f"o{n_}")
            need(pe, "V", "olo15")
            out1024(CH["nsa_out"], "B", "11")
            by("Y", "V", "11.u7")
            boundary("11", "12")
            ffn("ffn11", 3, "12")
            by("Y", "V", "12.u7")
            boundary("12", "b00", "ffn11")
            for l in range(2):
                c = CH[f"mix{l}"]

                def group(name, buf, key="S", before=None, op="A"):
                    nonlocal c
                    take(buf)
                    group512(c, buf, op, before)
                    c += 2
                    by(buf, key, f"b{l}.{name}")

                group("q", "A", before=lo_of(f"b{l}0"))
                group("k", "B")
                group("v0", "A")
                pe.wait_ge(b2_in, 32)
                take("Y")
                need(pe, "S", f"b{l}.k")
                for t in range(8):
                    last = nc.tensor.matmul(PY[:, t, :], rotm, t3(X[0], 8)[:, t, :], start=True, stop=True)
                S(last, f"b{l}.rot")
                by("Y", "V", f"b{l}.rot")
                group("v1", "B")
                group("g0", "A")
                take("Y")
                need(pe, "S", f"b{l}.v1")
                for jc in range(2):
                    for t in range(8):
                        last = nc.tensor.transpose(flat["Y"][:, (jc * 8 + t) * P:(jc * 8 + t + 1) * P],
                                                   t3(X[1], 8)[:, t, jc * P:jc * P + P], ident)
                S(last, f"b{l}.vt")
                by("Y", "S", f"b{l}.vtok")
                group("g1", "B")
                group("u0", "A")
                take("Y")
                need(pe, "V", f"b{l}.rotk")
                X0 = t3(X[0], 8)
                for h in range(4):
                    nc.tensor.matmul(PY[:, 2 * h, :], X0[:, 4 + h, 0:P], X0[:, h, :], start=True, stop=True)
                    last = nc.tensor.matmul(PY[:, 2 * h + 1, 0:P], X0[:, 4 + h, P:2 * P], X0[:, h, P:2 * P],
                                            start=True, stop=True)
                S(last, f"b{l}.sc")
                by("Y", "V", f"b{l}.dec")
                group("u1", "B")
                take("Y")
                sd_ = t3(tmp8[:].rearrange("p a b -> p (a b)")[:, 0:1536], 4)
                vt = X[3].rearrange("p (j e) -> p j e", j=2)
                for h in range(4):
                    for e in range(2):
                        t = 2 * h + e
                        nc.tensor.matmul(PY[:, t, :], vt[:, 0, t * P:t * P + P], sd_[:, h, 0:T], start=e == 0, stop=False,
                                         skip_group_check=True)
                        last = nc.tensor.matmul(PY[:, t, P:T], vt[:, 1, t * P:t * P + P], sd_[:, h, T:T + P], start=False,
                                                stop=True, skip_group_check=True)
                S(last, f"b{l}.o")
                by("Y", "V", f"b{l}.rety")
                group("s0", "A")
                take("B")
                for h in range(4):
                    need(pe, "S", f"b{l}.osq{h}")
                    for e in range(2):
                        for j in range(2):
                            last = nc.tensor.matmul(flat["B"][:, 2 * h + j:2 * h + j + 1], tmp8[:, 2 * h + e, j * P:j * P + P],
                                                    onesD[:, 0:1], start=h == 0 and e == 0 and j == 0, stop=e == 1,
                                                    skip_group_check=True)
                S(last, f"b{l}.ossq")
                by("B", "S", f"b{l}.osd")
                group("s1", "A")
                take("B")
                need(pe, "V", f"b{l}.odiag")
                for h in range(4):
                    last = nc.tensor.matmul(PB[:, h, :], onesD, hdiag[:, h, :], start=h % 2 == 0, stop=True, skip_group_check=True)
                S(last, f"b{l}.ospread")
                by("B", "S", f"b{l}.rr")
                group("p0", "B")
                group("p1", "A")
                ssq(f"b{l}.v")
                group("h00", "A")
                group("h01", "B")
                take("A")
                need(pe, "G", f"b{l}.tril")
                for g in range(4):
                    last = nc.tensor.transpose(flat["A"][:, g * P:g * P + P], wsr[:, g * P:g * P + P], ident)
                S(last, f"b{l}.wt")
                by("A", "S", f"b{l}.wT")
                group("r00", "A", "V", lambda k, l=l: need(pe, "V", f"b{l}.rlo") if k == 0 else None, "B")
                group("r01", "B", "V", None, "B")
                take("Y")
                need(pe, "V", f"b{l}.vn7")
                for jc in range(2):
                    for t in range(8):
                        last = nc.tensor.transpose(flat["Y"][:, (jc * 8 + t) * P:(jc * 8 + t + 1) * P],
                                                   t3(X[5], 8)[:, t, jc * P:jc * P + P], ident)
                S(last, f"b{l}.vnt")
                by("Y", "S", f"b{l}.vntok")
                group("h10", "A")
                take("Y")
                for t in range(8):
                    for n_ in range(2):
                        last = nc.tensor.matmul(PY[:, t, n_ * P:n_ * P + P], vt[:, n_, t * P:t * P + P], wT[:, t // 2, :],
                                                start=t % 2 == 0 and n_ == 0, stop=True, skip_group_check=True)
                S(last, f"b{l}.mix")
                by("Y", "V", f"b{l}.mix")
                group("h11", "B")
                group("r10", "A", "V", lambda k, l=l: need(pe, "V", f"b{l}.slo") if k == 0 else None, "B")
                group("r11", "B", "V", None, "B")
                group("h20", "A")
                take("Y")
                need(pe, "V", f"b{l}.pooled")
                pe.wait_ge(lay_in, 48 * (l + 1))
                wp = wpool.rearrange("p (g k n) -> p g k n", g=4, k=2)
                for g in range(4):
                    for m in range(2):
                        for k in range(2):
                            last = nc.tensor.matmul(PY[:, 2 * g + m, :], wp[:, g, k, m * P:m * P + P],
                                                    t3(X[3], 8)[:, 2 * g + k, :], start=m == 0 and k == 0, stop=k == 1,
                                                    skip_group_check=True)
                S(last, f"b{l}.pm")
                by("Y", "V", f"b{l}.pm7")
                group("h21", "B")
                group("r20", "A", "V", lambda k, l=l: need(pe, "V", f"b{l}.plo") if k == 0 else None, "B")
                group("r21", "B", "V", None, "B")
                out1024(c, "A", f"b{l}0", lambda k, l=l: need(pe, "V", f"b{l}.mlo{k // 4}"))
                by("Y", "V", f"b{l}0.u7")
                boundary(f"b{l}0", f"b{l}1")
                ff2(l, f"b{l}1")
                by("Y", "V", f"b{l}1.u7")
                boundary("b01" if l == 0 else "b11", "b10" if l == 0 else "fin")

        @block.scalar
        def _(act):
            S = Steps(steps["S"], "S", seen)
            nxt = [0]
            AC = nc.scalar.activation

            def prep(c, slot, w=CHUNK):
                act.wait_ge(raw_ready[slot], 32 * (c // RING + 1))
                if c >= RING:
                    act.wait_ge(multiplied, c - (RING - 1))
                AC(whi[slot][:, 0:w], raw[slot][:, 0:w], ACT.Copy).then_inc(hi_ready, 1)

            def prep_to(c, w=CHUNK):
                while nxt[0] < min(c, N_CHUNKS):
                    prep(nxt[0], nxt[0] % RING, 384 if nxt[0] == CH["nsa_in"] + 4 else w)
                    nxt[0] += 1

            def dyn(c0, per, i, k):
                c = c0 + k
                slot = c % RING
                act.wait_ge(raw_ready[slot], 32 * (c // RING + 1) + i * (32 * (per // RING)))
                act.wait_ge(multiplied, i * per + c - (RING - 1))
                AC(whi[slot][:], raw[slot][:], ACT.Copy).then_inc(hi_ready, 1)

            def squares(tag, src, wait, own=None):
                if own:
                    need(act, "S", own)
                for q in range(4):
                    wait(q)
                    S(AC(tmp8[:, 2 * q:2 * q + 2, :], src[:, 2 * q:2 * q + 2, :], ACT.Square), f"{tag}.sq{q}")

            def root(tag):
                need(act, "T", f"{tag}.ssq")
                S(AC(sd[:], PB[:, 0, :], ACT.Sqrt, bias=epsc[:]), f"{tag}.sd")

            def load_table(func):
                act.wait_ge(steps["S"], S.n)
                S(AC(warm[:], epsc[:], func))

            def pre(sub, op, tag=None):
                tag = tag or sub
                for k in range(KT):
                    need(act, "V", f"{tag}.t{k}")
                    S(AC(oph[op][:, k, :], tmp8[:, k, :], ACT.Identity, bias=B_(sub)[:, k:k + 1]), f"{tag}.hi{k}")

            def boundary(sub, nsub, c_done, c_next, ops=None):
                prep_to(c_next + 2)
                load_table(ACT.Sqrt)

                def y_there(q):
                    if q < 3:
                        need(act, "T", f"{sub}.bank{q}")
                    else:
                        act.wait_ge(multiplied, c_done)

                def x_there(q):
                    if sub.startswith("b"):
                        need(act, "V", f"{sub}.u{2 * q + 1}")
                        return
                    for k in (2 * q, 2 * q + 1):
                        need(act, "G" if k in POOL_ADDS else "V", f"{sub}.x{k}")

                if not sub.startswith("b"):
                    squares(f"{sub}.y", PY, y_there)
                    root(f"{sub}.y")
                    prep_to(c_next + 3)
                squares(f"{nsub}.x", x, x_there)
                root(f"{nsub}.x")
                prep_to(c_next + 3)
                for s_, op in ops or [(nsub, "A")]:
                    pre(s_, op)

            def ffn(name):
                c0 = CH[name]
                h0 = HID0[name]
                prep_to(c0 + 3)

                def made(j, c_in, ps=PA):
                    act.wait_ge(multiplied, c_in + 1)
                    AC(gact[:], ps[:, 0:2, :], ACT.Silu).then_inc(act_made, 1)

                def high(j, c_prev):
                    act.wait_ge(hid_made, h0 + j + 1)
                    act.wait_ge(multiplied, c_prev + 1)
                    AC(oph["B"][:, 0:2, :], hidf[:], ACT.Copy).then_inc(hid_hi, 1)

                made(0, c0 + 1, PB)
                prep_to(c0 + 4)
                act.wait_ge(hid_made, h0 + 1)
                AC(oph["B"][:, 0:2, :], hidf[:], ACT.Copy).then_inc(hid_hi, 1)
                prep_to(c0 + 6)
                with act.Fori(0, 8) as i:
                    made(i + 1, i * 3 + (c0 + 3))
                    dyn(c0, 3, i, 6)
                    high(i + 1, i * 3 + (c0 + 4))
                    dyn(c0, 3, i, 7)
                    dyn(c0, 3, i, 8)
                nxt[0] = c0 + 30
                made(9, c0 + 27)
                prep_to(c0 + 31)
                high(9, c0 + 28)
                prep_to(c0 + 33)
                made(10, c0 + 30)
                high(10, c0 + 31)
                prep_to(c0 + 34)

            def ff2(l):
                c0 = CH[f"ff{l}"]
                h0 = HID0[f"ff{l}"]
                prep_to(c0 + 2)

                def made(j, c_in, ps=PA):
                    act.wait_ge(multiplied, c_in + 1)
                    act.wait_ge(hid_made, h0 + j)
                    act.wait_ge(hid_hi, h0 + j)
                    AC(gact[:], ps[:, 0:2, :], ACT.Relu).then_inc(act_made, 1)

                def high(j, c_prev):
                    act.wait_ge(multiplied, c_prev + 1)
                    act.wait_ge(act_made, HID0[f"ff{l}"] + j + 1)
                    AC(oph["B"][:, 0:2, :], gact[:], ACT.Square).then_inc(hid_hi, 1)

                made(0, c0, PB)
                prep_to(c0 + 3)
                high(0, c0 - 1)
                prep_to(c0 + 4)
                for j in range(1, 4):
                    made(j, c0 + 2 * j - 1)
                    prep_to(c0 + 2 * j + 3)
                    high(j, c0 + 2 * j)
                    prep_to(c0 + 2 * j + 4)
                with act.Fori(0, 3) as i:
                    for jj in range(4, 7):
                        made(i * 3 + jj, i * 6 + (c0 + 2 * jj - 1))
                        dyn(c0, 6, i, 2 * jj + 2)
                        high(i * 3 + jj, i * 6 + (c0 + 2 * jj))
                        dyn(c0, 6, i, 2 * jj + 3)
                nxt[0] = c0 + 28
                for j in range(13, 16):
                    made(j, c0 + 2 * j - 1)
                    prep_to(min(c0 + 2 * j + 3, c0 + 32))
                    high(j, c0 + 2 * j)
                    prep_to(min(c0 + 2 * j + 4, c0 + 32))

            act.wait_ge(vec_in, 16)
            S(AC(csil[:], V("c", 0, 16), ACT.Silu), "csil")
            act.wait_ge(x_in, 16)
            need(act, "G", "consts")
            squares("00.x", x, lambda q: None)
            root("00.x")
            prep_to(2)
            pre("00", "A")
            ffn("ffn00")
            boundary("00", "01", CH["conv_in"], CH["conv_in"])
            for g in (0, 1, 2, 4):
                c = CH["conv_in"] + 2 * g
                prep_to(c + 4)
                act.wait_ge(multiplied, c + 2)
                dst = cb_ if g < 2 else cc_
                half_ = g if g < 2 else (g - 2) // 2
                S(AC(dst[:, 4 * half_:4 * half_ + 4, :], PS["AB"[g % 2]][:], ACT.Copy), f"conv{g}")
            prep_to(CH["conv_out"] + 1)
            for g in range(2):
                need(act, "V", f"conv.y{g}")
                S(AC(oph["B"][:, 4 * g:4 * g + 4, :], cy_[:, 4 * g:4 * g + 4, :], ACT.Copy), f"conv.hi{g}")
                prep_to(CH["conv_out"] + 3)
            boundary("01", "02", CH["ffn01"], CH["ffn01"])
            ffn("ffn01")
            boundary("02", "10", CH["kv"], CH["kv"], [("kv", "B"), ("10", "A")])
            for g in range(3):
                c = CH["kv"] + 2 * g
                prep_to(c + 4)
                act.wait_ge(multiplied, c + 2)
                ps = PS["ABA"[g]]
                if g == 0:
                    S(AC(kvc, ps[:], ACT.Copy), "kv0")
                else:
                    S(AC((kslc, kwin)[g - 1], ps[:, 0:2, :], ACT.Copy))
                    S(AC(vtmp[("slc", "win")[g - 1]], ps[:, 2:4, :], ACT.Copy), f"kv{g}")
            need(act, "T", "vtrans")
            for n_, br in enumerate(("slc", "win")):
                S(AC(vtok[br], t3(flat["Y"][:, n_ * 512:n_ * 512 + 512], 2), ACT.Copy), "vtok")
            bh = oph["B"][:].rearrange("p a b -> p (a b)")
            tf = tmp8[:].rearrange("p a b -> p (a b)")
            act.wait_ge(multiplied, CH["kv"] + 6)
            for kv in range(2):
                need(act, "V", f"blk{kv}")
                S(AC(bh[:, kv * 960:kv * 960 + 960], tf[:, kv * 960:kv * 960 + 960], ACT.Copy), f"bhi{kv}")
            prep_to(CH["cmp"] + 5)
            act.wait_ge(multiplied, CH["cmp"] + 4)
            S(AC(hidc.rearrange("p k m c -> p (k m) c"), PA[:, :, 0:60], ACT.Gelu_apprx_tanh), "gelu")
            ffn("ffn10")
            boundary("10", "11", CH["nsa_in"], CH["nsa_in"])
            for g in range(2):
                c = CH["nsa_in"] + 2 * g
                prep_to(c + 4)
                act.wait_ge(multiplied, c + 2)
                S(AC(qf[:, 4 * g:4 * g + 4, :], PS["AB"[g]][:], ACT.Copy, scale=DH ** -0.5), f"q{g}")
            prep_to(CH["nsa_in"] + 6)
            act.wait_ge(multiplied, CH["nsa_in"] + 5)
            S(AC(gexp, flat["A"][:, 0:96], ACT.Exp, scale=-1.0), "gexp")
            prep_to(CH["nsa_in"] + 8)
            UNITS = [(ic, a, r) for ic in range(2) for a in range(2) for r in range(R)]
            for ic in range(2):
                need(act, "V", f"csub{ic}")
                S(AC(pc32[:, ic, :, 0:N_CMP], sc_[:, ic], ACT.Exp), f"cexp{ic}")

            def exps(n_):
                ic = UNITS[n_][0]
                need(act, "V", f"m{n_}")
                for x_ in range(4):
                    S(AC(ssb[n_ % 3][:, x_, 0:(ic + 1) * P], ssb[n_ % 3][:, x_, 0:(ic + 1) * P], ACT.Exp,
                         bias=small[:, 4 * (n_ % 3) + x_:4 * (n_ % 3) + x_ + 1],
                         accum_out=small[:, 96 + 4 * (n_ % 3) + x_:97 + 4 * (n_ % 3) + x_]), f"e{n_}")

            exps(0)
            need(act, "T", "pct")
            S(AC(ptc.rearrange("p i r c -> p (i r c)"), flat["Y"][:, 0:1024], ACT.Copy), "ptc")
            for n_, (ic, a, r) in enumerate(UNITS):
                if n_ + 1 < 16:
                    exps(n_ + 1)
                need(act, "T", f"pt{n_}")
                if n_:
                    need(act, "T", f"o{n_ - 1}")
                nb = 4 * (ic + 1)
                S(AC(ptsb[:, 0:nb, :].rearrange("p a b -> p (a b)"), flat["Y"][:, 0:nb * P], ACT.Copy), f"pt{n_}")
                need(act, "T", f"o{n_}")
                S(AC(oph["B"][:, a * 4 + r, ic * P:ic * P + P], PY[:, 4 + 2 * (n_ % 2), 0:P], ACT.Copy), f"ohi{n_}")
            boundary("11", "12", CH["ffn11"], CH["ffn11"])
            ffn("ffn11")
            boundary("12", "b00", CH["mix0"], CH["mix0"])
            for l in range(2):
                c = CH[f"mix{l}"]
                q_ = f"b{l}."
                def group(name, i, buf, dst, func, wait=None):
                    prep_to(c + 2 * i + 4)
                    act.wait_ge(multiplied, c + 2 * i + 2)
                    if wait:
                        need(act, *wait)
                    S(AC(dst, PS[buf][:], func), q_ + name)

                def half(i, h):
                    return t3(X[i], 8)[:, 4 * h:4 * h + 4, :]

                group("q", 0, "A", half(0, 0), ACT.Copy)
                if l == 0:
                    need(act, "V", "ang")
                    S(AC(sin_, sin_, ACT.Sin))
                    S(AC(cos_, cos_, ACT.Sin), "sincos")
                group("k", 1, "B", half(0, 1), ACT.Copy)
                group("v0", 2, "A", half(1, 0), ACT.Copy)
                group("v1", 3, "B", half(1, 1), ACT.Copy)
                group("g0", 4, "A", half(2, 0), ACT.Silu)
                need(act, "T", q_ + "vt")
                S(AC(X[3], flat["Y"], ACT.Copy), q_ + "vtok")
                group("g1", 5, "B", half(2, 1), ACT.Silu)
                group("u0", 6, "A", half(4, 0), ACT.Gelu_apprx_tanh)
                group("u1", 7, "B", half(4, 1), ACT.Gelu_apprx_tanh)
                need(act, "T", q_ + "o")
                for h in range(4):
                    S(AC(tmp8[:, 2 * h:2 * h + 2, :], PY[:, 2 * h:2 * h + 2, :], ACT.Square), q_ + f"osq{h}")
                group("s0", 8, "A", half(5, 0), ACT.Gelu_apprx_tanh)
                need(act, "T", q_ + "ossq")
                S(AC(osd[:], flat["B"][:, 0:8], ACT.Sqrt, bias=epsc[:], scale=D / 256.0), q_ + "osd")
                group("s1", 9, "A", half(5, 1), ACT.Gelu_apprx_tanh)
                need(act, "T", q_ + "ospread")
                S(AC(t3(rr, 4), PB[:], ACT.Copy), q_ + "rr")
                prep_to(c + 23)
                need(act, "V", q_ + "rety2")
                S(AC(oph["B"][:], tmp8[:], ACT.Copy), q_ + "rhi")
                group("p0", 10, "B", half(1, 0), ACT.Copy)
                need(act, "V", q_ + "rlo")
                squares(f"b{l}.v", t3(X[5], 8), lambda q: None, own=q_ + "s1")
                group("p1", 11, "A", half(1, 1), ACT.Copy)
                root(f"b{l}.v")
                group("h00", 12, "A", half(0, 0), ACT.Sigmoid)
                group("h01", 13, "B", half(0, 1), ACT.Sigmoid)
                need(act, "T", q_ + "wt")
                S(AC(wT.rearrange("p g t -> p (g t)"), flat["A"][:, 0:512], ACT.Copy), q_ + "wT")
                prep_to(c + 34)
                need(act, "T", q_ + "vnt")
                S(AC(X[3], flat["Y"], ACT.Copy), q_ + "vntok")
                group("h10", 16, "A", half(0, 0), ACT.Sigmoid, ("V", q_ + "m0.0"))
                need(act, "V", q_ + "sgu")
                act.wait_ge(multiplied, c + 32)
                S(AC(oph["B"][:], tmp8[:], ACT.Copy), q_ + "shi")
                group("h11", 17, "B", half(0, 1), ACT.Sigmoid, ("V", q_ + "m0.1"))
                group("h20", 20, "A", half(0, 0), ACT.Sigmoid, ("V", q_ + "m1.0"))
                need(act, "V", q_ + "pm7")
                act.wait_ge(multiplied, c + 40)
                S(AC(oph["B"][:], tmp8[:], ACT.Copy), q_ + "phi")
                group("h21", 21, "B", half(0, 1), ACT.Sigmoid, ("V", q_ + "m1.1"))
                for h in range(2):
                    prep_to(c + 48 + 2 * h)
                    need(act, "V", q_ + f"m2.{h}")
                    act.wait_ge(multiplied, c + 44)
                    S(AC(oph["A"][:, 4 * h:4 * h + 4, :], macc(h), ACT.Copy), q_ + f"mhi{h}")
                boundary(f"b{l}0", f"b{l}1", CH[f"ff{l}"], CH[f"ff{l}"])
                ff2(l)
                if l == 0:
                    boundary("b01", "b10", CH["mix1"], CH["mix1"])
                else:
                    squares("fin.x", x, lambda q: need(act, "V", f"b11.u{2 * q + 1}"))
                    root("fin.x")

        @block.vector
        def _(dve):
            S = Steps(steps["V"], "V", seen)
            nxt = [0]
            TT, STT, TS = nc.vector.tensor_tensor, nc.vector.scalar_tensor_tensor, nc.vector.tensor_scalar

            def own(v):
                dve.wait_ge(steps["V"], v)

            def settle():
                dve.wait_ge(steps["V"], S.n)

            def split(slot, w=CHUNK):
                TT(wlo[slot][:, 0:w], raw[slot][:, 0:w], whi[slot][:, 0:w].bitcast(F32), ALU.subtract).then_inc(lo_ready, 1)

            def prep_to(c):
                while nxt[0] < min(c, N_CHUNKS):
                    dve.wait_ge(hi_ready, nxt[0] + 1)
                    split(nxt[0] % RING, 384 if nxt[0] == CH["nsa_in"] + 4 else CHUNK)
                    nxt[0] += 1

            def dyn(c0, per, i, k):
                dve.wait_ge(hi_ready, i * per + (c0 + k + 1))
                split((c0 + k) % RING)

            def ada(name, f, i=0, per=0):
                which, slots, _ = JOBS[name]
                slot, width, o_, loads = slots[f % 4]
                k, n = f // 4, 16 * len(loads)
                cs = csil[:, bass.ds(i * per + (KT * which + k), 1)] if per else csil[:, KT * which + k:KT * which + k + 1]
                ready = first_ready if name == "first" else ada_ready
                dve.wait_ge(ready[slot], i * (per * n) + (16 * LOADS0[name][slot] + n * (k + 1)))
                if ADA0[name] + k > 0:
                    dve.wait_ge(ada_used[slot], i * per + (ADA0[name] + k))
                STT(acc[:, o_:o_ + width], slab[slot][:, 0:width], cs, acc[:, o_:o_ + width],
                    ALU.mult, ALU.add).then_inc(ada_used[slot], 1)

            def mods(name, later=False):
                mark = f"{name}.mod2" if later else f"{name}.mod"
                need(dve, "T", f"{name}.mods2" if later else f"{name}.mods")
                first = LATER[name][0] if name in LATER else 99
                for t0, n, m0, bias in MODS[name]:
                    if (t0 >= first) == later:
                        v = S(TT(mod[:, m0:m0 + n], flat["B"][:, t0 + 512 * later:t0 + 512 * later + n], bias, ALU.add), mark)
                own(v)
                for s_ in LATER[name][1] if later else SCALES[name]:
                    sh = SUB[s_]["shift"]
                    v = S(STT(A_(s_), mod[:, sh + 8:sh + 16], 1.0, SUB[s_]["g_pre"], ALU.add, ALU.mult))
                for s_ in LATER[name][2] if later else GATES[name]:
                    sh = SUB[s_]["shift"]
                    if SUB[s_]["g_post"] is not None:
                        v = S(STT(G_(s_), mod[:, sh + 16:sh + 24], SUB[s_]["w"], SUB[s_]["g_post"], ALU.mult, ALU.mult))
                    else:
                        v = S(TS(G_(s_), mod[:, sh + 16:sh + 24], 1.0, None, ALU.mult))
                own(v)

            def inverse(tag):
                need(dve, "S", f"{tag}.sd")
                settle()
                own(S(nc.vector.reciprocal(rstd[:], sd[:])))

            def pre(sub, op, hold=None):
                if hold:
                    settle()
                if hold:
                    settle()

                def low(k):
                    need(dve, "S", f"{sub}.hi{k}")
                    S(STT(opl[op][:, k, :], tmp8[:, k, :], B_(sub)[:, k:k + 1], oph[op][:, k, :].bitcast(F32),
                          ALU.add, ALU.subtract), f"{sub}.lo{k}")

                for k in range(KT):
                    if hold:
                        need(dve, "S", f"{hold}.hi{k}")
                    S(STT(tmp8[:, k, :], x[:, k, :], A_(sub)[:, k:k + 1], rstd[:], ALU.mult, ALU.mult), f"{sub}.t{k}")
                    if k > 0:
                        low(k - 1)
                low(KT - 1)

            def boundary(sub, nsub, c_done, c_next, ops=None, last=False, job_=None):
                prep_to(c_next + 2)
                if not sub.startswith("b"):
                    for q in range(4):
                        need(dve, "S", f"{sub}.y.sq{q}")
                        S(TT(tmp8[:, 2 * q, :], tmp8[:, 2 * q, :], tmp8[:, 2 * q + 1, :], ALU.add), f"{sub}.y.pair{q}")
                    inverse(f"{sub}.y")
                    def add(k):
                        if k not in POOL_ADDS:
                            need(dve, "V", f"{sub}.u{k}")
                            S(TT(x[:, k, :], x[:, k, :], tmp8[:, k, :], ALU.add), f"{sub}.x{k}")

                    for k in range(KT):
                        S(STT(tmp8[:, k, :], PY[:, k, :], G_(sub)[:, k:k + 1], rstd[:], ALU.mult, ALU.mult), f"{sub}.u{k}")
                        if k > 0:
                            add(k - 1)
                    add(KT - 1)
                    prep_to(c_next + 3)
                else:
                    for k in range(KT):
                        if k == 6:
                            dve.wait_ge(multiplied, c_done)
                        elif k % 2 == 0:
                            need(dve, "T", f"{sub}.bank{k // 2}")
                        S(STT(x[:, k, :], PY[:, k, :], G_(sub)[:, k:k + 1], x[:, k, :], ALU.mult, ALU.add), f"{sub}.u{k}")
                if last:
                    return
                inverse(f"{nsub}.x")
                hold = None
                for s_, op in ops or [(nsub, "A")]:
                    pre(s_, op, hold)
                    hold = s_
                if job_ in LATER:
                    mods(job_, True)
                prep_to(c_next + 3)

            def ffn(name):
                c0 = CH[name]
                h0 = HID0[name]
                prep_to(c0 + 3)

                def made(j, ps=PA):
                    dve.wait_ge(act_made, h0 + j + 1)
                    if not (isinstance(j, int) and h0 + j == 0):
                        dve.wait_ge(hid_lo, h0 + j)
                    TT(hidf[:], gact[:], ps[:, 2:4, :], ALU.mult).then_inc(hid_made, 1)

                def low(j):
                    dve.wait_ge(hid_hi, h0 + j + 1)
                    TT(opl["B"][:, 0:2, :], hidf[:], oph["B"][:, 0:2, :].bitcast(F32), ALU.subtract).then_inc(hid_lo, 1)

                need(dve, "G", f"{name}.zero")
                ada(name, 0)
                ada(name, 1)
                made(0, PB)
                prep_to(c0 + 4)
                low(0)
                prep_to(c0 + 5)
                ada(name, 2)
                prep_to(c0 + 6)
                ada(name, 3)
                with dve.Fori(0, 2) as i:
                    for u in range(4):
                        made(i * 4 + (u + 1))
                        dyn(c0, 12, i, 3 * u + 6)
                        ada(name, 4 + 3 * u, i, 3)
                        low(i * 4 + (u + 1))
                        dyn(c0, 12, i, 3 * u + 7)
                        ada(name, 5 + 3 * u, i, 3)
                        dyn(c0, 12, i, 3 * u + 8)
                        ada(name, 6 + 3 * u, i, 3)
                nxt[0] = c0 + 30
                made(9)
                prep_to(c0 + 31)
                ada(name, 28)
                low(9)
                ada(name, 29)
                prep_to(c0 + 33)
                ada(name, 30)
                ada(name, 31)
                made(10)
                low(10)
                prep_to(c0 + 34)
                mods(name)

            def ff2(l):
                c0 = CH[f"ff{l}"]
                h0 = HID0[f"ff{l}"]
                prep_to(c0 + 2)

                def made(j):
                    dve.wait_ge(act_made, h0 + j + 1)
                    dve.wait_ge(hid_lo, h0 + j)
                    TT(hidf[:], gact[:], gact[:], ALU.mult).then_inc(hid_made, 1)

                def low(j):
                    dve.wait_ge(hid_made, h0 + j + 1)
                    dve.wait_ge(hid_hi, h0 + j + 1)
                    TT(opl["B"][:, 0:2, :], hidf[:], oph["B"][:, 0:2, :].bitcast(F32), ALU.subtract).then_inc(hid_lo, 1)

                made(0)
                prep_to(c0 + 3)
                low(0)
                prep_to(c0 + 4)
                if l == 0:
                    need(dve, "G", "ff0.zero")
                    for f in range(2):
                        ada("ff0", f)
                for j in range(1, 3):
                    made(j)
                    prep_to(c0 + 2 * j + 3)
                    if l == 0:
                        ada("ff0", 3 * j - 1)
                    low(j)
                    prep_to(c0 + 2 * j + 4)
                    if l == 0:
                        ada("ff0", 3 * j)
                        ada("ff0", 3 * j + 1)
                with dve.Fori(0, 2) as i:
                    for u in range(6):
                        made(i * 6 + (u + 3))
                        dyn(c0, 12, i, 2 * u + 8)
                        if l == 0:
                            ada("ff0", 8 + 2 * u, i, 3)
                        low(i * 6 + (u + 3))
                        dyn(c0, 12, i, 2 * u + 9)
                        if l == 0:
                            ada("ff0", 9 + 2 * u, i, 3)
                nxt[0] = c0 + 32
                made(15)
                low(15)
                if l == 0:
                    mods("ff0")

            need(dve, "S", "csil")
            need(dve, "G", "first.zero")
            for k in range(KT):
                if k == 5:
                    inverse("00.x")
                if k == KT - 1:
                    prep_to(1)
                for q in range(4):
                    ada("first", 4 * k + q)
            mods("first")
            pre("00", "A")
            ffn("ffn00")
            boundary("00", "01", CH["conv_in"], CH["conv_in"], job_="ffn00")
            need(dve, "G", "cpad")
            for g in range(2):
                pos = 3 + 2 * g
                c = CH["conv_in"] + 2 * pos
                prep_to(c + 4)
                dve.wait_ge(multiplied, c + 2)
                need(dve, "S", f"conv{pos - 1}")
                ts = range(4 * g, 4 * g + 4)
                own(S(TT(cv_[:, 4 * g:4 * g + 4, 2:258], PB[:], cc_[:, 4 * g:4 * g + 4, :], ALU.mult), f"conv{pos}"))
                for t in ts:
                    v = S(TS(cy_[:, t, :], cv_[:, t, 0:256], V("a_conv", t, 1), None, ALU.mult))
                for tap in (1, 2):
                    for n_, t in enumerate(ts):
                        own(v - 3 + n_)
                        S(STT(cy_[:, t, :], cv_[:, t, tap:tap + 256], V("a_conv", 8 * tap + t, 1), cy_[:, t, :],
                              ALU.mult, ALU.add))
                    v += 4
                own(v)
                own(S(TT(cy_[:, 4 * g:4 * g + 4, :], cy_[:, 4 * g:4 * g + 4, :], cb_[:, 4 * g:4 * g + 4, :], ALU.mult),
                      f"conv.y{g}"))
                if g == 0:
                    prep_to(CH["conv_out"] + 1)
                need(dve, "S", f"conv.hi{g}")
                S(TT(opl["B"][:, 4 * g:4 * g + 4, :], cy_[:, 4 * g:4 * g + 4, :], oph["B"][:, 4 * g:4 * g + 4, :].bitcast(F32),
                     ALU.subtract), f"conv.lo{g}")
            boundary("01", "02", CH["ffn01"], CH["ffn01"])
            ffn("ffn01")
            boundary("02", "10", CH["kv"], CH["kv"], [("kv", "B"), ("10", "A")], job_="ffn01")
            prep_to(CH["cmp"] + 2)
            tf = tmp8[:].rearrange("p a b -> p (a b)")
            bh, bl = (z["B"][:].rearrange("p a b -> p (a b)") for z in (oph, opl))
            dve.wait_ge(cmp_in, 64)
            for k in range(KT):
                need(dve, "S", f"10.hi{k}")
            for kv, hf in ((0, 0), (0, 1), (1, 0), (1, 1)):
                need(dve, "T", f"dup{kv}")
                ps = PS["BA"[kv]]
                ps_h = slice(64 * hf, 64 * hf + 64)
                for l8 in range(2):
                    src = ps[ps_h, :, 16 * l8:16 * l8 + 16 * N_CMP].rearrange("p g (n l b) -> p l g n b", l=8, b=2)[:, :, :, :, hf]
                    dst = tf[ps_h, kv * 960:kv * 960 + 960].rearrange("p (l g n) -> p l g n", l=16, g=4)[:, 8 * l8:8 * l8 + 8]
                    ps_pos = pos2[ps_h, kv, 8 * l8:8 * l8 + 8].unsqueeze(2).unsqueeze(3).broadcast_to([64, 8, GROUPS, N_CMP])
                    S(TT(dst, src, ps_pos, ALU.add), f"blk{kv}")
                if kv == 1:
                    need(dve, "S", f"bhi{hf}")
                    sl = slice(hf * 960, hf * 960 + 960)
                    S(TT(bl[:, sl], tf[:, sl], bh[:, sl].bitcast(F32), ALU.subtract), f"blo{hf}")
            prep_to(CH["cmp"] + 5)
            need(dve, "T", "cmpkv")
            need(dve, "G", "vpad")
            S(nc.vector.tensor_copy(kcmp, PB[:, 0, 0:60]))
            for g in range(GROUPS):
                S(nc.vector.tensor_copy(vcmp[32 * g:32 * g + N_CMP, :], PB[32 * g:32 * g + N_CMP, 2, 0:64]), "vcmp")
            ffn("ffn10")
            boundary("10", "11", CH["nsa_in"], CH["nsa_in"], job_="ffn10")
            prep_to(CH["nsa_in"] + 8)
            need(dve, "S", "gexp")
            v = S(TS(gexp, gexp, 1.0, None, ALU.add))
            own(v)
            S(nc.vector.reciprocal(gates.rearrange("p i c -> p (i c)"), gexp), "gates")
            need(dve, "T", "scmp")
            for ic in range(2):
                for u in range(2):
                    dst = sc_[:, ic].rearrange("p (x u) n -> p x u n", u=2)[:, :, u, :]
                    bia = cbias[:, ic].rearrange("p (x u) n -> p x u n", u=2)[:, :, u, :]
                    src = flat["B"][:, u * 512 + ic * 120:u * 512 + ic * 120 + 120].rearrange("p (x n) -> p x n", n=N_CMP)
                    v = S(TT(dst, src, bia, ALU.add), "scmp")
            own(v)
            mx = [small[:, 16 + 16 * ic:32 + 16 * ic] for ic in range(2)]
            sm = [small[:, 48 + 16 * ic:64 + 16 * ic] for ic in range(2)]
            for ic in range(2):
                v = S(nc.vector.tensor_reduce(mx[ic], sc_[:, ic], AX.X, ALU.max))
            own(v)
            for ic in range(2):
                v = S(TS(mx[ic], mx[ic], NEG / 1e10, None, ALU.max))
            own(v)
            for ic in range(2):
                S(TT(sc_[:, ic], sc_[:, ic], mx[ic].unsqueeze(2).broadcast_to([P, 16, N_CMP]), ALU.subtract), f"csub{ic}")
            UNITS = [(ic, a, r) for ic in range(2) for a in range(2) for r in range(R)]
            sl_ = slopes()

            def soft(n_):
                ic, a, r = UNITS[n_]
                W = (ic + 1) * P
                need(dve, "T", f"sc{n_}")
                if n_ >= 3:
                    need(dve, "T", f"pt{n_ - 3}")
                for u in range(2):
                    h = (2 * a + u) * R + r
                    v = S(STT(ssb[n_ % 3][:, 2 * u:2 * u + 2, 0:W], dist[:, T - W:T].unsqueeze(1).broadcast_to([P, 2, W]),
                              sl_[h], PS["AB"[n_ % 2]][:, 2 * u:2 * u + 2, 0:W], ALU.mult, ALU.add), f"s{n_}")
                own(v)
                S(nc.vector.tensor_reduce(small[:, 4 * (n_ % 3):4 * (n_ % 3) + 4], ssb[n_ % 3][:, :, 0:W], AX.X, ALU.max,
                                          negate=True), f"m{n_}")

            soft(0)
            for ic in range(2):
                need(dve, "S", f"cexp{ic}")
                own(S(nc.vector.tensor_reduce(sm[ic], pc32[:, ic, :, 0:N_CMP], AX.X, ALU.add)))
                own(S(TS(sm[ic], sm[ic], 1e-30, None, ALU.max)))
                own(S(nc.vector.reciprocal(sm[ic], sm[ic])))
                own(S(TT(sm[ic], sm[ic], gates[:, ic, 0:16], ALU.mult)))
                S(TT(pc32[:, ic, :, 0:N_CMP], pc32[:, ic, :, 0:N_CMP], sm[ic].unsqueeze(2).broadcast_to([P, 16, N_CMP]),
                     ALU.mult), f"pc{ic}")

            def olow(n_):
                ic, a, r = UNITS[n_]
                need(dve, "S", f"ohi{n_}")
                S(TT(opl["B"][:, a * 4 + r, ic * P:ic * P + P], PY[:, 4 + 2 * (n_ % 2), 0:P],
                     oph["B"][:, a * 4 + r, ic * P:ic * P + P].bitcast(F32), ALU.subtract), f"olo{n_}")

            for n_, (ic, a, r) in enumerate(UNITS):
                rs = small[:, 80 + 4 * (n_ % 3):84 + 4 * (n_ % 3)]
                W = (ic + 1) * P
                if n_ + 1 < 16:
                    soft(n_ + 1)
                need(dve, "S", f"e{n_}")
                own(S(nc.vector.reciprocal(rs, small[:, 96 + 4 * (n_ % 3):100 + 4 * (n_ % 3)])))
                gt = gates[:, ic, 16:48].rearrange("p (b h) -> p h b", b=2)[:, r * 4 + 2 * a:r * 4 + 2 * a + 2, :]
                own(S(TT(t3(rs, 2), t3(rs, 2), gt, ALU.mult)))
                S(TT(ssb[n_ % 3][:, :, 0:W], ssb[n_ % 3][:, :, 0:W], rs.unsqueeze(2).broadcast_to([P, 4, W]), ALU.mult), f"p{n_}")
                if n_:
                    olow(n_ - 1)
            olow(15)
            boundary("11", "12", CH["ffn11"], CH["ffn11"])
            ffn("ffn11")
            boundary("12", "b00", CH["mix0"], CH["mix0"], job_="ffn11")
            for l in range(2):
                c = CH[f"mix{l}"]
                q_ = f"b{l}."
                prep_to(c + 4)
                if l == 0:
                    dve.wait_ge(b2_in, 32)
                    t0, t1, t2 = (rr[:, 256 * i:256 * i + 256] for i in range(3))
                    TWO_PI = 2 * np.pi
                    C1 = 6.28125
                    C2 = 0.0019350051879882812
                    C3 = TWO_PI - C1 - C2
                    MAGIC = 12582912.0
                    own(S(nc.vector.tensor_copy(t0, posi.bitcast(I32))))
                    own(S(TS(t0, t0, invf, None, ALU.mult)))
                    own(S(TS(t1, t0, 1.0 / TWO_PI, None, ALU.mult)))
                    own(S(TS(t1, t1, MAGIC, None, ALU.add)))
                    own(S(TS(t1, t1, -MAGIC, None, ALU.add)))
                    for cc in (C1, C2, C3):
                        own(S(STT(t0, t1, -cc, t0, ALU.mult, ALU.add)))
                    own(S(TS(sin_, t0, 3.1415925, -3.1415925, ALU.min, ALU.max)))
                    own(S(TS(t0, sin_, float(np.pi / 2), None, ALU.add)))
                    own(S(TS(t1, t0, float(np.pi), -TWO_PI, ALU.is_gt, ALU.mult)))
                    own(S(TT(t0, t0, t1, ALU.add)))
                    own(S(TS(cos_, t0, 3.1415925, -3.1415925, ALU.min, ALU.max), "ang"))
                prep_to(c + 8)
                X0 = t3(X[0], 8)
                need(dve, "S", "sincos")
                need(dve, "S", q_ + "k")
                for k in range(KT):
                    need(dve, "S", f"b{l}0.hi{k}")
                settle()
                own(S(TT(tmp8[:], X0, cos_.unsqueeze(1).broadcast_to([P, 8, T]), ALU.mult)))
                need(dve, "T", q_ + "rot")
                own(S(TT(X0, PY[:], sin_.unsqueeze(1).broadcast_to([P, 8, T]), ALU.mult), q_ + "rot"))
                own(S(TT(X0, X0, tmp8[:], ALU.add), q_ + "rotk"))
                prep_to(c + 16)
                need(dve, "T", q_ + "sc")
                settle()
                sdm = t3(tmp8[:].rearrange("p a b -> p (a b)")[:, 0:1536], 4)
                own(S(TT(sdm[:, :, 0:T], PY[:].rearrange("p (h e) t -> p h e t", h=4)[:, :, 0, :], decay, ALU.mult)))
                S(TT(sdm[:, :, T:T + P], PY[:].rearrange("p (h e) t -> p h e t", h=4)[:, :, 1, 0:P], decay[:, :, 0:P], ALU.mult),
                  q_ + "dec")
                prep_to(c + 20)
                need(dve, "S", q_ + "osd")
                own(S(nc.vector.reciprocal(osd[:], osd[:])))
                for h in range(4):
                    for j in range(2):
                        S(TS(hdiag[:, h, j * P:j * P + P], ident, osd[:, 2 * h + j:2 * h + j + 1], float(D), ALU.mult, ALU.mult),
                          q_ + "odiag")
                prep_to(c + 22)
                need(dve, "S", q_ + "rr")
                t84 = tmp8[:].rearrange("p (h e) t -> p h e t", e=2)
                for e in range(2):
                    v = S(TT(t84[:, :, e, :], PY[:].rearrange("p (h e) t -> p h e t", e=2)[:, :, e, :], t3(rr, 4), ALU.mult), q_ + "rety")
                own(v)
                own(S(TT(tmp8[:], tmp8[:], t3(X[2], 8), ALU.mult), q_ + "rety2"))
                prep_to(c + 23)
                need(dve, "S", q_ + "rhi")
                S(TT(opl["B"][:], tmp8[:], oph["B"][:].bitcast(F32), ALU.subtract), q_ + "rlo")
                prep_to(c + 25)
                inverse(f"b{l}.v")
                prep_to(c + 28)
                for k in range(KT):
                    S(STT(t3(X[5], 8)[:, k, :], t3(X[5], 8)[:, k, :], V("vnorm", 8 * l + k, 1), rstd[:], ALU.mult, ALU.mult),
                      q_ + f"vn{k}")
                G8 = t3(X[0], 8)

                def merge(b, h, buf, c_in):
                    prep_to(c_in + 4)
                    dve.wait_ge(multiplied, c_in + 2)
                    settle()
                    need(dve, "S", q_ + f"h{b}{h}")
                    g_ = G8[:, 4 * h:4 * h + 4, :]
                    if b == 0:
                        seen["V", q_ + f"m{b}.{h}"] = S(TT(macc(h), PS[buf][:], g_, ALU.mult), q_ + f"r{b}{h}")
                    else:
                        own(S(TT(g_, PS[buf][:], g_, ALU.mult), q_ + f"r{b}{h}"))
                        own(S(TT(macc(h), macc(h), g_, ALU.add), q_ + f"m{b}.{h}"))

                prep_to(c + 28)
                merge(0, 0, "A", c + 28)
                merge(0, 1, "B", c + 30)
                prep_to(c + 36)
                need(dve, "T", q_ + "mix")
                dve.wait_ge(lay_in, 48 * (l + 1))
                for g in range(4):
                    v = S(TT(tmp8[:, 2 * g:2 * g + 2, :].rearrange("p e (n t) -> p (e n) t", n=2),
                             PY[:, 2 * g:2 * g + 2, :].rearrange("p e (n t) -> p (e n) t", n=2),
                             bs[:, g, :].unsqueeze(1).broadcast_to([P, 4, P]), ALU.add), q_ + "mix")
                own(v)
                own(S(TT(tmp8[:], tmp8[:], t3(X[4], 8), ALU.mult), q_ + "sgu"))
                need(dve, "S", q_ + "shi")
                own(S(TT(opl["B"][:], tmp8[:], oph["B"][:].bitcast(F32), ALU.subtract), q_ + "slo"))
                prep_to(c + 38)
                p_, ping, pong = t3(X[1], 8), t3(X[4], 8), t3(X[5], 8)
                need(dve, "S", q_ + "p1")
                src = p_
                def pool_level(lev, src):
                    dst = (ping, pong)[lev % 2]
                    sh = 1 << lev
                    t0 = 2 * lev
                    settle()
                    S(nc.vector.tensor_copy(dst[:, t0:8, 0:sh], src[:, t0:8, 0:sh]))
                    own(S(TT(dst[:, t0:8, sh:T], src[:, t0:8, sh:T], src[:, t0:8, 0:T - sh], ALU.add)))
                    res = t3(X[3], 8)[:, t0:t0 + 2, :]
                    S(STT(res[:, :, 16:T], dst[:, t0:t0 + 2, 16:T], 1.0 / POOL_WINDOWS[lev], p_[:, t0:t0 + 2, 16:T],
                          ALU.mult, ALU.subtract))
                    own(S(TT(res[:, :, 0:16], dst[:, t0:t0 + 2, 0:16], cnt[:, lev, :].unsqueeze(1).broadcast_to([P, 2, 16]), ALU.mult)))
                    S(TT(res[:, :, 0:16], res[:, :, 0:16], p_[:, t0:t0 + 2, 0:16], ALU.subtract), q_ + "pooled")
                    return dst

                for lev in range(2):
                    src = pool_level(lev, src)
                    prep_to(c + 39 + lev)
                merge(1, 0, "A", c + 36)
                src = pool_level(2, src)
                merge(1, 1, "B", c + 38)
                pool_level(3, src)
                prep_to(c + 44)
                need(dve, "T", q_ + "pm")
                for k in range(KT):
                    S(TS(tmp8[:, k, :], PY[:, k, :], V("b_pool", 8 * l + k, 1), V("pool_scale", 8 * l + k, 1), ALU.add, ALU.mult),
                      q_ + f"pm{k}")
                own(S.n)
                need(dve, "S", q_ + "phi")
                own(S(TT(opl["B"][:], tmp8[:], oph["B"][:].bitcast(F32), ALU.subtract), q_ + "plo"))
                for h in range(2):
                    merge(2, h, "AB"[h], c + 44 + 2 * h)
                    need(dve, "S", q_ + f"mhi{h}")
                    seen["V", q_ + "branch_done"] = S.n
                    S(TT(opl["A"][:, 4 * h:4 * h + 4, :], macc(h), oph["A"][:, 4 * h:4 * h + 4, :].bitcast(F32), ALU.subtract),
                      q_ + f"mlo{h}")
                boundary(f"b{l}0", f"b{l}1", CH[f"ff{l}"], CH[f"ff{l}"])
                ff2(l)
                if l == 0:
                    boundary("b01", "b10", CH["mix1"], CH["mix1"])
                else:
                    boundary("b11", None, N_CHUNKS, N_CHUNKS, last=True)
                    inverse("fin.x")
                    for k in range(KT):
                        S(STT(tmp8[:, k, :], x[:, k, :], V("final", k, 1), rstd[:], ALU.mult, ALU.mult), f"fin.t{k}")

        @block.gpsimd
        def _(pool):
            S = Steps(steps["G"], "G", seen)

            def zero(name):
                S(pool.memset(acc[:, 0:JOBS[name][2]], 0.0), f"{name}.zero")

            def add_x(sub):
                for k in POOL_ADDS:
                    need(pool, "V", f"{sub}.u{k}")
                    S(pool.tensor_tensor(x[:, k, :], x[:, k, :], tmp8[:, k, :], ALU.add), f"{sub}.x{k}")

            def ada(name, k):
                for slot, _, _, loads in JOBS[name][1]:
                    use = k + ADA0[name]
                    if not isinstance(use, int) or use > 0:
                        pool.wait_ge(ada_used[slot], use)
                    if not isinstance(use, int):
                        pool.sem_inc(ada_free, 1)
                    for w, c0, width, o in loads:
                        pool.dma_start(slab[slot][:, o:o + width], w[bass.ds(k * P, P), c0:c0 + width]).then_inc(ada_ready[slot], 16)

            def ada_all(name):
                with pool.Fori(0, KT) as i:
                    ada(name, i)

            zero("first")
            S(pool.memset(epsc[:], EPS), "consts")
            need(pool, "T", "first.mods")
            zero("ffn00")
            S(pool.memset(cv_[:, :, 0:2], 0.0), "cpad")
            ada_all("ffn00")
            add_x("00")
            need(pool, "T", "ffn00.mods2")
            zero("ffn01")
            add_x("01")
            ada_all("ffn01")
            S(pool.memset(vcmp, 0.0), "vpad")
            add_x("02")
            need(pool, "T", "ffn01.mods2")
            zero("ffn10")
            ada_all("ffn10")
            add_x("10")
            need(pool, "T", "ffn10.mods2")
            S(pool.memset(pc32[:, :, :, N_CMP:32], 0.0), "ppad")
            add_x("11")
            zero("ffn11")
            ada_all("ffn11")
            add_x("12")
            for l in range(2):
                pool.wait_ge(lay_in, 48 * (l + 1))
                v = wsr.rearrange("p (g s) -> p g s", g=4)
                S(pool.affine_select(out=v, in_=v, compare_op=ALU.is_ge, fill=0.0, base=0, pattern=[[0, 4], [-1, P]],
                                     channel_multiplier=1), f"b{l}.tril")
                if l == 0:
                    need(pool, "V", "b00.u7")
                    zero("ff0")
                    ada_all("ff0")

    return seen


def kernel(**inputs):
    import concourse.bacc as bacc
    from concourse.bass_utils import run_bass_kernel_spmd

    a = {k: np.asarray(v) for k, v in inputs.items()}

    def fm(v):
        return np.ascontiguousarray(v.reshape(-1, P).T)

    vec = np.concatenate([fm(a[n]) for n in ("norm_g", "ada_b", "kv_norm_g", "kv_ada_b", "b_ada_2", "norm1_2", "norm2_2",
                                             "a_conv", "vnorm_gmlp_2", "b_pool_2", "pool_scale_2", "final_norm_2", "c", "c_2")], 1)
    wb = a["b_w_in"][0]
    wq = wb[:, :D].reshape(D, 2, 2, R, DH).transpose(0, 1, 3, 2, 4).reshape(D, D)
    wg = wb[:, D:].reshape(D, 3, GROUPS, R).transpose(0, 1, 3, 2).reshape(D, 48)
    wo = a["b_w_out"][0].reshape(2, 2, R, DH, D).transpose(0, 2, 1, 3, 4).reshape(D, D)
    pos2 = a["cmp_pos"].reshape(2, 16, 2, DH).transpose(2, 3, 0, 1).reshape(P, 2, 16)
    dram = {
        "x_fm": a["x"][0].T.reshape(KT, P, T).transpose(1, 0, 2),
        "vec": vec,
        "ada_w": a["ada_w"], "kv_ada_w": a["kv_ada_w"], "w_ada_2": a["w_ada_2"],
        "ffn_w_in": a["ffn_w_in"], "ffn_w_out": a["ffn_w_out"],
        "a_w_in": a["a_w_in"][0], "a_w_out": a["a_w_out"][0],
        "kv_w": a["kv_w"], "cmp_pos2": pos2, "cmp_w1": a["cmp_w1"], "cmp_w2": a["cmp_w2"],
        "b_w_in_p": np.concatenate([wq, wg], 1), "b_w_out_p": wo,
        "positions": a["positions_2"],
        "w_in_2": a["w_in_2"], "ws": a["ws_gmlp_2"].transpose(0, 2, 1, 3).reshape(DEPTH, P, 4 * P),
        "bs": a["bs_gmlp_2"].reshape(DEPTH, 4 * P), "w_pool": a["w_pool_2"].reshape(DEPTH, D, 256),
        "w_branch": a["w_branch_2"], "w_out_2": a["w_out_2"], "w_ff1": a["w_ff1_2"], "w_ff2": a["w_ff2_2"],
        **tables(),
    }
    dram = {n: np.ascontiguousarray(v) for n, v in dram.items()}

    def program(at):
        nc = bacc.Bacc("TRN2", target_bir_lowering=False, num_devices=1)
        ins = {n: nc.dram_tensor(n, v.shape, mybir.dt.from_np(v.dtype), kind="ExternalInput").ap() for n, v in dram.items()}
        out = nc.dram_tensor("out_fm", (P, KT, T), F32, kind="ExternalOutput").ap()
        return nc, build(nc, ins, out, at)

    class Any(dict):
        def __missing__(self, key):
            return 1

    _, at = program(Any())
    nc, again = program(at)
    assert at == again
    r = run_bass_kernel_spmd(nc, [dram], core_ids=[0])
    y = r.results[0]["out_fm"]
    return np.ascontiguousarray(y.transpose(2, 1, 0).reshape(1, T, D))
```
